# Optimizing a Trainium2 kernel written in Bass

```python
import jax
import jax.numpy as jnp
from jax import lax
import numpy as np

D_MODEL = 1024
BATCH = 1
SEQ = 1024
DEPTH = 2

HEAD_DIM = 64
N_MIXERS = 4
HEADS_PER_MIXER = D_MODEL // (N_MIXERS * HEAD_DIM)
GROUP_WIDTH = HEADS_PER_MIXER * HEAD_DIM
MIX_WIDTH = N_MIXERS * GROUP_WIDTH
BLOCK = 128
NORM_EPS = 1e-6
MLA_Q_RANK = 192
MLA_KV_RANK = 128
MLA_NOPE = 32
MLA_ROPE = 32
MLA_V = HEAD_DIM
ROPE_BASE = 10000.0
DILATED_PAIRS = ((128, 1), (512, 4), (2048, 16))
DIL_ALIGN = BLOCK * 16
SWA_WINDOW = 128
SWA_KV_HEADS = 2
SWA_GROUP = HEADS_PER_MIXER // SWA_KV_HEADS
N_GROUPS = 4
EXPERTS_PER_GROUP = 8
N_EXPERTS = N_GROUPS * EXPERTS_PER_GROUP
TOP_K = 2
D_EXPERT = 256
EXPERT_BLOCK = 128
IN_SPLITS = (MLA_Q_RANK, MLA_KV_RANK, MLA_ROPE, 3 * GROUP_WIDTH, 3 * GROUP_WIDTH, HEADS_PER_MIXER, GROUP_WIDTH, 2 * SWA_KV_HEADS * HEAD_DIM)
IN_WIDTH = sum(IN_SPLITS)

kernel_name = 'hybrid_headgroup_mla_dilated_fox_swa_hmoe'

def rmsnorm(x, g):
    xf = x.astype(jnp.float32)
    y = xf * lax.rsqrt(jnp.mean(xf * xf, axis=-1, keepdims=True) + NORM_EPS)
    return (y * g.astype(jnp.float32)).astype(x.dtype)

def rope(x):
    S, dr = x.shape[1], x.shape[-1]
    inv = ROPE_BASE ** (-jnp.arange(0, dr, 2, dtype=jnp.float32) / dr)
    ang = jnp.arange(S, dtype=jnp.float32)[:, None] * inv[None, :]
    cos = jnp.cos(ang)[None, :, None, :]
    sin = jnp.sin(ang)[None, :, None, :]
    xf = x.astype(jnp.float32)
    x1, x2 = xf[..., : dr // 2], xf[..., dr // 2:]
    return jnp.concatenate([x1 * cos - x2 * sin, x2 * cos + x1 * sin], axis=-1).astype(x.dtype)

def alibi_slopes():
    n = 2 * HEADS_PER_MIXER
    s = 2.0 ** (-8.0 * jnp.arange(1, n + 1, dtype=jnp.float32) / n)
    return s[HEADS_PER_MIXER:], s[:HEADS_PER_MIXER]

def banded_attention(q, k, v, max_dist, unit, slopes, sink=None):
    b, L, hk, g, dh = q.shape
    nb = L // BLOCK
    qb = q.reshape(b, nb, BLOCK, hk, g, dh)

    def band(t):
        t = t.reshape(b, nb, BLOCK, hk, dh)
        prev = jnp.concatenate([jnp.zeros_like(t[:, :1]), t[:, :-1]], axis=1)
        return jnp.concatenate([prev, t], axis=2)

    kc, vc = band(k), band(v)
    s = jnp.einsum('bnqhgd,bnkhd->bnhgqk', qb, kc).astype(jnp.float32) * (dh ** -0.5)
    dist = jnp.arange(BLOCK)[:, None] + BLOCK - jnp.arange(2 * BLOCK)[None, :]
    kpos = jnp.arange(nb)[:, None] * BLOCK + jnp.arange(2 * BLOCK)[None, :] - BLOCK
    valid = ((dist >= 0) & (dist <= max_dist))[None] & (kpos >= 0)[:, None, :]
    s = s - slopes[:, :, None, None] * (dist * unit).astype(jnp.float32)
    s = jnp.where(valid[None, :, None, None], s, -jnp.inf)
    lse = jax.nn.logsumexp(s, axis=-1)
    if sink is not None:
        lse = jnp.logaddexp(lse, sink.astype(jnp.float32)[:, :, None])
    p = jnp.exp(s - lse[..., None]).astype(v.dtype)
    out = jnp.einsum('bnhgqk,bnkhd->bnqhgd', p, vc).reshape(b, L, hk, g, dh)
    lse = jnp.moveaxis(lse, -1, 2).reshape(b, L, hk, g)
    return out, lse

def causal_block_attention(q, k, v, cum=None):
    b, S, h, dk = q.shape
    nb = S // BLOCK
    kpos = jnp.arange(S)
    cum_t = None if cum is None else jnp.swapaxes(cum, 1, 2)

    def one_block(n):
        start = n * BLOCK
        qblk = lax.dynamic_slice_in_dim(q, start, BLOCK, axis=1)
        s = jnp.einsum('bqhd,bkhd->bhqk', qblk, k).astype(jnp.float32) * (dk ** -0.5)
        if cum_t is not None:
            cq = lax.dynamic_slice_in_dim(cum_t, start, BLOCK, axis=2)
            s = s + cq[..., None] - cum_t[:, :, None, :]
        qpos = start + jnp.arange(BLOCK)
        s = jnp.where(kpos[None, :] <= qpos[:, None], s, -jnp.inf)
        p = jax.nn.softmax(s, axis=-1).astype(v.dtype)
        return jnp.einsum('bhqk,bkhd->bqhd', p, v)

    out = lax.map(one_block, jnp.arange(nb))
    return jnp.moveaxis(out, 0, 1).reshape(b, S, h, v.shape[-1])

def dilated_attention(q, k, v, slopes):
    b, S, h, dh = q.shape
    Sp = -(-S // DIL_ALIGN) * DIL_ALIGN
    pad = ((0, 0), (0, Sp - S), (0, 0), (0, 0))
    q, k, v = (jnp.pad(t, pad) for t in (q, k, v))
    outs, lses = [], []
    for window, dil in DILATED_PAIRS:
        L = Sp // dil

        def fold(t):
            return t.reshape(b, L, dil, h, dh).transpose(0, 2, 1, 3, 4).reshape(b * dil, L, h, dh)

        o, lse = banded_attention(fold(q)[:, :, :, None], fold(k), fold(v), window // dil, dil, slopes[:, None])
        outs.append(o[:, :, :, 0].reshape(b, dil, L, h, dh).transpose(0, 2, 1, 3, 4).reshape(b, Sp, h, dh))
        lses.append(lse[..., 0].reshape(b, dil, L, h).transpose(0, 2, 1, 3).reshape(b, Sp, h))
    w = jax.nn.softmax(jnp.stack(lses), axis=0).astype(q.dtype)
    out = jnp.einsum('nbsh,nbshd->bshd', w, jnp.stack(outs))
    return out[:, :S]

def hierarchical_moe(xn, w_rg, b_rg, w_re, b_re, w1, w3, w2):
    b, S, d = xn.shape
    xt = xn.reshape(-1, d)
    T = xt.shape[0]
    g_prob = jax.nn.softmax((xt @ w_rg).astype(jnp.float32) + b_rg.astype(jnp.float32), axis=-1)
    g_sel = jnp.argmax(g_prob, axis=-1)
    p_g = jnp.max(g_prob, axis=-1)
    e_logit = ((xt @ w_re).astype(jnp.float32) + b_re.astype(jnp.float32)).reshape(T, N_GROUPS, EXPERTS_PER_GROUP)
    e_logit = jnp.take_along_axis(e_logit, g_sel[:, None, None], axis=1)[:, 0]
    top_p, top_i = lax.top_k(jax.nn.softmax(e_logit, axis=-1), TOP_K)
    gate = p_g[:, None] * top_p / jnp.sum(top_p, axis=-1, keepdims=True)
    expert = g_sel[:, None] * EXPERTS_PER_GROUP + top_i

    A = T * TOP_K
    flat_e = expert.reshape(-1)
    flat_tok = jnp.repeat(jnp.arange(T), TOP_K)
    flat_gate = gate.reshape(-1)
    order = jnp.argsort(flat_e)
    se = flat_e[order]
    counts = jnp.bincount(flat_e, length=N_EXPERTS)
    start = jnp.cumsum(counts) - counts
    padded = (counts + EXPERT_BLOCK - 1) // EXPERT_BLOCK * EXPERT_BLOCK
    pend = jnp.cumsum(padded)
    pstart = pend - padded
    dest = pstart[se] + jnp.arange(A) - start[se]
    nblk = -(-A // EXPERT_BLOCK) + N_EXPERTS
    P = nblk * EXPERT_BLOCK
    buf_tok = jnp.zeros((P,), jnp.int32).at[dest].set(flat_tok[order])
    buf_gate = jnp.zeros((P,), jnp.float32).at[dest].set(flat_gate[order])
    blk_e = jnp.minimum(jnp.searchsorted(pend, jnp.arange(nblk) * EXPERT_BLOCK, side='right'), N_EXPERTS - 1)
    xbuf = xt[buf_tok].reshape(nblk, EXPERT_BLOCK, d)

    def expert_block(args):
        xb, e = args
        hid = jax.nn.silu(xb @ w1[e]) * (xb @ w3[e])
        return hid @ w2[e]

    ybuf = lax.map(expert_block, (xbuf, blk_e)).reshape(P, d)
    y = jnp.zeros((T, d), xn.dtype).at[buf_tok].add(ybuf * buf_gate[:, None].astype(ybuf.dtype))
    return y.reshape(b, S, d)

def hybrid_layer(x, norm1_g, w_in, mla_gcq, mla_gckv, mla_wuq, mla_wukv, qk_gq, qk_gk, fox_bf, sink, w_o,
                 norm2_g, w_rg, b_rg, w_re, b_re, w1, w3, w2):
    b, S, _ = x.shape
    H, hd = HEADS_PER_MIXER, HEAD_DIM
    slopes_dil, slopes_swa = alibi_slopes()
    u = rmsnorm(x, norm1_g)
    proj = u @ w_in
    offs = [int(o) for o in np.cumsum(IN_SPLITS)[:-1]]
    cq, ckv, kr, pb, pc, fg, pdq, pdkv = jnp.split(proj, offs, axis=-1)

    qa = (rmsnorm(cq, mla_gcq) @ mla_wuq).reshape(b, S, H, MLA_NOPE + MLA_ROPE)
    kva = (rmsnorm(ckv, mla_gckv) @ mla_wukv).reshape(b, S, H, MLA_NOPE + MLA_V)
    ka = jnp.concatenate([kva[..., :MLA_NOPE], jnp.broadcast_to(kr[:, :, None, :], (b, S, H, MLA_ROPE))], axis=-1)
    va = kva[..., MLA_NOPE:]
    qa = rmsnorm(qa, qk_gq[0])
    ka = rmsnorm(ka, qk_gk[0])
    qa = jnp.concatenate([qa[..., :MLA_NOPE], rope(qa[..., MLA_NOPE:])], axis=-1)
    ka = jnp.concatenate([ka[..., :MLA_NOPE], rope(ka[..., MLA_NOPE:])], axis=-1)
    oa = causal_block_attention(qa, ka, va)

    pb = pb.reshape(b, S, 3, H, hd)
    ob = dilated_attention(rmsnorm(pb[:, :, 0], qk_gq[1]), rmsnorm(pb[:, :, 1], qk_gk[1]), pb[:, :, 2], slopes_dil)

    pc = pc.reshape(b, S, 3, H, hd)
    cum = jnp.cumsum(jax.nn.log_sigmoid(fg.astype(jnp.float32) + fox_bf.astype(jnp.float32)), axis=1)
    oc = causal_block_attention(rmsnorm(pc[:, :, 0], qk_gq[2]), rmsnorm(pc[:, :, 1], qk_gk[2]), pc[:, :, 2], cum)

    qd = rmsnorm(pdq.reshape(b, S, SWA_KV_HEADS, SWA_GROUP, hd), qk_gq[3])
    pdkv = pdkv.reshape(b, S, 2, SWA_KV_HEADS, hd)
    od, _ = banded_attention(qd, rmsnorm(pdkv[:, :, 0], qk_gk[3]), pdkv[:, :, 1], SWA_WINDOW - 1, 1,
                             slopes_swa.reshape(SWA_KV_HEADS, SWA_GROUP), sink.reshape(SWA_KV_HEADS, SWA_GROUP))

    mix = jnp.concatenate([oa.reshape(b, S, GROUP_WIDTH), ob.reshape(b, S, GROUP_WIDTH),
                           oc.reshape(b, S, GROUP_WIDTH), od.reshape(b, S, GROUP_WIDTH)], axis=-1)
    h = x + mix @ w_o
    return h + hierarchical_moe(rmsnorm(h, norm2_g), w_rg, b_rg, w_re, b_re, w1, w3, w2)

def setup_inputs(seed: int = 0) -> dict:
    key = jax.random.key(seed)
    ks = jax.random.split(key, 20)

    def nrm(k, shape, scale):
        return jax.random.normal(k, shape, jnp.float32) * scale

    def gain(k, shape):
        return 1.0 + 0.02 * jax.random.normal(k, shape, jnp.float32)

    H = HEADS_PER_MIXER
    return {
        'x': nrm(ks[0], (BATCH, SEQ, D_MODEL), 1.0),
        'norm1_g': gain(ks[1], (DEPTH, D_MODEL)),
        'w_in': nrm(ks[2], (DEPTH, D_MODEL, IN_WIDTH), D_MODEL ** -0.5),
        'mla_gcq': gain(ks[3], (DEPTH, MLA_Q_RANK)),
        'mla_gckv': gain(ks[4], (DEPTH, MLA_KV_RANK)),
        'mla_wuq': nrm(ks[5], (DEPTH, MLA_Q_RANK, H * (MLA_NOPE + MLA_ROPE)), MLA_Q_RANK ** -0.5),
        'mla_wukv': nrm(ks[6], (DEPTH, MLA_KV_RANK, H * (MLA_NOPE + MLA_V)), MLA_KV_RANK ** -0.5),
        'qk_gq': gain(ks[7], (DEPTH, N_MIXERS, HEAD_DIM)),
        'qk_gk': gain(ks[8], (DEPTH, N_MIXERS, HEAD_DIM)),
        'fox_bf': 2.0 + 0.5 * jax.random.normal(ks[9], (DEPTH, H), jnp.float32),
        'sink': nrm(ks[10], (DEPTH, H), 0.5),
        'w_o': nrm(ks[11], (DEPTH, MIX_WIDTH, D_MODEL), 0.5 * MIX_WIDTH ** -0.5),
        'norm2_g': gain(ks[12], (DEPTH, D_MODEL)),
        'w_rg': nrm(ks[13], (DEPTH, D_MODEL, N_GROUPS), D_MODEL ** -0.5),
        'b_rg': nrm(ks[14], (DEPTH, N_GROUPS), 0.01),
        'w_re': nrm(ks[15], (DEPTH, D_MODEL, N_EXPERTS), D_MODEL ** -0.5),
        'b_re': nrm(ks[16], (DEPTH, N_EXPERTS), 0.01),
        'w1': nrm(ks[17], (DEPTH, N_EXPERTS, D_MODEL, D_EXPERT), D_MODEL ** -0.5),
        'w3': nrm(ks[18], (DEPTH, N_EXPERTS, D_MODEL, D_EXPERT), D_MODEL ** -0.5),
        'w2': nrm(ks[19], (DEPTH, N_EXPERTS, D_EXPERT, D_MODEL), D_EXPERT ** -0.5),
    }

def reference(x, norm1_g, w_in, mla_gcq, mla_gckv, mla_wuq, mla_wukv, qk_gq, qk_gk, fox_bf, sink, w_o,
              norm2_g, w_rg, b_rg, w_re, b_re, w1, w3, w2):
    for l in range(DEPTH):
        x = hybrid_layer(x, norm1_g[l], w_in[l], mla_gcq[l], mla_gckv[l], mla_wuq[l], mla_wukv[l], qk_gq[l],
                         qk_gk[l], fox_bf[l], sink[l], w_o[l], norm2_g[l], w_rg[l], b_rg[l], w_re[l], b_re[l],
                         w1[l], w3[l], w2[l])
    return x


_drawn_inputs = setup_inputs


def setup_inputs(seed=0):
    import zlib

    import numpy as np

    out = dict(_drawn_inputs(seed))
    spreads = {}
    factors = {'norm1_g': 2.763,
     'mla_gcq': 6.918,
     'mla_gckv': 5.742,
     'qk_gq': 3.596,
     'qk_gk': 4.575,
     'sink': 8.0}
    for name, (base, spread) in spreads.items():
        noise = np.random.default_rng([zlib.crc32(name.encode()), seed]).standard_normal(out[name].shape)
        drawn = base * np.exp(spread * noise) if base else spread * noise
        out[name] = jnp.asarray(drawn.astype(out[name].dtype))
    for name, factor in factors.items():
        out[name] = (out[name] * factor).astype(out[name].dtype)
    return out
```

```python
from contextlib import ExitStack

import concourse.bass as bass
from concourse import mybir

ALU = mybir.AluOpType
ACT = mybir.ActivationFunctionType
AX = mybir.AxisListType
F32 = mybir.dt.float32
I32 = mybir.dt.int32
U32 = mybir.dt.uint32

P = 128
EPS = 1e-6
NEG = -1e30
HD = 64
HEADS = 4
MIXERS = 4
NQR, NKV, NROPE, NNOPE = 192, 128, 32, 32
GW = HEADS * HD
CHUNKS = (352, 384, 384, 384, 388, 512)
AUG = HD + 2
BIG = 1e30


class Signal:

    def __init__(self, sem, per_pass):
        self.sem, self.per_pass = sem, per_pass

    def at(self, done, k):
        return done * self.per_pass + k


def trunk(nc, ins, consts, scratch, out):
    x_in = ins["x"]
    _, SEQ, D = x_in.shape
    L = ins["w_in"].shape[0]
    NT = SEQ // P
    KT = D // P
    E = ins["w1"].shape[1]
    F = ins["w1"].shape[3]
    NG = ins["w_rg"].shape[2]
    PER = E // NG
    R = NG + E
    ROUNDS = SEQ // P
    W1D = sum(CHUNKS)
    coff = [sum(CHUNKS[:c]) for c in range(len(CHUNKS))]
    widths = (3 * GW, 3 * GW, 3 * GW, 2 * GW)
    pbase = [NT * sum(widths[:m]) for m in range(MIXERS)]

    out_f = out.rearrange("b s d -> (b s) d")
    x_f = x_in.rearrange("b s d -> (b s) d")
    xn_dram, y_dram, table = scratch["xn"], scratch["y"], scratch["table"]

    ctx = ExitStack()
    with ctx:
        def sb(name, shape, dt=F32):
            return ctx.enter_context(nc.sbuf_tensor(name, shape, dt))

        def counted(name, per_pass):
            return Signal(ctx.enter_context(nc.semaphore(name)), per_pass)

        r_proj = sb("r_proj", [P, NT * sum(widths)])
        r_win = sb("r_win", [P, KT * W1D])
        r_tile = sb("r_tile", [P, 8 * SEQ])
        bank_pairs = [ctx.enter_context(nc.psum_tensor(f"banks{b}", [P, 1024], F32)) for b in range(4)]
        banks = [bank_pairs[b // 2][:, 512 * (b % 2):512 * (b % 2) + 512] for b in range(8)]

        ident = sb("ident", [P, P])
        ones = sb("ones", [P, P])
        w_lat = sb("w_lat", [P, 2 * GW + 384])
        upto = sb("upto", [P, P])
        before = sb("before", [P, P])
        cos_sin = sb("cos_sin", [P, 2, NT, NROPE // 2])
        iota = sb("iota", [P, E])
        tokid = sb("tokid", [P, NT], I32)
        eps = sb("eps", [P, 1])
        gain1 = sb("gain1", [P, KT])
        gain2 = sb("gain2", [P, KT])
        gain_lat = sb("gain_lat", [P, 3])
        gain_a = sb("gain_a", [P, 2 * HEADS, HD])
        gain_raw = sb("gain_raw", [P, 2 * MIXERS])
        gain_qk = sb("gain_qk", [P, 2 * MIXERS])
        sink_b = sb("sink_b", [P, HEADS])
        fox_b = sb("fox_b", [P, HEADS])
        route_b = sb("route_b", [P, R])
        rx = sb("rx", [P, 2, 3])
        rl = sb("rl", [P, 2, 3, 2])
        ssq = sb("ssq", [P, NT, 30])
        rs = sb("rs", [P, NT, 30])
        fg = sb("fg", [P, NT, HEADS])
        fox = sb("fox", [P, 4, NT, HEADS])
        cum = sb("cum", [P, 2, NT, HEADS])
        rowmax = sb("rowmax", [P, 2])
        negmax = sb("negmax", [P, 2, NT])
        den = sb("den", [P, 2, NT])
        sinkexp = sb("sinkexp", [P, 2, NT])
        rden = sb("rden", [P, 2, NT])
        never = sb("never", [P, 1])
        gates = sb("gates", [P, NT, 2])
        base_row = sb("base_row", [P, NT, 2])
        rel = sb("rel", [P, NT, 2])
        nrounds = sb("nrounds", [1, 1], I32)
        junk = sb("junk", [P, 4])

        start_loads = counted("start_loads", 0)
        start_sets = counted("start_sets", 0)
        zeros_i = r_tile[:, 0:256].bitcast(I32)

        with nc.Block() as block:
            @block.sync
            def _(sp):
                n = 0
                for dst, src in ((ident[:, :], consts["ident"]), (ones[:, :], consts["ones"]),
                                 (upto[:, :], consts["upto"]), (before[:, :], consts["before"]),
                                 (cos_sin[:, :, :, :], consts["cos_sin"]), (iota[:, :], consts["iota"]),
                                 (tokid[:, :], consts["tokid"]), (out_f, x_f)):
                    sp.dma_start(dst, src).then_inc(start_loads.sem, 16)
                    n += 16
                sp.wait_ge(start_sets.sem, 1)
                sp.dma_start(table.rearrange("(p c) o -> p (c o)", p=P), zeros_i).then_inc(start_loads.sem, 16)
                sp.wait_ge(start_loads.sem, n + 16)

            @block.vector
            def _(dve):
                nc.vector.memset(zeros_i, 0).then_inc(start_sets.sem, 1)
                nc.vector.memset(eps[:, :], EPS)
                nc.vector.memset(never[:, :], NEG)
                nc.vector.memset(gain_raw[:, :], 1.0)
                nc.vector.memset(gain_qk[:, :], 1.0)
                nc.vector.memset(gain_lat[:, :], 1.0)
                nc.vector.memset(junk[:, :], 0.0)

        s = Shared()
        s.D = D
        s.E = E
        s.F = F
        s.KT = KT
        s.NG = NG
        s.NT = NT
        s.PER = PER
        s.R = R
        s.SEQ = SEQ
        s.bank_pairs = bank_pairs
        s.banks = banks
        s.base_row = base_row
        s.before = before
        s.coff = coff
        s.consts = consts
        s.cos_sin = cos_sin
        s.counted = counted
        s.cum = cum
        s.den = den
        s.eps = eps
        s.fg = fg
        s.fox = fox
        s.fox_b = fox_b
        s.gain1 = gain1
        s.gain2 = gain2
        s.gain_a = gain_a
        s.gain_lat = gain_lat
        s.gain_qk = gain_qk
        s.gain_raw = gain_raw
        s.gates = gates
        s.ident = ident
        s.ins = ins
        s.iota = iota
        s.junk = junk
        s.negmax = negmax
        s.never = never
        s.nrounds = nrounds
        s.ones = ones
        s.out_f = out_f
        s.pbase = pbase
        s.r_proj = r_proj
        s.r_tile = r_tile
        s.r_win = r_win
        s.rden = rden
        s.rel = rel
        s.rl = rl
        s.route_b = route_b
        s.rowmax = rowmax
        s.rs = rs
        s.rx = rx
        s.sink_b = sink_b
        s.sinkexp = sinkexp
        s.ssq = ssq
        s.start_sets = start_sets
        s.table = table
        s.tokid = tokid
        s.upto = upto
        s.w_lat = w_lat
        s.widths = widths
        s.xn_dram = xn_dram
        s.y_dram = y_dram
        project_sems = project_signals(s)
        attend_sems = attend_signals(s)
        out_sems = out_signals(s)
        route_sems = route_signals(s)
        expert_sems = expert_signals(s)

        rounds_done = {}
        for eng in (nc.sync, nc.scalar, nc.vector, nc.gpsimd, nc.tensor):
            rounds_done[eng.engine] = eng.alloc_register("rounds_done")
            eng.reg_mov(rounds_done[eng.engine], 0)
        s.rounds_done = rounds_done
        s.attend_sems = attend_sems
        s.wait_value = {e.engine: e.alloc_register("wait_value") for e in (nc.sync, nc.scalar, nc.vector, nc.gpsimd, nc.tensor)}

        with nc.Fori(0, L) as layer:
            project(nc, s, project_sems, layer)
            attend(nc, s, attend_sems, layer)
            out_route(nc, s, out_sems, layer)
            route(nc, s, route_sems, layer)
            rounds = nc.values_load(nrounds[0:1, 0:1], min_val=1, max_val=ROUNDS)
            with nc.Fori(0, rounds) as rnd:
                experts(nc, s, expert_sems, layer, rnd)



class Shared:
    pass


def bcast(ap, shape):
    return ap.to_broadcast(shape)


def project_signals(s):
    sig = s.counted
    NT = s.NT
    g = Shared()
    g.w_in = [sig(f"w_in_loaded{c}", 16) for c in range(len(CHUNKS))]
    g.small = sig("layer_tables_loaded", 0)
    g.x = [sig(f"x_loaded{j}", 16 * NT // 2) for j in range(2)]
    g.x_sq = sig("x_squares_summed", NT)
    g.x_rt = sig("x_root_taken", NT)
    g.x_r = sig("x_scale_ready", NT)
    g.xT = sig("x_transposed", NT)
    g.uT = sig("uT_ready", 2 * NT)
    g.mm = sig("projected", 6 * NT)
    g.mo = sig("projection_out", 7 * NT + 3)
    g.l_sq = sig("latent_squares_summed", 2 * NT)
    g.l_rt = sig("latent_root_taken", NT)
    g.l_r = sig("latent_scale_ready", NT)
    g.lT = sig("latent_transposed", NT)
    g.lo = sig("latentT_ready", 3 * NT)
    g.am = sig("latents_expanded", NT)
    g.ao = sig("mixer_a_out", 4 * NT + 1)
    g.rope = sig("rope_steps", 7 * NT)
    g.sq = sig("head_squares_ready", 4 * NT)
    g.red = sig("head_squares_summed", NT + 1)
    g.wl = sig("expand_weights_loaded", 0)
    g.gq = sig("gain_tables_ready", 1)
    return g


def project(nc, s, g, layer):
    P_, NT, KT = P, s.NT, s.KT
    D = s.D
    x_t = [s.r_tile[:, j * 1024:(j + 1) * 1024] for j in range(2)]
    uT = [s.r_tile[:, 2048 + j * 1024:2048 + (j + 1) * 1024].rearrange("p (k n) -> p k n", n=P) for j in range(2)]
    uT_flat = [s.r_tile[:, 2048 + j * 1024:2048 + (j + 1) * 1024] for j in range(2)]
    latT_flat = [s.r_tile[:, 4800 + j * 384:4800 + (j + 1) * 384] for j in range(2)]
    lat = [s.r_tile[:, 4096 + j * 352:4096 + (j + 1) * 352] for j in range(2)]
    latT = [s.r_tile[:, 4800 + j * 384:4800 + (j + 1) * 384].rearrange("p (k n) -> p k n", n=P) for j in range(2)]
    sqb = s.r_tile[:, 5568:5568 + 1920]
    rot = s.r_tile[:, 7488:7488 + 512].rearrange("p (a h c) -> p a h c", a=4, h=8)
    w_ch = [s.r_win[:, KT * s.coff[c]:KT * (s.coff[c] + CHUNKS[c])].rearrange("p (k n) -> p k n", k=KT)
            for c in range(6)]
    pm = [s.r_proj[:, s.pbase[m]:s.pbase[m] + NT * s.widths[m]].rearrange("p (t n) -> p t n", t=NT)
          for m in range(4)]
    s.pm = pm
    w_l = s.w_lat
    bk = s.banks
    ins = s.ins

    def blockfn(block):
        @block.sync
        def _(sp):
            for c in range(6):
                src = ins["w_in"][layer].rearrange("(p k) n -> p k n", k=KT)[:, :, s.coff[c]:s.coff[c] + CHUNKS[c]]
                sp.dma_start(w_ch[c], src).then_inc(g.w_in[c].sem, 16)
                if c == 0:
                    for j in range(2):
                        sp.dma_start(x_t[j], s.out_f[j * P:(j + 1) * P]).then_inc(g.x[j].sem, 16)
            with sp.Fori(0, NT // 2 - 1) as i:
                for j in range(2):
                    sp.wait_ge(g.uT.sem, g.uT.at(layer, 2 * (2 * i + j + 1)))
                    sp.dma_start(x_t[j], s.out_f[bass.ds((2 * i + 2 + j) * P, P)]).then_inc(g.x[j].sem, 16)

        @block.tensor
        def _(pe):
            def transpose_x(i, j):
                pe.wait_ge(g.x[j].sem, g.x[j].at(layer, 16 * (i + 1)))
                xs = x_t[j].rearrange("p (q k) -> p k q", k=KT)
                for k in range(KT):
                    mm = pe.transpose(bk[3 + k // 4][:, (k % 4) * P:(k % 4 + 1) * P], xs[:, k, :], s.ident[:, :])
                mm.then_inc(g.xT.sem, 1)

            def tile(i, j, last):
                t = 2 * i + j

                def chunk(c):
                    n = 6 * j + c
                    b = n % 3
                    pe.wait_ge(g.w_in[c].sem, g.w_in[c].at(layer, 16))
                    if c == 0:
                        pe.wait_ge(g.uT.sem, g.uT.at(layer, 2 * t + 2))
                    prev = n - 3
                    reads = 7 * (prev // 6) + (prev % 6 + 1) + (1 if prev % 6 >= 4 else 0)
                    if n > 0:
                        pe.wait_ge(g.mo.sem, g.mo.at(layer, 14 * i + reads + 3))
                    for k in range(KT):
                        mm = pe.matmul(bk[b][:, 0:CHUNKS[c]], uT[j][:, k, :], w_ch[c][:, k, :],
                                       start=(k == 0), stop=(k == KT - 1))
                    mm.then_inc(g.mm.sem, 1)

                chunk(0)
                chunk(1)
                if not last:
                    transpose_x(i + (j + 1) // 2, (j + 1) % 2)
                chunk(2)
                chunk(3)
                pe.wait_ge(g.mo.sem, g.mo.at(layer, 7 * t + 4))
                for n, (a, b) in enumerate(((0, 128), (128, 192), (192, 320))):
                    mm = pe.transpose(bk[5][0:b - a, n * P:(n + 1) * P], lat[j][:, a:b], s.ident[:, :])
                mm.then_inc(g.lT.sem, 1)
                chunk(4)
                chunk(5)
                pe.wait_ge(g.lo.sem, g.lo.at(layer, 3 * t + 3))
                pe.wait_ge(g.wl.sem, layer * 48 + 48)
                pe.wait_ge(g.ao.sem, g.ao.at(layer, 4 * t + 1))
                pe.matmul(bk[6][:, 0:GW], latT[j][:, 0, :], w_l[:, 0:GW], start=True, stop=False)
                pe.matmul(bk[6][:, 0:GW], latT[j][0:64, 1, :], w_l[0:64, GW:2 * GW], start=False, stop=True)
                pe.matmul(bk[7][:, 0:384], latT[j][:, 2, :], w_l[:, 2 * GW:2 * GW + 384],
                          start=True, stop=True).then_inc(g.am.sem, 1)

            transpose_x(0, 0)
            with pe.Fori(0, NT // 2 - 1) as i:
                tile(i, 0, False)
                tile(i, 1, False)
            tile(NT // 2 - 1, 0, False)
            tile(NT // 2 - 1, 1, True)

        @block.scalar
        def _(act):
            act.dma_start(w_l[:, 0:GW], ins["mla_wuq"][layer][0:128]).then_inc(g.wl.sem, 16)
            act.dma_start(w_l[0:64, GW:2 * GW], ins["mla_wuq"][layer][128:192]).then_inc(g.wl.sem, 16)
            act.dma_start(w_l[:, 2 * GW:2 * GW + 384], ins["mla_wukv"][layer]).then_inc(g.wl.sem, 16)
            tabs = []
            for gain, name in ((s.gain1, "norm1_g"), (s.gain2, "norm2_g")):
                tabs.append((gain[:, :], ins[name][layer].rearrange("(p k) -> p k", k=KT)))
            gq, gk = ins["qk_gq"][layer], ins["qk_gk"][layer]
            cq, ck = ins["mla_gcq"][layer], ins["mla_gckv"][layer]
            tabs.append((s.gain_lat[:, 0:1], cq[0:128].rearrange("(p o) -> p o", o=1)))
            tabs.append((s.gain_lat[0:64, 1:2], cq[128:192].rearrange("(p o) -> p o", o=1)))
            tabs.append((s.gain_lat[:, 2:3], ck.rearrange("(p o) -> p o", o=1)))
            for h in range(HEADS):
                tabs.append((s.gain_a[:, h, :], gq[0].partition_broadcast(P)))
                tabs.append((s.gain_a[:, HEADS + h, :], gk[0].partition_broadcast(P)))
            for m in range(1, MIXERS):
                tabs.append((s.gain_raw[0:HD, m:m + 1], gq[m].rearrange("(p o) -> p o", o=1)))
                tabs.append((s.gain_raw[0:HD, MIXERS + m:MIXERS + m + 1], gk[m].rearrange("(p o) -> p o", o=1)))
            for dst, name in ((s.sink_b[:, :], "sink"), (s.fox_b[:, :], "fox_bf"), (s.route_b[:, 0:s.NG], "b_rg"),
                              (s.route_b[:, s.NG:s.R], "b_re")):
                tabs.append((dst, ins[name][layer].partition_broadcast(P)))
            for dst, src in tabs:
                act.dma_start(dst, src).then_inc(g.small.sem, 16)
            g.small.per_pass = 16 * len(tabs)
            act.wait_ge(g.small.sem, g.small.at(layer, 16 * len(tabs)))

            def square_x(i, j):
                t = 2 * i + j
                act.wait_ge(g.x[j].sem, g.x[j].at(layer, 16 * (i + 1)))
                nc.scalar.activation(uT_flat[j], x_t[j], ACT.Square, scale=D ** -0.5,
                                     accum_out=s.rx[:, j, 0:1]).then_inc(g.x_sq.sem, 1)
                act.wait_ge(g.x_sq.sem, g.x_sq.at(layer, t + 1))
                nc.scalar.activation(s.rx[:, j, 1:2], s.rx[:, j, 0:1], ACT.Sqrt,
                                     bias=s.eps[:, 0:1]).then_inc(g.x_rt.sem, 1)

            def tile(i, j, last):
                t = 2 * i + j

                def evac(c):
                    n = 6 * j + c
                    b = n % 3
                    act.wait_ge(g.mm.sem, g.mm.at(layer, 6 * t + c + 1))
                    if c == 0:
                        act.wait_ge(g.x_r.sem, g.x_r.at(layer, t + 1))
                        dst = lat[j]
                    elif c < 3:
                        dst = pm[1][:, t, (c - 1) * 384:c * 384]
                    elif c < 5:
                        dst = pm[2][:, t, (c - 3) * 384:(c - 2) * 384]
                    else:
                        dst = pm[3][:, t, :]
                    if c == 4:
                        nc.scalar.activation(s.fg[:, t, :], bk[b][:, 384:388], ACT.Copy,
                                             scale=s.rx[:, j, 2:3]).then_inc(g.mo.sem, 1)
                    nc.scalar.activation(dst, bk[b][:, 0:(384 if c == 4 else CHUNKS[c])], ACT.Copy,
                                         scale=s.rx[:, j, 2:3]).then_inc(g.mo.sem, 1)

                evac(0)
                act.wait_ge(g.mo.sem, g.mo.at(layer, 7 * t + 4))
                nc.scalar.activation(latT_flat[j][:, 0:192], lat[j][:, 0:192], ACT.Square, scale=192 ** -0.5,
                                     accum_out=s.rl[:, j, 0, 0:1]).then_inc(g.l_sq.sem, 1)
                nc.scalar.activation(latT_flat[j][:, 192:320], lat[j][:, 192:320], ACT.Square, scale=128 ** -0.5,
                                     accum_out=s.rl[:, j, 0, 1:2]).then_inc(g.l_sq.sem, 1)
                act.wait_ge(g.l_sq.sem, g.l_sq.at(layer, 2 * t + 2))
                nc.scalar.activation(s.rl[:, j, 1, :], s.rl[:, j, 0, :], ACT.Sqrt,
                                     bias=s.eps[:, 0:1]).then_inc(g.l_rt.sem, 1)
                evac(1)
                if not last:
                    square_x(i + (j + 1) // 2, (j + 1) % 2)
                evac(2)
                evac(3)
                act.wait_ge(g.lT.sem, g.lT.at(layer, t + 1))
                for n in range(3):
                    q = 64 if n == 1 else P
                    nc.scalar.activation(latT[j][0:q, n, :], bk[5][0:q, n * P:(n + 1) * P], ACT.Copy,
                                         scale=s.gain_lat[0:q, n:n + 1]).then_inc(g.lo.sem, 1)
                evac(4)
                evac(5)

            nc.scalar.activation(s.junk[:, 1:2], s.eps[:, 0:1], ACT.Copy).then_inc(g.mo.sem, 3)
            square_x(0, 0)
            with act.Fori(0, NT // 2 - 1) as i:
                tile(i, 0, False)
                tile(i, 1, False)
            tile(NT // 2 - 1, 0, False)
            tile(NT // 2 - 1, 1, True)

        @block.vector
        def _(dve):
            dve.wait_ge(g.small.sem, g.small.at(layer, g.small.per_pass))
            nc.vector.tensor_scalar(s.gain_qk[0:HD, 0:MIXERS], s.gain_raw[0:HD, 0:MIXERS], HD ** -0.5, None,
                                    ALU.mult)
            nc.vector.tensor_copy(s.gain_qk[0:HD, MIXERS:2 * MIXERS],
                                  s.gain_raw[0:HD, MIXERS:2 * MIXERS]).then_inc(g.gq.sem, 1)
            nc.vector.memset(s.junk[:, 0:1], 0.0).then_inc(g.red.sem, 1)
            nc.vector.memset(s.junk[:, 2:3], 0.0).then_inc(g.ao.sem, 1)

            def evac_x(i, j):
                t = 2 * i + j
                dve.wait_ge(g.x_rt.sem, g.x_rt.at(layer, t + 1))
                nc.vector.reciprocal(s.rx[:, j, 2:3], s.rx[:, j, 1:2]).then_inc(g.x_r.sem, 1)
                dve.wait_ge(g.xT.sem, g.xT.at(layer, t + 1))
                for half in range(2):
                    nc.vector.tensor_tensor(
                        uT[j][:, 4 * half:4 * half + 4, :], bk[3 + half][:, :].rearrange("p (k n) -> p k n", k=4),
                        bcast(s.gain1[:, 4 * half:4 * half + 4].unsqueeze(2), [P, 4, P]),
                        ALU.mult).then_inc(g.uT.sem, 1)

            def tile(i, j, last):
                t = 2 * i + j
                if not last:
                    evac_x(i + (j + 1) // 2, (j + 1) % 2)
                dve.wait_ge(g.l_rt.sem, g.l_rt.at(layer, t + 1))
                nc.vector.reciprocal(s.rl[:, j, 2, :], s.rl[:, j, 1, :]).then_inc(g.l_r.sem, 1)
                pa = pm[0][:, t, :]
                kva = bk[7][:, 0:384].rearrange("p (h c) -> p h c", h=HEADS)
                ka = pa[:, GW:2 * GW].rearrange("p (h c) -> p h c", h=HEADS)
                dve.wait_ge(g.am.sem, g.am.at(layer, t + 1))
                dve.wait_ge(g.l_r.sem, g.l_r.at(layer, t + 1))
                nc.vector.tensor_scalar(pa[:, 0:GW], bk[6][:, 0:GW], s.rl[:, j, 2, 0:1], None,
                                        ALU.mult).then_inc(g.ao.sem, 1)
                nc.vector.tensor_scalar(ka[:, :, 0:NNOPE], kva[:, :, 0:NNOPE], s.rl[:, j, 2, 1:2], None,
                                        ALU.mult).then_inc(g.ao.sem, 1)
                nc.vector.tensor_scalar(pa[:, 2 * GW:3 * GW].rearrange("p (h c) -> p h c", h=HEADS),
                                        kva[:, :, NNOPE:NNOPE + HD], s.rl[:, j, 2, 1:2], None,
                                        ALU.mult).then_inc(g.ao.sem, 1)
                nc.vector.tensor_tensor(ka[:, :, NNOPE:HD],
                                        bcast(lat[j][:, 320:352].unsqueeze(1), [P, HEADS, NROPE]),
                                        bcast(s.ones[:, 0:NROPE].unsqueeze(1), [P, HEADS, NROPE]),
                                        ALU.mult).then_inc(g.ao.sem, 1)
                dve.wait_ge(g.sq.sem, g.sq.at(layer, 4 * t + 4))
                nc.vector.tensor_reduce(s.ssq[:, t, :], sqb.rearrange("p (h c) -> p h c", c=HD), AX.X,
                                        ALU.add).then_inc(g.red.sem, 1)

            evac_x(0, 0)
            with dve.Fori(0, NT // 2 - 1) as i:
                tile(i, 0, False)
                tile(i, 1, False)
            tile(NT // 2 - 1, 0, False)
            tile(NT // 2 - 1, 1, True)

        @block.gpsimd
        def _(pool):
            wait_alone(pool, s, g.small.sem, g.small.at(layer, g.small.per_pass))

            def tile(i, j):
                t = 2 * i + j
                wait_alone(pool, s, g.red.sem, g.red.at(layer, t + 1))
                wait_alone(pool, s, g.ao.sem, g.ao.at(layer, 4 * t + 5))
                qk = pm[0][:, t, 0:2 * GW]
                nc.gpsimd.tensor_tensor(sqb[:, 0:512], qk, qk, ALU.mult).then_inc(g.sq.sem, 1)
                wait_alone(pool, s, g.sq.sem, g.sq.at(layer, 4 * t + 1))
                nc.gpsimd.tensor_tensor(qk, qk, s.gain_a[:, :, :].rearrange("p h c -> p (h c)"),
                                        ALU.mult).then_inc(g.rope.sem, 1)
                hv = qk.rearrange("p (h c) -> p h c", c=HD)
                x1, x2 = hv[:, :, 32:48], hv[:, :, 48:64]
                co = bcast(s.cos_sin[:, 0, t, :].unsqueeze(1), [P, 8, 16])
                si = bcast(s.cos_sin[:, 1, t, :].unsqueeze(1), [P, 8, 16])
                wait_alone(pool, s, g.rope.sem, g.rope.at(layer, 7 * t + 1))
                for a, (u, v) in enumerate(((x1, co), (x2, si), (x2, co), (x1, si))):
                    nc.gpsimd.tensor_tensor(rot[:, a], u, v, ALU.mult).then_inc(g.rope.sem, 1)
                wait_alone(pool, s, g.rope.sem, g.rope.at(layer, 7 * t + 5))
                nc.gpsimd.tensor_tensor(x1, rot[:, 0], rot[:, 1], ALU.subtract).then_inc(g.rope.sem, 1)
                nc.gpsimd.tensor_tensor(x2, rot[:, 2], rot[:, 3], ALU.add).then_inc(g.rope.sem, 1)
                for m, reads in ((1, 3), (2, 6), (3, 7)):
                    w = 512 if m < 3 else 384
                    wait_alone(pool, s, g.mo.sem, g.mo.at(layer, 7 * t + reads + 3))
                    pq = pm[m][:, t, 0:w]
                    nc.gpsimd.tensor_tensor(sqb[:, 512 * m:512 * m + w], pq, pq, ALU.mult).then_inc(g.sq.sem, 1)

            with pool.Fori(0, NT // 2) as i:
                tile(i, 0)
                tile(i, 1)

    with nc.Block() as block:
        blockfn(block)


def key_span(m, qb):
    k0 = max(0, qb - 1) * P if m == 3 else 0
    return k0, (qb + 1) * P - k0


def groups(m, qb):
    return -(-key_span(m, qb)[1] // 512)


def attend_signals(s):
    sig = s.counted
    NT = s.NT
    pgroups = sum(HEADS * sum(groups(m, qb) for qb in range(NT)) for m in range(MIXERS))
    g = Shared()
    g.rt = sig("head_roots_taken", 1)
    g.rsr = sig("head_scales_ready", 1)
    g.fxd = sig("fox_vector_steps", 3)
    g.fxa = sig("fox_scalar_steps", 3)
    g.fxp = sig("fox_summed", 1)
    g.fxo = sig("fox_cumulated", 2)
    g.causal = sig("causal_table_loaded", 16)
    g.bias = [sig(f"bias_table_loaded{j}", 16 * 4) for j in range(2)]
    g.wo = sig("w_o_loaded", 16)
    g.stage = sig("heads_scaled", 2 * HEADS * MIXERS + 2 * HEADS)
    g.qkt = sig("qk_transposed", 4 * HEADS * MIXERS)
    g.qko = sig("qkT_ready", 4 * HEADS * MIXERS)
    g.lg = sig("logits_done", NT * HEADS * MIXERS)
    g.mx = sig("logits_biased", NT * HEADS * MIXERS + 2)
    g.ng = sig("negmax_ready", NT * HEADS * MIXERS)
    g.ex = sig("weights_ready", NT * HEADS * MIXERS)
    g.pt = sig("weights_transposed", pgroups)
    g.po = sig("weightsT_ready", pgroups)
    g.pv = sig("values_summed", NT * HEADS * MIXERS)
    g.sk = sig("sink_terms_ready", HEADS)
    g.dn = sig("denominators_ready", HEADS * (MIXERS + 1))
    g.on = sig("heads_normalised", HEADS * MIXERS)
    g.ot = sig("mix_transposed", 2 * 2 * MIXERS)
    g.oo = sig("mixT_ready", 2 * 2 * MIXERS + 2)
    return g


def attend(nc, s, g, layer):
    NT, SEQ = s.NT, s.SEQ
    bk, pairs, pm = s.banks, s.bank_pairs, s.pm
    w = s.r_win
    qs = [w[:, j * 528:(j + 1) * 528].rearrange("p (t c) -> p t c", c=AUG) for j in range(2)]
    ks = [w[:, 1056 + j * 528:1056 + (j + 1) * 528].rearrange("p (t c) -> p t c", c=AUG) for j in range(2)]
    qT = [w[:, 2112 + j * 1024:2112 + (j + 1) * 1024] for j in range(2)]
    kT = [w[:, 4160 + j * 1024:4160 + (j + 1) * 1024] for j in range(2)]
    sbuf = [w[:, 6208 + j * 1024:6208 + (j + 1) * 1024] for j in range(2)]
    pT = [w[:, 8256 + j * 1024:8256 + (j + 1) * 1024] for j in range(2)]
    causal = w[:, 10304:11328]
    bias = [w[:, 11328 + j * 1024:11328 + (j + 1) * 1024] for j in range(2)]
    o_s = w[:, 13376:14400].rearrange("p (t c) -> p t c", c=P)
    mixT = s.r_tile[:, :].rearrange("p (k n) -> p k n", k=8)
    s.w_o = s.r_proj[:, 0:8192].rearrange("p (k n) -> p k n", k=8)
    pg_base = [sum(HEADS * sum(groups(q, b) for b in range(NT)) for q in range(m)) for m in range(MIXERS)]
    st_base = [2 * HEADS * m + (2 * HEADS if m == 3 else 0) for m in range(MIXERS)]
    dn_base = [HEADS * m for m in range(MIXERS)]
    neg_cum, pos_cum = s.cum[:, 1], s.cum[:, 0]

    with nc.Block() as block:
        @block.sync
        def _(sp):
            sp.dma_start(causal, s.consts["causal"]).then_inc(g.causal.sem, 16)
            for m in (1, 3):
                if m == 3:
                    sp.wait_ge(g.on.sem, g.on.at(layer, 2 * HEADS))
                    sp.dma_start(s.w_o, s.ins["w_o"][layer].rearrange("(k p) n -> p k n", p=P)).then_inc(g.wo.sem, 16)
                with sp.Fori(0, HEADS // 2) as hp:
                    for j in range(2):
                        sp.wait_ge(g.mx.sem, g.mx.at(layer, 2 + NT * (HEADS * m + 2 * hp + j - 1)))
                        if m == 1:
                            sp.dma_start(bias[j], s.consts["dilated"][2 * hp + j]).then_inc(g.bias[j].sem, 16)
                        else:
                            sp.dma_start(bias[j][:, 0:2 * P], s.consts["window"][2 * hp + j]).then_inc(
                                g.bias[j].sem, 16)

        @block.tensor
        def _(pe):
            pe.wait_ge(g.fxd.sem, g.fxd.at(layer, 3))
            ls = s.fox[:, 3]
            mm = pe.matmul(bk[6][:, 0:NT * HEADS], s.upto[:, :], ls.rearrange("p t h -> p (t h)"),
                           start=True, stop=False)
            for t in range(NT - 1):
                left = NT - 1 - t
                mm = pe.matmul(bk[6][:, (t + 1) * HEADS:NT * HEADS], s.ones[:, :],
                               bcast(ls[:, t:t + 1, :], [P, left, HEADS]),
                               start=False, stop=(t == NT - 2))
            mm.then_inc(g.fxp.sem, 1)

            for m in range(MIXERS):
                K = AUG if m == 2 else HD
                per_pair = 2 * sum(groups(m, qb) for qb in range(NT))

                def pair(hp):
                    n0 = HEADS * m + 2 * hp
                    ring = []

                    def bank_for(kind):
                        gi = len(ring)
                        if gi >= 2:
                            prev = ring[gi - 2]
                            c = sum(1 for x in ring[:gi - 1] if x == prev)
                        else:
                            prev, c = "o", gi - 1
                        if prev == "qk":
                            wait_alone(pe, s, g.qko.sem, g.qko.at(layer, 4 * n0 + c))
                        elif prev == "p":
                            wait_alone(pe, s, g.po.sem, g.po.at(layer, pg_base[m] + hp * per_pair + c))
                        else:
                            wait_alone(pe, s, g.oo.sem, g.oo.at(layer, 2 + n0 + c))
                        ring.append(kind)
                        return bk[4 + gi % 2]

                    def logits(j, qb):
                        idx = NT * (n0 + j) + qb
                        k0, nk = key_span(m, qb)
                        pe.wait_ge(g.mx.sem, g.mx.at(layer, idx + 1))
                        for c in range(0, nk, 512):
                            cw = min(512, nk - c)
                            mm = pe.matmul(bk[2 * (qb % 2) + c // 512][:, 0:cw], qT[j][0:K, qb * P:(qb + 1) * P],
                                           kT[j][0:K, k0 + c:k0 + c + cw], start=True, stop=True)
                        mm.then_inc(g.lg.sem, 1)

                    def values(j, qb):
                        idx = NT * (n0 + j) + qb
                        k0, nk = key_span(m, qb)
                        pe.wait_ge(g.ex.sem, g.ex.at(layer, idx + 1))
                        for c in range(0, nk, 512):
                            bank = bank_for("p")
                            for b in range(0, min(512, nk - c), P):
                                mm = pe.transpose(bank[:, b:b + P], sbuf[qb % 2][:, c + b:c + b + P], s.ident[:, :])
                            mm.then_inc(g.pt.sem, 1)
                        done = sum(1 for x in ring if x == "p")
                        pe.wait_ge(g.po.sem, g.po.at(layer, pg_base[m] + hp * per_pair + done))
                        h = 2 * hp + j
                        v0 = 384 + HD * hp if m == 3 else 2 * GW + HD * h
                        for b in range(0, nk, P):
                            mm = pe.matmul(bk[6 + j][:, qb * HD:(qb + 1) * HD], pT[qb % 2][:, b:b + P],
                                           pm[m][:, (k0 + b) // P, bass.ds(v0, HD)],
                                           start=(b == 0), stop=(b == nk - P))
                        mm.then_inc(g.pv.sem, 1)

                    for j in range(2):
                        stages = st_base[m] + (4 if m == 2 else 2) * (2 * hp + j + 1)
                        pe.wait_ge(g.stage.sem, g.stage.at(layer, stages))
                        for src in (qs[j], ks[j]):
                            for half in range(2):
                                bank = bank_for("qk")
                                for t in range(4):
                                    mm = pe.transpose(bank[0:K, t * P:(t + 1) * P], src[:, 4 * half + t, 0:K],
                                                      s.ident[:, :])
                                mm.then_inc(g.qkt.sem, 1)
                        pe.wait_ge(g.qko.sem, g.qko.at(layer, 4 * (n0 + j) + 4))
                        logits(j, 0)
                        for qb in range(1, NT):
                            logits(j, qb)
                            values(j, qb - 1)
                        values(j, NT - 1)
                    pe.wait_ge(g.on.sem, g.on.at(layer, n0 + 2))
                    for half in range(2):
                        bank = bank_for("o")
                        for t in range(4):
                            mm = pe.transpose(bank[:, t * P:(t + 1) * P], o_s[:, 4 * half + t, :], s.ident[:, :])
                        mm.then_inc(g.ot.sem, 1)

                if m == 0:
                    wait_alone(pe, s, g.fxo.sem, g.fxo.at(layer, 2))
                with pe.Fori(0, HEADS // 2) as hp:
                    pair(hp)

        @block.scalar
        def _(act):
            nc.scalar.activation(s.rs[:, :, :], s.ssq[:, :, :], ACT.Sqrt, scale=1.0 / HD,
                                 bias=s.eps[:, 0:1]).then_inc(g.rt.sem, 1)
            act.wait_ge(g.fxd.sem, g.fxd.at(layer, 1))
            nc.scalar.activation(s.fox[:, 1], s.fox[:, 0], ACT.Abs).then_inc(g.fxa.sem, 1)
            act.wait_ge(g.fxa.sem, g.fxa.at(layer, 1))
            nc.scalar.activation(s.fox[:, 1], s.fox[:, 1], ACT.Exp, scale=-1.0).then_inc(g.fxa.sem, 1)
            act.wait_ge(g.fxa.sem, g.fxa.at(layer, 2))
            nc.scalar.activation(s.fox[:, 2], s.fox[:, 1], ACT.Ln, bias=s.ones[:, 0:1]).then_inc(g.fxa.sem, 1)
            for m in range(MIXERS):
                per_pair = 2 * sum(groups(m, qb) for qb in range(NT))

                def pair(hp):
                    n0 = HEADS * m + 2 * hp
                    pg = 0

                    for j in range(2):
                        for step in range(NT + 1):
                            if step < NT:
                                qb = step
                                idx = NT * (n0 + j) + qb
                                k0, nk = key_span(m, qb)
                                act.wait_ge(g.ng.sem, g.ng.at(layer, idx + 1))
                                nc.scalar.activation(sbuf[qb % 2][:, 0:nk], sbuf[qb % 2][:, 0:nk], ACT.Exp,
                                                     bias=s.negmax[:, j, qb:qb + 1],
                                                     accum_out=s.den[:, j, qb:qb + 1]).then_inc(g.ex.sem, 1)
                            if step >= 1:
                                qb = step - 1
                                k0, nk = key_span(m, qb)
                                for c in range(0, nk, 512):
                                    cw = min(512, nk - c)
                                    pg += 1
                                    gi = ring_at[(j, qb, c)]
                                    act.wait_ge(g.pt.sem, g.pt.at(layer, pg_base[m] + hp * per_pair + pg))
                                    nc.scalar.activation(pT[qb % 2][:, c:c + cw], bk[4 + gi % 2][:, 0:cw],
                                                         ACT.Copy).then_inc(g.po.sem, 1)
                        if m == 3:
                            h = 2 * hp + j
                            nc.scalar.activation(s.sinkexp[:, j, :], s.negmax[:, j, :], ACT.Exp,
                                                 bias=s.sink_b[:, bass.ds(h, 1)]).then_inc(g.sk.sem, 1)

                ring_at, gi = {}, 0
                for j in range(2):
                    gi += 4
                    for qb in range(NT):
                        for c in range(0, key_span(m, qb)[1], 512):
                            ring_at[(j, qb, c)] = gi
                            gi += 1
                with act.Fori(0, HEADS // 2) as hp:
                    pair(hp)

        @block.vector
        def _(dve):
            nc.vector.memset(s.junk[:, 0:1], 0.0).then_inc(g.mx.sem, 2)
            nc.vector.memset(s.junk[:, 2:3], 0.0).then_inc(g.oo.sem, 2)
            for j in range(2):
                nc.vector.memset(qs[j][:, :, HD:HD + 1], 1.0)
                nc.vector.memset(ks[j][:, :, HD + 1:HD + 2], 1.0)
            dve.wait_ge(g.rt.sem, g.rt.at(layer, 1))
            nc.vector.reciprocal(s.rs[:, :, :], s.rs[:, :, :]).then_inc(g.rsr.sem, 1)
            nc.vector.tensor_tensor(s.fox[:, 0], s.fg[:, :, :], bcast(s.fox_b[:, :].unsqueeze(1), [P, NT, HEADS]),
                                    ALU.add).then_inc(g.fxd.sem, 1)
            dve.wait_ge(g.fxa.sem, g.fxa.at(layer, 3))
            dve.wait_ge(g.fxd.sem, g.fxd.at(layer, 1))
            nc.vector.tensor_scalar(s.fox[:, 3], s.fox[:, 0], 0.0, None, ALU.min).then_inc(g.fxd.sem, 1)
            dve.wait_ge(g.fxd.sem, g.fxd.at(layer, 2))
            nc.vector.tensor_tensor(s.fox[:, 3], s.fox[:, 3], s.fox[:, 2], ALU.subtract).then_inc(g.fxd.sem, 1)
            dve.wait_ge(g.fxp.sem, g.fxp.at(layer, 1))
            flat = bk[6][:, 0:NT * HEADS].rearrange("p (t h) -> p t h", h=HEADS)
            nc.vector.tensor_copy(pos_cum, flat).then_inc(g.fxo.sem, 1)
            nc.vector.tensor_scalar(neg_cum, flat, -1.0, None, ALU.mult).then_inc(g.fxo.sem, 1)
            dve.wait_ge(g.rsr.sem, g.rsr.at(layer, 1))
            dve.wait_ge(g.causal.sem, g.causal.at(layer, 16))
            wait_alone(dve, s, g.fxo.sem, g.fxo.at(layer, 2))

            for m in range(MIXERS):
                K = AUG if m == 2 else HD

                def pair(hp):
                    n0 = HEADS * m + 2 * hp
                    for j in range(2):
                        n = n0 + j
                        h = 2 * hp + j
                        kv = hp if m == 3 else h
                        for dst, col, r in ((qs[j], HD * h, 8 * m + h), (ks[j], GW + HD * kv, 8 * m + HEADS + kv)):
                            nc.vector.tensor_tensor(dst[:, :, 0:HD], pm[m][:, :, bass.ds(col, HD)],
                                                    bcast(s.rs[:, :, bass.ds(r, 1)], [P, NT, HD]),
                                                    ALU.mult).then_inc(g.stage.sem, 1)
                        if m == 2:
                            nc.vector.tensor_scalar(ks[j][:, :, HD:HD + 1], neg_cum[:, :, bass.ds(h, 1)], 1.0, None,
                                                    ALU.mult).then_inc(g.stage.sem, 1)
                            nc.vector.tensor_scalar(qs[j][:, :, HD + 1:AUG], pos_cum[:, :, bass.ds(h, 1)], 1.0, None,
                                                    ALU.mult).then_inc(g.stage.sem, 1)
                        for a, dst in enumerate((qT[j], kT[j])):
                            for half in range(2):
                                dve.wait_ge(g.qkt.sem, g.qkt.at(layer, 4 * n + 2 * a + half + 1))
                                gi = ring_qk[j] + 2 * a + half
                                nc.vector.tensor_scalar(dst[0:K, 512 * half:512 * half + 512],
                                                        bk[4 + gi % 2][0:K, :],
                                                        s.gain_qk[0:K, MIXERS * a + m:MIXERS * a + m + 1], None,
                                                        ALU.mult).then_inc(g.qko.sem, 1)
                        if m in (1, 3):
                            dve.wait_ge(g.bias[j].sem, g.bias[j].at(layer, (32 if m == 3 else 0) + 16 * (hp + 1)))
                        for qb in range(NT):
                            idx = NT * n + qb
                            k0, nk = key_span(m, qb)
                            tab = bias[j][:, 2 * P - nk:2 * P] if m == 3 else (
                                (bias[j] if m == 1 else causal)[:, SEQ - nk:SEQ])
                            wait_alone(dve, s, g.lg.sem, g.lg.at(layer, idx + 1))
                            nc.vector.tensor_tensor_reduce(out=sbuf[qb % 2][:, 0:nk], in0=pairs[qb % 2][:, 0:nk],
                                                           in1=tab, scale=1.0, scalar=-3e38, op0=ALU.add,
                                                           op1=ALU.max,
                                                           accum_out=s.rowmax[:, qb % 2:qb % 2 + 1]).then_inc(
                                                               g.mx.sem, 1)
                            dve.wait_ge(g.mx.sem, g.mx.at(layer, 2 + idx + 1))
                            floor = s.sink_b[:, bass.ds(h, 1)] if m == 3 else s.never[:, 0:1]
                            nc.vector.tensor_scalar(s.negmax[:, j, qb:qb + 1], s.rowmax[:, qb % 2:qb % 2 + 1], floor,
                                                    -1.0, ALU.max, ALU.mult).then_inc(g.ng.sem, 1)
                        dve.wait_ge(g.pv.sem, g.pv.at(layer, NT * (n + 1)))
                        if m == 3:
                            dve.wait_ge(g.sk.sem, g.sk.at(layer, h + 1))
                            nc.vector.tensor_tensor(s.den[:, j, :], s.den[:, j, :], s.sinkexp[:, j, :],
                                                    ALU.add).then_inc(g.dn.sem, 1)
                            dve.wait_ge(g.dn.sem, g.dn.at(layer, dn_base[m] + 2 * h + 1))
                            dn = dn_base[m] + 2 * h + 2
                        else:
                            dn = dn_base[m] + h + 1
                        nc.vector.reciprocal(s.rden[:, j, :], s.den[:, j, :]).then_inc(g.dn.sem, 1)
                        dve.wait_ge(g.dn.sem, g.dn.at(layer, dn))
                        nc.vector.tensor_tensor(o_s[:, :, HD * j:HD * (j + 1)],
                                                bk[6 + j][:, :].rearrange("p (t c) -> p t c", c=HD),
                                                bcast(s.rden[:, j, :].unsqueeze(2), [P, NT, HD]),
                                                ALU.mult).then_inc(g.on.sem, 1)
                    for half in range(2):
                        dve.wait_ge(g.ot.sem, g.ot.at(layer, n0 + half + 1))
                        gi = ring_o + half
                        nc.vector.tensor_scalar(mixT[:, bass.ds(2 * m + hp, 1), 512 * half:512 * half + 512],
                                                bk[4 + gi % 2].unsqueeze(1), 1.0, None,
                                                ALU.mult).then_inc(g.oo.sem, 1)

                per_head = sum(groups(m, qb) for qb in range(NT))
                ring_qk = [0, 4 + per_head]
                ring_o = 8 + 2 * per_head
                with dve.Fori(0, HEADS // 2) as hp:
                    pair(hp)


def over_pairs(eng, n, body):
    body(0)
    with eng.Fori(1, n - 1) as i:
        body(i)
    body(n - 1)


def first(i):
    return isinstance(i, int) and i == 0


def out_signals(s):
    sig = s.counted
    NT = s.NT
    half = 16 * NT // 2
    g = Shared()
    g.wr = sig("router_weights_loaded", 32)
    g.x = [sig(f"residual_loaded{j}", half) for j in range(2)]
    g.hs = [sig(f"h_stored{j}", half) for j in range(2)]
    g.xs = [sig(f"normed_stored{j}", half) for j in range(2)]
    g.mt = sig("mix_tile_ready", NT)
    g.wo = sig("output_projected", NT)
    g.h = sig("h_ready", NT)
    g.sq = sig("h_squares_summed", NT)
    g.rt = sig("h_root_taken", NT)
    g.r = sig("h_scale_ready", NT)
    g.xn = sig("normed_ready", NT)
    g.xt = sig("normed_transposed", NT)
    g.xo = sig("normedT_ready", 2 * NT)
    g.lm = sig("router_logits_done", NT)
    g.lo = sig("router_logits_out", NT)
    return g


def out_route(nc, s, g, layer):
    NT, KT, D, R, NG = s.NT, s.KT, s.D, s.R, s.NG
    bk, pairs, ins = s.banks, s.bank_pairs, s.ins
    w = s.r_proj

    def pair_of(at, n):
        return [w[:, at + j * n:at + (j + 1) * n] for j in range(2)]

    mt = [a.rearrange("p (k n) -> p k n", k=KT) for a in pair_of(8192, 1024)]
    x_t, h_t, xn_t = pair_of(10240, 1024), pair_of(12288, 1024), pair_of(14336, 1024)
    xnT = [a.rearrange("p (k n) -> p k n", k=KT) for a in pair_of(16384, 1024)]
    w_r = w[:, 18432:18432 + KT * R].rearrange("p (k n) -> p k n", k=KT)
    s.lg = lg = w[:, 18720:18720 + NT * R].rearrange("p (t n) -> p t n", t=NT)
    mixT = s.r_tile[:, :].rearrange("p (k n) -> p k n", k=KT)
    NP = NT // 2

    def rows(dram, i, j):
        return dram[bass.ds((2 * i + j) * P, P)]

    with nc.Block() as block:
        @block.sync
        def _(sp):
            sp.dma_start(w_r[:, :, 0:NG], ins["w_rg"][layer].rearrange("(p k) n -> p k n", k=KT)).then_inc(
                g.wr.sem, 16)
            sp.dma_start(w_r[:, :, NG:R], ins["w_re"][layer].rearrange("(p k) n -> p k n", k=KT)).then_inc(
                g.wr.sem, 16)

            def body(i):
                for j in range(2):
                    if not first(i):
                        sp.wait_ge(g.h.sem, g.h.at(layer, 2 * i + j - 1))
                    sp.dma_start(x_t[j], rows(s.out_f, i, j)).then_inc(g.x[j].sem, 16)
                for j in range(2):
                    t = 2 * i + j
                    sp.wait_ge(g.h.sem, g.h.at(layer, t + 1))
                    sp.dma_start(rows(s.out_f, i, j), h_t[j]).then_inc(g.hs[j].sem, 16)
                    sp.wait_ge(g.xn.sem, g.xn.at(layer, t + 1))
                    sp.dma_start(rows(s.xn_dram, i, j), xn_t[j]).then_inc(g.xs[j].sem, 16)

            over_pairs(sp, NP, body)
            for j in range(2):
                wait_alone(sp, s, g.hs[j].sem, g.hs[j].at(layer, 16 * NP))
                wait_alone(sp, s, g.xs[j].sem, g.xs[j].at(layer, 16 * NP))

        @block.tensor
        def _(pe):
            def project_tile(i, j):
                t = 2 * i + j
                pe.wait_ge(g.mt.sem, g.mt.at(layer, t + 1))
                for c in range(2):
                    for k in range(KT):
                        mm = pe.matmul(bk[2 * j + c][:, :], mt[j][:, k, :], s.w_o[:, k, 512 * c:512 * c + 512],
                                       start=(k == 0), stop=(k == KT - 1))
                mm.then_inc(g.wo.sem, 1)

            def body(i):
                for j in range(2):
                    t = 2 * i + j
                    if not (isinstance(i, int) and i == NP - 1 and j == 1):
                        project_tile(i + j, 1 - j)
                    pe.wait_ge(g.xn.sem, g.xn.at(layer, t + 1))
                    xs = xn_t[j].rearrange("p (q k) -> p k q", k=KT)
                    for k in range(KT):
                        mm = pe.transpose(bk[4 + k // 4][:, (k % 4) * P:(k % 4 + 1) * P], xs[:, k, :], s.ident[:, :])
                    mm.then_inc(g.xt.sem, 1)
                    pe.wait_ge(g.xo.sem, g.xo.at(layer, 2 * t + 2))
                    if not (first(i) and j == 0):
                        pe.wait_ge(g.lo.sem, g.lo.at(layer, t))
                    for k in range(KT):
                        mm = pe.matmul(bk[6][:, 0:R], xnT[j][:, k, :], w_r[:, k, :], start=(k == 0),
                                       stop=(k == KT - 1))
                    mm.then_inc(g.lm.sem, 1)

            s_wo = s.attend_sems.wo
            pe.wait_ge(s_wo.sem, s_wo.at(layer, 16))
            pe.wait_ge(g.wr.sem, g.wr.at(layer, 32))
            project_tile(0, 0)
            over_pairs(pe, NP, body)

        @block.scalar
        def _(act):
            def body(i):
                for j in range(2):
                    t = 2 * i + j
                    act.wait_ge(g.h.sem, g.h.at(layer, t + 1))
                    if not first(i):
                        act.wait_ge(g.xs[j].sem, g.xs[j].at(layer, 16 * i))
                    nc.scalar.activation(xn_t[j], h_t[j], ACT.Square, scale=D ** -0.5,
                                         accum_out=s.rx[:, j, 0:1]).then_inc(g.sq.sem, 1)
                    act.wait_ge(g.sq.sem, g.sq.at(layer, t + 1))
                    nc.scalar.activation(s.rx[:, j, 1:2], s.rx[:, j, 0:1], ACT.Sqrt,
                                         bias=s.eps[:, 0:1]).then_inc(g.rt.sem, 1)
                    act.wait_ge(g.r.sem, g.r.at(layer, t + 1))
                    nc.scalar.activation(xn_t[j], h_t[j], ACT.Copy, scale=s.rx[:, j, 2:3]).then_inc(g.xn.sem, 1)

            over_pairs(act, NP, body)

        @block.vector
        def _(dve):
            def stage_mix(i, j):
                nc.vector.tensor_scalar(mt[j], mixT[:, :, bass.ds((2 * i + j) * P, P)], 1.0, None,
                                        ALU.mult).then_inc(g.mt.sem, 1)

            def body(i):
                for j in range(2):
                    t = 2 * i + j
                    dve.wait_ge(g.wo.sem, g.wo.at(layer, t + 1))
                    dve.wait_ge(g.x[j].sem, g.x[j].at(layer, 16 * (i + 1)))
                    if not first(i):
                        dve.wait_ge(g.hs[j].sem, g.hs[j].at(layer, 16 * i))
                    nc.vector.tensor_tensor(h_t[j], pairs[j][:, :], x_t[j], ALU.add).then_inc(g.h.sem, 1)
                    if not (isinstance(i, int) and i == NP - 1):
                        stage_mix(i + 1, j)
                    dve.wait_ge(g.rt.sem, g.rt.at(layer, t + 1))
                    nc.vector.reciprocal(s.rx[:, j, 2:3], s.rx[:, j, 1:2]).then_inc(g.r.sem, 1)
                    dve.wait_ge(g.xt.sem, g.xt.at(layer, t + 1))
                    for half in range(2):
                        nc.vector.tensor_tensor(
                            xnT[j][:, 4 * half:4 * half + 4, :], bk[4 + half].rearrange("p (k n) -> p k n", k=4),
                            bcast(s.gain2[:, 4 * half:4 * half + 4].unsqueeze(2), [P, 4, P]),
                            ALU.mult).then_inc(g.xo.sem, 1)
                    dve.wait_ge(g.lm.sem, g.lm.at(layer, t + 1))
                    nc.vector.tensor_tensor(lg[:, t, :], bk[6][:, 0:R], s.route_b[:, :], ALU.add).then_inc(
                        g.lo.sem, 1)

            stage_mix(0, 0)
            stage_mix(0, 1)
            over_pairs(dve, NP, body)


def route_signals(s):
    sig = s.counted
    g = Shared()
    g.v = sig("routing_vector_steps", 0)
    g.e = sig("routing_exps", 2)
    g.p = sig("routing_counted", 2)
    g.sc = sig("slots_scattered", 32 * s.NT)
    return g


def route(nc, s, g, layer):
    NT, NG, PER, E = s.NT, s.NG, s.PER, s.E
    bk, lg, t_ = s.banks, s.lg, s.r_tile
    at = [0]

    def take(*shape, dt=F32):
        n = 1
        for x in shape:
            n *= x
        a = t_[:, at[0]:at[0] + n]
        at[0] += n
        if dt is not F32:
            a = a.bitcast(dt)
        if len(shape) == 2:
            a = a.rearrange("p (a b) -> p a b", a=shape[0])
        return a

    m0, m1, mm_ = take(NT, E), take(NT, E), take(NT, E)
    pos, prod, masked = take(NT, E), take(NT, E), take(NT, E)
    gl, gm, em = take(NT, 8), take(NT, 8), take(NT, 8)
    gi, ei = take(NT, 8, dt=U32), take(NT, 8, dt=U32)
    oh, dg, eg = take(NT, NG), take(NT, NG), take(NT, NG)
    gif, pg, d, ed, den = take(NT, 1), take(NT, 1), take(NT, 1), take(NT, 1), take(NT, 1)
    eif, slf = take(NT, 2), take(NT, 2)
    slots = take(NT, 2, dt=I32)
    cnt, cnti = take(1), take(1, dt=I32)
    steps = 16 + 16 + 28

    with nc.Block() as block:
        g.v.per_pass = ROUTE_STEPS

        @block.vector
        def _(dve):
            n = [0]

            def link(ins):
                n[0] += 1
                ins.then_inc(g.v.sem, 1)
                wait_alone(dve, s, g.v.sem, g.v.at(layer, n[0]))
                return n[0]

            v = nc.vector
            link(v.memset(gl[:, :, NG:8], NEG))
            link(v.tensor_copy(gl[:, :, 0:NG], lg[:, :, 0:NG]))
            for t in range(NT):
                link(v.max(gm[:, t, :], gl[:, t, :]))
                link(v.max_index(gi[:, t, :], gm[:, t, :], gl[:, t, :]))
            g.dg_at = link(v.tensor_tensor(dg, gl[:, :, 0:NG], bcast(gm[:, :, 0:1], [P, NT, NG]), ALU.subtract))
            link(v.tensor_copy(gif, gi[:, :, 0:1]))
            link(v.tensor_tensor(oh, bcast(s.iota[:, 0:NG].unsqueeze(1), [P, NT, NG]),
                                 bcast(gif, [P, NT, NG]), ALU.is_equal))
            link(v.tensor_scalar(oh, oh, -1.0, BIG, ALU.add, ALU.mult))
            for t in range(NT):
                link(v.tensor_tensor(masked[:, t, :].rearrange("p (g e) -> p g e", g=NG),
                                     lg[:, t, NG:NG + E].rearrange("p (g e) -> p g e", g=NG),
                                     bcast(oh[:, t, :].unsqueeze(2), [P, NG, PER]), ALU.add))
                link(v.max(em[:, t, :], masked[:, t, :]))
                link(v.max_index(ei[:, t, :], em[:, t, :], masked[:, t, :]))
            g.d_at = link(v.tensor_tensor(d, em[:, :, 1:2], em[:, :, 0:1], ALU.subtract))
            link(v.tensor_copy(eif, ei[:, :, 0:2]))
            link(v.tensor_tensor(m0, bcast(s.iota[:, :].unsqueeze(1), [P, NT, E]),
                                 bcast(eif[:, :, 0:1], [P, NT, E]), ALU.is_equal))
            link(v.tensor_tensor(m1, bcast(s.iota[:, :].unsqueeze(1), [P, NT, E]),
                                 bcast(eif[:, :, 1:2], [P, NT, E]), ALU.is_equal))
            g.m_at = link(v.tensor_tensor(mm_, m0, m1, ALU.add))
            dve.wait_ge(g.e.sem, g.e.at(layer, 1))
            link(v.tensor_reduce(pg, eg, AX.X, ALU.add))
            link(v.reciprocal(pg, pg))
            dve.wait_ge(g.e.sem, g.e.at(layer, 2))
            link(v.tensor_scalar(den, ed, 1.0, None, ALU.add))
            link(v.reciprocal(den, den))
            link(v.tensor_tensor(s.gates[:, :, 0:1], pg, den, ALU.mult))
            link(v.tensor_tensor(s.gates[:, :, 1:2], s.gates[:, :, 0:1], ed, ALU.mult))
            dve.wait_ge(g.p.sem, g.p.at(layer, 1))
            link(v.tensor_copy(pos, bk[0][:, 0:NT * E].rearrange("p (t e) -> p t e", t=NT)))
            for k, mk in enumerate((m0, m1)):
                link(v.tensor_tensor(prod, mk, pos, ALU.mult))
                link(v.tensor_reduce(s.rel[:, :, k:k + 1], prod, AX.X, ALU.add))
            link(v.scalar_tensor_tensor(out=slf, in0=s.rel[:, :, :], scalar=float(E), in1=eif, op0=ALU.mult,
                                        op1=ALU.add))
            g.slots_at = link(v.tensor_copy(slots, slf))
            link(v.scalar_tensor_tensor(out=s.base_row[:, :, :], in0=eif, scalar=float(P), in1=s.rel[:, :, :],
                                        op0=ALU.mult, op1=ALU.add))
            dve.wait_ge(g.p.sem, g.p.at(layer, 2))
            link(v.tensor_reduce(cnt[0:1], bk[1][0:1, 0:E], AX.X, ALU.max))
            link(v.tensor_scalar(cnti[0:1], cnt[0:1], float(P - 1), None, ALU.add))
            link(v.tensor_scalar(s.nrounds[0:1, 0:1], cnti[0:1], 7, None, ALU.logical_shift_right))
            assert n[0] == ROUTE_STEPS, n[0]

        @block.scalar
        def _(act):
            act.wait_ge(g.v.sem, g.v.at(layer, g.dg_at))
            nc.scalar.activation(eg, dg, ACT.Exp).then_inc(g.e.sem, 1)
            act.wait_ge(g.v.sem, g.v.at(layer, g.d_at))
            nc.scalar.activation(ed, d, ACT.Exp).then_inc(g.e.sem, 1)

        @block.tensor
        def _(pe):
            pe.wait_ge(g.v.sem, g.v.at(layer, g.m_at))
            pe.matmul(bk[0][:, 0:NT * E], s.before[:, :], mm_.rearrange("p t e -> p (t e)"), start=True, stop=False)
            for t in range(NT - 1):
                mm = pe.matmul(bk[0][:, (t + 1) * E:NT * E], s.ones[:, :],
                               bcast(mm_[:, t:t + 1, :], [P, NT - 1 - t, E]), start=False, stop=(t == NT - 2))
            mm.then_inc(g.p.sem, 1)
            for t in range(NT):
                mm = pe.matmul(bk[1][:, 0:E], s.ones[:, :], mm_[:, t, :], start=(t == 0), stop=(t == NT - 1))
            mm.then_inc(g.p.sem, 1)

        @block.gpsimd
        def _(pool):
            wait_alone(pool, s, g.v.sem, g.v.at(layer, g.slots_at))
            for t in range(NT):
                for k in range(2):
                    nc.gpsimd.indirect_dma_start(
                        out=s.table, out_offset=bass.IndirectOffsetOnAxis(ap=slots[:, t, k:k + 1], axis=0),
                        in_=s.tokid[:, t:t + 1], in_offset=None).then_inc(g.sc.sem, 16)
            wait_alone(pool, s, g.sc.sem, g.sc.at(layer, 32 * NT))


ROUTE_STEPS = 68


def wait_alone(eng, s, sem, value):
    reg = s.wait_value[eng.engine]
    eng.reg_mov(reg, value)
    value = eng.snap(reg)
    eng.wait_ge(s.start_sets.sem, 1)
    eng.wait_ge(sem, value)


def expert_signals(s):
    sig = s.counted
    E, NT = s.E, s.NT
    g = Shared()
    g.ix = sig("slot_tokens_loaded", 16)
    g.gx = [sig(f"tokens_gathered{j}", 8 * E) for j in range(2)]
    g.w13 = [sig(f"w1_w3_loaded{j}", 16 * E) for j in range(2)]
    g.w2 = [sig(f"w2_loaded{j}", 8 * E) for j in range(2)]
    g.xt = sig("tokens_transposed", E)
    g.xo = sig("tokensT_ready", 2 * E)
    g.hm = sig("hidden_done", E)
    g.sl = sig("silu_ready", E)
    g.hd = sig("hidden_ready", E)
    g.ht = sig("hidden_transposed", E)
    g.ho = sig("hiddenT_ready", E)
    g.ym = sig("expert_rows_done", E)
    g.ya = sig("expert_rows_out_scalar", E)
    g.yv = sig("expert_rows_out_vector", E)
    g.ys = [sig(f"expert_rows_stored{j}", 8 * E) for j in range(2)]
    g.ci = sig("combine_steps", 7)
    g.yg = [sig(f"expert_rows_gathered{j}", 16 * NT) for j in range(2)]
    g.hl = [sig(f"h_reloaded{j}", 8 * NT) for j in range(2)]
    g.ad = sig("expert_rows_added", 2 * NT)
    g.st = [sig(f"layer_stored{j}", 8 * NT) for j in range(2)]
    return g


def experts(nc, s, g, layer, rnd):
    NT, KT, E, F, D = s.NT, s.KT, s.E, s.F, s.D
    bk, pairs, ins = s.banks, s.bank_pairs, s.ins
    w = s.r_proj
    at = [0]

    def pair_of(n, region=w):
        at[0] += 2 * n
        return [region[:, at[0] - 2 * n + j * n:at[0] - n + j * n] for j in range(2)]

    w13 = [a.rearrange("p (k n) -> p k n", k=KT) for a in pair_of(KT * 2 * F)]
    w2 = [a.rearrange("p (k n) -> p k n", k=F // P) for a in pair_of(F // P * D)]
    xg = pair_of(D)
    xT = [a.rearrange("p (k n) -> p k n", k=KT) for a in pair_of(D)]
    sil, hid = pair_of(F), pair_of(F)
    hidT = [a.rearrange("p (k n) -> p k n", n=P) for a in pair_of(F)]
    y_t = pair_of(D)
    at[0] = 0
    h_t = pair_of(D, s.r_tile)
    yg = [[s.r_tile[:, 2048 + 1024 * (2 * j + k):3072 + 1024 * (2 * j + k)] for k in range(2)] for j in range(2)]
    idx = s.r_tile[:, 6144:6144 + E].bitcast(I32)
    small = s.r_tile[:, 6176:6176 + 5 * 2 * NT].rearrange("p (a b) -> p a b", a=5)
    va, vb = small[:, 0], small[:, 1]
    cidx, geff, vc = small[:, 2].bitcast(I32), small[:, 3], small[:, 4]
    NP = E // 2
    table_r = s.table.rearrange("(r p e) o -> r p (e o)", p=P, e=E)

    def count(eng):
        return eng.snap(s.rounds_done[eng.engine])

    def next_round(eng):
        eng.reg_add(s.rounds_done[eng.engine], s.rounds_done[eng.engine], 1)

    with nc.Block() as block:
        @block.sync
        def _(sp):
            done = count(sp)
            sp.dma_start(idx, table_r[rnd]).then_inc(g.ix.sem, 16)

            def body(i):
                for j in range(2):
                    e = 2 * i + j
                    if not first(i):
                        sp.wait_ge(g.hm.sem, g.hm.at(done, e - 1))
                    for c, name in enumerate(("w1", "w3")):
                        sp.dma_start(w13[j][:, :, F * c:F * (c + 1)],
                                     ins[name][layer, e].rearrange("(p k) n -> p k n", k=KT)).then_inc(
                                         g.w13[j].sem, 16)
                    if not first(i):
                        sp.wait_ge(g.ym.sem, g.ym.at(done, e - 1))
                    sp.dma_start(w2[j], ins["w2"][layer, e].rearrange("(k p) n -> p k n", p=P)).then_inc(
                        g.w2[j].sem, 16)

            over_pairs(sp, NP, body)
            for j in range(2):
                sp.wait_ge(g.ys[j].sem, g.ys[j].at(done, 8 * E))
            for t in range(NT):
                j = t % 2
                if t >= 2:
                    sp.wait_ge(g.ad.sem, g.ad.at(done, 2 * (t - 1)))
                    sp.dma_start(s.out_f[(t - 2) * P:(t - 1) * P], h_t[j]).then_inc(g.st[j].sem, 16)
                    sp.wait_ge(g.st[j].sem, g.st[j].at(done, 16 * (t // 2)))
                sp.dma_start(h_t[j], s.out_f[t * P:(t + 1) * P]).then_inc(g.hl[j].sem, 16)
            for t in range(NT - 2, NT):
                sp.wait_ge(g.ad.sem, g.ad.at(done, 2 * (t + 1)))
                sp.dma_start(s.out_f[t * P:(t + 1) * P], h_t[t % 2]).then_inc(g.st[t % 2].sem, 16)
            for j in range(2):
                wait_alone(sp, s, g.st[j].sem, g.st[j].at(done, 8 * NT))
            next_round(sp)

        @block.gpsimd
        def _(pool):
            done = count(pool)
            wait_alone(pool, s, g.ix.sem, g.ix.at(done, 16))
            for e in range(E):
                if e >= 2:
                    wait_alone(pool, s, g.xt.sem, g.xt.at(done, e - 1))
                nc.gpsimd.indirect_dma_start(
                    out=xg[e % 2], out_offset=None, in_=s.xn_dram,
                    in_offset=bass.IndirectOffsetOnAxis(ap=idx[:, e:e + 1], axis=0)).then_inc(g.gx[e % 2].sem, 16)
            for j in range(2):
                wait_alone(pool, s, g.ys[j].sem, g.ys[j].at(done, 8 * E))
            wait_alone(pool, s, g.ci.sem, g.ci.at(done, 5))
            for t in range(NT):
                if t >= 2:
                    wait_alone(pool, s, g.ad.sem, g.ad.at(done, 2 * (t - 1)))
                for k in range(2):
                    nc.gpsimd.indirect_dma_start(
                        out=yg[t % 2][k], out_offset=None, in_=s.y_dram,
                        in_offset=bass.IndirectOffsetOnAxis(ap=cidx[:, 2 * t + k:2 * t + k + 1], axis=0)).then_inc(
                            g.yg[t % 2].sem, 16)
            next_round(pool)

        @block.tensor
        def _(pe):
            done = count(pe)

            def transpose_tokens(i, j):
                pe.wait_ge(g.gx[j].sem, g.gx[j].at(done, 16 * (i + 1)))
                xs = xg[j].rearrange("p (q k) -> p k q", k=KT)
                for k in range(KT):
                    mm = pe.transpose(bk[k // 4][:, (k % 4) * P:(k % 4 + 1) * P], xs[:, k, :], s.ident[:, :])
                mm.then_inc(g.xt.sem, 1)

            def body(i):
                for j in range(2):
                    e = 2 * i + j
                    pe.wait_ge(g.w13[j].sem, g.w13[j].at(done, 32 * (i + 1)))
                    pe.wait_ge(g.xo.sem, g.xo.at(done, 2 * e + 2))
                    if not first(i):
                        pe.wait_ge(g.hd.sem, g.hd.at(done, e - 1))
                    for k in range(KT):
                        mm = pe.matmul(bk[2 + j][:, 0:2 * F], xT[j][:, k, :], w13[j][:, k, :], start=(k == 0),
                                       stop=(k == KT - 1))
                    mm.then_inc(g.hm.sem, 1)
                    if not (isinstance(i, int) and i == NP - 1 and j == 1):
                        transpose_tokens(i + j, 1 - j)
                    pe.wait_ge(g.hd.sem, g.hd.at(done, e + 1))
                    for k in range(F // P):
                        mm = pe.transpose(bk[4][:, k * P:(k + 1) * P], hid[j][:, k * P:(k + 1) * P], s.ident[:, :])
                    mm.then_inc(g.ht.sem, 1)
                    pe.wait_ge(g.ho.sem, g.ho.at(done, e + 1))
                    pe.wait_ge(g.w2[j].sem, g.w2[j].at(done, 16 * (i + 1)))
                    if not (first(i) and j == 0):
                        pe.wait_ge(g.ya.sem, g.ya.at(done, e))
                        pe.wait_ge(g.yv.sem, g.yv.at(done, e))
                    for c in range(2):
                        for k in range(F // P):
                            mm = pe.matmul(bk[6 + c][:, :], hidT[j][:, k, :], w2[j][:, k, 512 * c:512 * c + 512],
                                           start=(k == 0), stop=(k == F // P - 1))
                    mm.then_inc(g.ym.sem, 1)

            transpose_tokens(0, 0)
            over_pairs(pe, NP, body)
            next_round(pe)

        @block.scalar
        def _(act):
            done = count(act)

            def body(i):
                for j in range(2):
                    e = 2 * i + j
                    act.wait_ge(g.hm.sem, g.hm.at(done, e + 1))
                    nc.scalar.activation(sil[j], bk[2 + j][:, 0:F], ACT.Silu).then_inc(g.sl.sem, 1)
                    act.wait_ge(g.ht.sem, g.ht.at(done, e + 1))
                    nc.scalar.activation(hidT[j], bk[4][:, 0:F].rearrange("p (k n) -> p k n", n=P),
                                         ACT.Copy).then_inc(g.ho.sem, 1)
                    act.wait_ge(g.ym.sem, g.ym.at(done, e + 1))
                    if not first(i):
                        act.wait_ge(g.ys[j].sem, g.ys[j].at(done, 16 * i))
                    nc.scalar.activation(y_t[j][:, 0:512], bk[6][:, :], ACT.Copy).then_inc(g.ya.sem, 1)
                    act.wait_ge(g.ya.sem, g.ya.at(done, e + 1))
                    act.wait_ge(g.yv.sem, g.yv.at(done, e + 1))
                    act.dma_start(s.y_dram[bass.ds(e * P, P)], y_t[j]).then_inc(g.ys[j].sem, 16)

            over_pairs(act, NP, body)
            next_round(act)

        @block.vector
        def _(dve):
            done = count(dve)

            def evac_tokens(i, j):
                e = 2 * i + j
                dve.wait_ge(g.xt.sem, g.xt.at(done, e + 1))
                for half in range(2):
                    nc.vector.tensor_tensor(
                        xT[j][:, 4 * half:4 * half + 4, :], bk[half].rearrange("p (k n) -> p k n", k=4),
                        bcast(s.gain2[:, 4 * half:4 * half + 4].unsqueeze(2), [P, 4, P]),
                        ALU.mult).then_inc(g.xo.sem, 1)

            def body(i):
                for j in range(2):
                    e = 2 * i + j
                    dve.wait_ge(g.sl.sem, g.sl.at(done, e + 1))
                    nc.vector.tensor_tensor(hid[j], sil[j], bk[2 + j][:, F:2 * F], ALU.mult).then_inc(g.hd.sem, 1)
                    if not (isinstance(i, int) and i == NP - 1 and j == 1):
                        evac_tokens(i + j, 1 - j)
                    dve.wait_ge(g.ym.sem, g.ym.at(done, e + 1))
                    if not first(i):
                        dve.wait_ge(g.ys[j].sem, g.ys[j].at(done, 16 * i))
                    nc.vector.tensor_copy(y_t[j][:, 512:1024], bk[7][:, :]).then_inc(g.yv.sem, 1)

            def step(n, ins):
                ins.then_inc(g.ci.sem, 1)
                wait_alone(dve, s, g.ci.sem, g.ci.at(done, n))

            rel, base, gates = (a[:, :, :].rearrange("p t k -> p (t k)") for a in (s.rel, s.base_row, s.gates))
            step(1, nc.vector.tensor_scalar(va, rel, 0.0, None, ALU.is_ge))
            step(2, nc.vector.tensor_scalar(vb, rel, float(P), None, ALU.is_lt))
            step(3, nc.vector.tensor_tensor(vc, va, vb, ALU.mult))
            step(4, nc.vector.tensor_tensor(geff, vc, gates, ALU.mult))
            step(5, nc.vector.tensor_tensor(cidx, vc, base, ALU.mult))
            step(6, nc.vector.tensor_scalar(rel, rel, -float(P), None, ALU.add))
            step(7, nc.vector.tensor_scalar(base, base, -float(P), None, ALU.add))

            evac_tokens(0, 0)
            over_pairs(dve, NP, body)

            for t in range(NT):
                j = t % 2
                dve.wait_ge(g.hl[j].sem, g.hl[j].at(done, 16 * (t // 2 + 1)))
                dve.wait_ge(g.yg[j].sem, g.yg[j].at(done, 32 * (t // 2 + 1)))
                for k in range(2):
                    nc.vector.scalar_tensor_tensor(out=h_t[j], in0=yg[j][k], scalar=geff[:, 2 * t + k:2 * t + k + 1],
                                                   in1=h_t[j], op0=ALU.mult, op1=ALU.add).then_inc(g.ad.sem, 1)
                    if k == 0:
                        dve.wait_ge(g.ad.sem, g.ad.at(done, 2 * t + 1))
            next_round(dve)


def tables(seq, experts_n):
    import numpy as np

    p = np.arange(P)
    nt = seq // P
    slopes = 2.0 ** (-8.0 * np.arange(1, 2 * HEADS + 1) / (2 * HEADS))
    inv = np.float32(10000.0) ** (-np.arange(0, NROPE, 2, dtype=np.float32) / np.float32(NROPE))
    ang = (np.arange(seq, dtype=np.float32)[:, None] * inv[None, :]).astype(np.float32)
    cs = np.stack([np.cos(ang), np.sin(ang)], 0).reshape(2, nt, P, NROPE // 2).transpose(2, 0, 1, 3)
    dist = p[:, None] + (seq - P) - np.arange(seq)[None, :]
    mult = sum(((dist >= 0) & (dist <= w) & (dist % dl == 0)).astype(np.float64)
               for w, dl in ((128, 1), (512, 4), (2048, 16)))
    dilated = [np.where(mult > 0, np.log(np.maximum(mult, 1)) - sl * dist, NEG) for sl in slopes[HEADS:]]
    near = p[:, None] + P - np.arange(2 * P)[None, :]
    window = [np.where((near >= 0) & (near < P), -sl * near, NEG) for sl in slopes[:HEADS]]
    f = np.float32
    return {
        "ident": np.eye(P, dtype=f), "ones": np.ones((P, P), f),
        "upto": (p[:, None] <= p[None, :]).astype(f), "before": (p[:, None] < p[None, :]).astype(f),
        "cos_sin": np.ascontiguousarray(cs).astype(f),
        "iota": np.tile(np.arange(experts_n, dtype=f), (P, 1)),
        "tokid": (p[:, None] + P * np.arange(nt)[None, :]).astype(np.int32),
        "causal": np.where(dist >= 0, 0.0, NEG).astype(f),
        "dilated": np.stack(dilated).astype(f), "window": np.stack(window).astype(f),
    }


_INS = ("x", "norm1_g", "w_in", "mla_gcq", "mla_gckv", "mla_wuq", "mla_wukv", "qk_gq", "qk_gk", "fox_bf", "sink",
        "w_o", "norm2_g", "w_rg", "b_rg", "w_re", "b_re", "w1", "w3", "w2")


def kernel(**inputs):
    import numpy as np
    import concourse.bacc as bacc
    from concourse.bass_utils import run_bass_kernel_spmd

    nc = bacc.Bacc("TRN2", target_bir_lowering=False, num_devices=1)
    arrays, ins, consts = {}, {}, {}
    for name in _INS:
        a = np.ascontiguousarray(inputs[name])
        arrays["in_" + name] = a
        ins[name] = nc.dram_tensor("in_" + name, a.shape, F32, kind="ExternalInput").ap()
    seq, d = inputs["x"].shape[1:]
    n_exp = inputs["w1"].shape[1]
    for name, a in tables(seq, n_exp).items():
        arrays["table_" + name] = a
        consts[name] = nc.dram_tensor("table_" + name, a.shape, mybir.dt.from_np(a.dtype), kind="ExternalInput").ap()
    scratch = {
        "xn": nc.dram_tensor("normed", (seq, d), F32, kind="Internal").ap(),
        "y": nc.dram_tensor("expert_rows", (n_exp * P, d), F32, kind="Internal").ap(),
        "table": nc.dram_tensor("slot_tokens", (seq * n_exp, 1), I32, kind="Internal").ap(),
    }
    out = nc.dram_tensor("out", inputs["x"].shape, F32, kind="ExternalOutput").ap()
    trunk(nc, ins, consts, scratch, out)
    return run_bass_kernel_spmd(nc, [arrays], core_ids=[0]).results[0]["out"]
```

```python
from contextlib import ExitStack

import concourse.bass as bass
from concourse import mybir

ALU = mybir.AluOpType
ACT = mybir.ActivationFunctionType
AX = mybir.AxisListType
F32 = mybir.dt.float32
I32 = mybir.dt.int32
U32 = mybir.dt.uint32

P = 128
EPS = 1e-6
NEG = -1e30
HD = 64
HEADS = 4
MIXERS = 4
NQR, NKV, NROPE, NNOPE = 192, 128, 32, 32
GW = HEADS * HD
CHUNKS = (352, 384, 384, 384, 388, 512)
AUG = HD + 2
BIG = 1e30


class Signal:

    def __init__(self, sem, per_pass):
        self.sem, self.per_pass = sem, per_pass

    def at(self, done, k):
        return done * self.per_pass + k


def trunk(nc, ins, consts, scratch, out):
    x_in = ins["x"]
    _, SEQ, D = x_in.shape
    L = ins["w_in"].shape[0]
    NT = SEQ // P
    KT = D // P
    E = ins["w1"].shape[1]
    F = ins["w1"].shape[3]
    NG = ins["w_rg"].shape[2]
    PER = E // NG
    R = NG + E
    ROUNDS = SEQ // P
    W1D = sum(CHUNKS)
    coff = [sum(CHUNKS[:c]) for c in range(len(CHUNKS))]
    widths = (3 * GW, 3 * GW, 3 * GW, 2 * GW)
    pbase = [NT * sum(widths[:m]) for m in range(MIXERS)]

    out_f = out.rearrange("b s d -> (b s) d")
    x_f = x_in.rearrange("b s d -> (b s) d")
    xn_dram, y_dram, table = scratch["xn"], scratch["y"], scratch["table"]

    ctx = ExitStack()
    with ctx:
        def sb(name, shape, dt=F32):
            return ctx.enter_context(nc.sbuf_tensor(name, shape, dt))

        def counted(name, per_pass):
            return Signal(ctx.enter_context(nc.semaphore(name)), per_pass)

        r_proj = sb("r_proj", [P, NT * sum(widths)])
        r_win = sb("r_win", [P, KT * W1D])
        r_tile = sb("r_tile", [P, 8 * SEQ])
        bank_pairs = [ctx.enter_context(nc.psum_tensor(f"banks{b}", [P, 1024], F32)) for b in range(4)]
        banks = [bank_pairs[b // 2][:, 512 * (b % 2):512 * (b % 2) + 512] for b in range(8)]

        ident = sb("ident", [P, P])
        ones = sb("ones", [P, P])
        w_lat = sb("w_lat", [P, 1024])
        upto = sb("upto", [P, P])
        before = sb("before", [P, P])
        cos_sin = sb("cos_sin", [P, 2, NT, NROPE // 2])
        iota = sb("iota", [P, E])
        tokid = sb("tokid", [P, NT], I32)
        eps = sb("eps", [P, 1])
        gain1 = sb("gain1", [P, KT])
        gain2 = sb("gain2", [P, KT])
        gain_lat = sb("gain_lat", [P, 3])
        gain_a = sb("gain_a", [P, 2 * HEADS, HD])
        gain_raw = sb("gain_raw", [P, 2 * MIXERS])
        gain_qk = sb("gain_qk", [P, 2 * MIXERS])
        sink_b = sb("sink_b", [P, HEADS])
        fox_b = sb("fox_b", [P, HEADS])
        route_b = sb("route_b", [P, R])
        rx = sb("rx", [P, 2, 3])
        rl = sb("rl", [P, 2, 3, 2])
        ssq = sb("ssq", [P, NT, 30])
        rs = sb("rs", [P, NT, 30])
        fg = sb("fg", [P, NT, HEADS])
        fox = sb("fox", [P, 4, NT, HEADS])
        cum = sb("cum", [P, 2, NT, HEADS])
        rowmax = sb("rowmax", [P, 2])
        never = sb("never", [P, 1])
        gates = sb("gates", [P, NT, 2])
        base_row = sb("base_row", [P, NT, 2])
        rel = sb("rel", [P, NT, 2])
        nrounds = sb("nrounds", [1, 1], I32)
        junk = sb("junk", [P, 4])

        start_loads = counted("start_loads", 0)
        start_sets = counted("start_sets", 0)
        zeros_i = r_tile[:, 0:256].bitcast(I32)

        with nc.Block() as block:
            @block.sync
            def _(sp):
                n = 0
                for dst, src in ((ident[:, :], consts["ident"]), (ones[:, :], consts["ones"]),
                                 (upto[:, :], consts["upto"]), (before[:, :], consts["before"]),
                                 (cos_sin[:, :, :, :], consts["cos_sin"]), (iota[:, :], consts["iota"]),
                                 (tokid[:, :], consts["tokid"]), (out_f, x_f)):
                    sp.dma_start(dst, src).then_inc(start_loads.sem, 16)
                    n += 16
                sp.wait_ge(start_sets.sem, 1)
                sp.dma_start(table.rearrange("(p c) o -> p (c o)", p=P), zeros_i).then_inc(start_loads.sem, 16)
                sp.wait_ge(start_loads.sem, n + 16)

            @block.vector
            def _(dve):
                nc.vector.memset(zeros_i, 0).then_inc(start_sets.sem, 1)
                nc.vector.memset(eps[:, :], EPS)
                nc.vector.memset(never[:, :], NEG)
                nc.vector.memset(gain_raw[:, :], 1.0)
                nc.vector.memset(gain_qk[:, :], 1.0)
                nc.vector.memset(gain_lat[:, :], 1.0)
                nc.vector.memset(junk[:, :], 0.0)

        s = Shared()
        s.D = D
        s.E = E
        s.F = F
        s.KT = KT
        s.NG = NG
        s.NT = NT
        s.PER = PER
        s.R = R
        s.SEQ = SEQ
        s.bank_pairs = bank_pairs
        s.banks = banks
        s.base_row = base_row
        s.before = before
        s.coff = coff
        s.consts = consts
        s.cos_sin = cos_sin
        s.counted = counted
        s.cum = cum
        s.eps = eps
        s.fg = fg
        s.fox = fox
        s.fox_b = fox_b
        s.gain1 = gain1
        s.gain2 = gain2
        s.gain_a = gain_a
        s.gain_lat = gain_lat
        s.gain_qk = gain_qk
        s.gain_raw = gain_raw
        s.gates = gates
        s.ident = ident
        s.ins = ins
        s.iota = iota
        s.junk = junk
        s.never = never
        s.nrounds = nrounds
        s.ones = ones
        s.out_f = out_f
        s.pbase = pbase
        s.r_proj = r_proj
        s.r_tile = r_tile
        s.r_win = r_win
        s.rel = rel
        s.rl = rl
        s.route_b = route_b
        s.rowmax = rowmax
        s.rs = rs
        s.rx = rx
        s.sink_b = sink_b
        s.ssq = ssq
        s.start_sets = start_sets
        s.table = table
        s.tokid = tokid
        s.upto = upto
        s.w_lat = w_lat
        s.widths = widths
        s.xn_dram = xn_dram
        s.y_dram = y_dram
        project_sems = project_signals(s)
        attend_sems = attend_signals(s)
        out_sems = out_signals(s)
        route_sems = route_signals(s)
        expert_sems = expert_signals(s)

        rounds_done = {}
        for eng in (nc.sync, nc.scalar, nc.vector, nc.gpsimd, nc.tensor):
            rounds_done[eng.engine] = eng.alloc_register("rounds_done")
            eng.reg_mov(rounds_done[eng.engine], 0)
        s.rounds_done = rounds_done
        s.attend_sems = attend_sems
        s.wait_value = {e.engine: e.alloc_register("wait_value") for e in (nc.sync, nc.scalar, nc.vector, nc.gpsimd, nc.tensor)}

        with nc.Fori(0, L) as layer:
            project(nc, s, project_sems, layer)
            attend(nc, s, attend_sems, layer)
            out_route(nc, s, out_sems, layer)
            route(nc, s, route_sems, layer)
            rounds = nc.values_load(nrounds[0:1, 0:1], min_val=1, max_val=ROUNDS)
            with nc.Fori(0, rounds) as rnd:
                experts(nc, s, expert_sems, layer, rnd)



class Shared:
    pass


def bcast(ap, shape):
    return ap.to_broadcast(shape)


def project_signals(s):
    sig = s.counted
    NT = s.NT
    g = Shared()
    g.w_in = [sig(f"w_in_loaded{c}", 16) for c in range(len(CHUNKS))]
    g.small = sig("layer_tables_loaded", 0)
    g.x = [sig(f"x_loaded{j}", 16 * NT // 2) for j in range(2)]
    g.x_sq = sig("x_squares_summed", NT)
    g.x_rt = sig("x_root_taken", NT)
    g.x_r = sig("x_scale_ready", NT)
    g.xT = sig("x_transposed", NT)
    g.uT = sig("uT_ready", 2 * NT)
    g.mm = sig("projected", 6 * NT)
    g.mo = sig("projection_out", 7 * NT + 3)
    g.l_sq = sig("latent_squares_summed", 2 * NT)
    g.l_rt = sig("latent_root_taken", NT)
    g.l_r = sig("latent_scale_ready", NT)
    g.lT = sig("latent_transposed", NT)
    g.lo = sig("latentT_ready", 3 * NT)
    g.am = sig("latents_expanded", NT)
    g.ao = sig("mixer_a_out", 4 * NT + 1)
    g.rope = sig("rope_steps", 7 * NT)
    g.sq = sig("head_squares_ready", 4 * NT)
    g.red = sig("head_squares_summed", NT + 1)
    g.wl = sig("expand_weights_loaded", 0)
    g.gq = sig("gain_tables_ready", 1)
    return g


def project(nc, s, g, layer):
    P_, NT, KT = P, s.NT, s.KT
    D = s.D
    x_t = [s.r_tile[:, j * 1024:(j + 1) * 1024] for j in range(2)]
    uT = [s.r_tile[:, 2048 + j * 1024:2048 + (j + 1) * 1024].rearrange("p (k n) -> p k n", n=P) for j in range(2)]
    uT_flat = [s.r_tile[:, 2048 + j * 1024:2048 + (j + 1) * 1024] for j in range(2)]
    latT_flat = [s.r_tile[:, 4800 + j * 384:4800 + (j + 1) * 384] for j in range(2)]
    lat = [s.r_tile[:, 4096 + j * 352:4096 + (j + 1) * 352] for j in range(2)]
    latT = [s.r_tile[:, 4800 + j * 384:4800 + (j + 1) * 384].rearrange("p (k n) -> p k n", n=P) for j in range(2)]
    sqb = s.r_tile[:, 5568:5568 + 1920]
    rot = s.r_tile[:, 7488:7488 + 512].rearrange("p (a h c) -> p a h c", a=4, h=8)
    w_ch = [s.r_win[:, KT * s.coff[c]:KT * (s.coff[c] + CHUNKS[c])].rearrange("p (k n) -> p k n", k=KT)
            for c in range(6)]
    pm = [s.r_proj[:, s.pbase[m]:s.pbase[m] + NT * s.widths[m]].rearrange("p (t n) -> p t n", t=NT)
          for m in range(4)]
    s.pm = pm
    w_l = s.w_lat
    bk = s.banks
    ins = s.ins

    def blockfn(block):
        @block.sync
        def _(sp):
            for c in range(6):
                src = ins["w_in"][layer].rearrange("(p k) n -> p k n", k=KT)[:, :, s.coff[c]:s.coff[c] + CHUNKS[c]]
                sp.dma_start(w_ch[c], src).then_inc(g.w_in[c].sem, 16)
                if c == 0:
                    for j in range(2):
                        sp.dma_start(x_t[j], s.out_f[j * P:(j + 1) * P]).then_inc(g.x[j].sem, 16)
            with sp.Fori(0, NT // 2 - 1) as i:
                for j in range(2):
                    sp.wait_ge(g.uT.sem, g.uT.at(layer, 2 * (2 * i + j + 1)))
                    sp.dma_start(x_t[j], s.out_f[bass.ds((2 * i + 2 + j) * P, P)]).then_inc(g.x[j].sem, 16)

        @block.tensor
        def _(pe):
            def transpose_x(i, j):
                pe.wait_ge(g.x[j].sem, g.x[j].at(layer, 16 * (i + 1)))
                xs = x_t[j].rearrange("p (q k) -> p k q", k=KT)
                for k in range(KT):
                    mm = pe.transpose(bk[3 + k // 4][:, (k % 4) * P:(k % 4 + 1) * P], xs[:, k, :], s.ident[:, :])
                mm.then_inc(g.xT.sem, 1)

            def tile(i, j, last):
                t = 2 * i + j

                def chunk(c):
                    n = 6 * j + c
                    b = n % 3
                    pe.wait_ge(g.w_in[c].sem, g.w_in[c].at(layer, 16))
                    if c == 0:
                        pe.wait_ge(g.uT.sem, g.uT.at(layer, 2 * t + 2))
                    prev = n - 3
                    reads = 7 * (prev // 6) + (prev % 6 + 1) + (1 if prev % 6 >= 4 else 0)
                    if n > 0:
                        pe.wait_ge(g.mo.sem, g.mo.at(layer, 14 * i + reads + 3))
                    for k in range(KT):
                        mm = pe.matmul(bk[b][:, 0:CHUNKS[c]], uT[j][:, k, :], w_ch[c][:, k, :],
                                       start=(k == 0), stop=(k == KT - 1))
                    mm.then_inc(g.mm.sem, 1)

                chunk(0)
                chunk(1)
                if not last:
                    transpose_x(i + (j + 1) // 2, (j + 1) % 2)
                chunk(2)
                chunk(3)
                pe.wait_ge(g.mo.sem, g.mo.at(layer, 7 * t + 4))
                for n, (a, b) in enumerate(((0, 128), (128, 192), (192, 320))):
                    mm = pe.transpose(bk[5][0:b - a, n * P:(n + 1) * P], lat[j][:, a:b], s.ident[:, :])
                mm.then_inc(g.lT.sem, 1)
                chunk(4)
                chunk(5)
                pe.wait_ge(g.lo.sem, g.lo.at(layer, 3 * t + 3))
                pe.wait_ge(g.wl.sem, layer * 48 + 48)
                pe.wait_ge(g.ao.sem, g.ao.at(layer, 4 * t + 1))
                pe.matmul(bk[6][:, 0:GW], latT[j][:, 0, :], w_l[:, 0:GW], start=True, stop=False)
                pe.matmul(bk[6][:, 0:GW], latT[j][0:64, 1, :], w_l[0:64, GW:2 * GW], start=False, stop=True)
                pe.matmul(bk[7][:, 0:384], latT[j][:, 2, :], w_l[:, 2 * GW:2 * GW + 384],
                          start=True, stop=True).then_inc(g.am.sem, 1)

            transpose_x(0, 0)
            with pe.Fori(0, NT // 2 - 1) as i:
                tile(i, 0, False)
                tile(i, 1, False)
            tile(NT // 2 - 1, 0, False)
            tile(NT // 2 - 1, 1, True)

        @block.scalar
        def _(act):
            act.dma_start(w_l[:, 0:GW], ins["mla_wuq"][layer][0:128]).then_inc(g.wl.sem, 16)
            act.dma_start(w_l[0:64, GW:2 * GW], ins["mla_wuq"][layer][128:192]).then_inc(g.wl.sem, 16)
            act.dma_start(w_l[:, 2 * GW:2 * GW + 384], ins["mla_wukv"][layer]).then_inc(g.wl.sem, 16)
            tabs = []
            for gain, name in ((s.gain1, "norm1_g"), (s.gain2, "norm2_g")):
                tabs.append((gain[:, :], ins[name][layer].rearrange("(p k) -> p k", k=KT)))
            gq, gk = ins["qk_gq"][layer], ins["qk_gk"][layer]
            cq, ck = ins["mla_gcq"][layer], ins["mla_gckv"][layer]
            tabs.append((s.gain_lat[:, 0:1], cq[0:128].rearrange("(p o) -> p o", o=1)))
            tabs.append((s.gain_lat[0:64, 1:2], cq[128:192].rearrange("(p o) -> p o", o=1)))
            tabs.append((s.gain_lat[:, 2:3], ck.rearrange("(p o) -> p o", o=1)))
            for h in range(HEADS):
                tabs.append((s.gain_a[:, h, :], gq[0].partition_broadcast(P)))
                tabs.append((s.gain_a[:, HEADS + h, :], gk[0].partition_broadcast(P)))
            for m in range(1, MIXERS):
                tabs.append((s.gain_raw[0:HD, m:m + 1], gq[m].rearrange("(p o) -> p o", o=1)))
                tabs.append((s.gain_raw[0:HD, MIXERS + m:MIXERS + m + 1], gk[m].rearrange("(p o) -> p o", o=1)))
            for dst, name in ((s.sink_b[:, :], "sink"), (s.fox_b[:, :], "fox_bf"), (s.route_b[:, 0:s.NG], "b_rg"),
                              (s.route_b[:, s.NG:s.R], "b_re")):
                tabs.append((dst, ins[name][layer].partition_broadcast(P)))
            for dst, src in tabs:
                act.dma_start(dst, src).then_inc(g.small.sem, 16)
            g.small.per_pass = 16 * len(tabs)
            act.wait_ge(g.small.sem, g.small.at(layer, 16 * len(tabs)))

            def square_x(i, j):
                t = 2 * i + j
                act.wait_ge(g.x[j].sem, g.x[j].at(layer, 16 * (i + 1)))
                nc.scalar.activation(uT_flat[j], x_t[j], ACT.Square, scale=D ** -0.5,
                                     accum_out=s.rx[:, j, 0:1]).then_inc(g.x_sq.sem, 1)
                act.wait_ge(g.x_sq.sem, g.x_sq.at(layer, t + 1))
                nc.scalar.activation(s.rx[:, j, 1:2], s.rx[:, j, 0:1], ACT.Sqrt,
                                     bias=s.eps[:, 0:1]).then_inc(g.x_rt.sem, 1)

            def tile(i, j, last):
                t = 2 * i + j

                def evac(c):
                    n = 6 * j + c
                    b = n % 3
                    act.wait_ge(g.mm.sem, g.mm.at(layer, 6 * t + c + 1))
                    if c == 0:
                        act.wait_ge(g.x_r.sem, g.x_r.at(layer, t + 1))
                        dst = lat[j]
                    elif c < 3:
                        dst = pm[1][:, t, (c - 1) * 384:c * 384]
                    elif c < 5:
                        dst = pm[2][:, t, (c - 3) * 384:(c - 2) * 384]
                    else:
                        dst = pm[3][:, t, :]
                    if c == 4:
                        nc.scalar.activation(s.fg[:, t, :], bk[b][:, 384:388], ACT.Copy,
                                             scale=s.rx[:, j, 2:3]).then_inc(g.mo.sem, 1)
                    nc.scalar.activation(dst, bk[b][:, 0:(384 if c == 4 else CHUNKS[c])], ACT.Copy,
                                         scale=s.rx[:, j, 2:3]).then_inc(g.mo.sem, 1)

                evac(0)
                act.wait_ge(g.mo.sem, g.mo.at(layer, 7 * t + 4))
                nc.scalar.activation(latT_flat[j][:, 0:192], lat[j][:, 0:192], ACT.Square, scale=192 ** -0.5,
                                     accum_out=s.rl[:, j, 0, 0:1]).then_inc(g.l_sq.sem, 1)
                nc.scalar.activation(latT_flat[j][:, 192:320], lat[j][:, 192:320], ACT.Square, scale=128 ** -0.5,
                                     accum_out=s.rl[:, j, 0, 1:2]).then_inc(g.l_sq.sem, 1)
                act.wait_ge(g.l_sq.sem, g.l_sq.at(layer, 2 * t + 2))
                nc.scalar.activation(s.rl[:, j, 1, :], s.rl[:, j, 0, :], ACT.Sqrt,
                                     bias=s.eps[:, 0:1]).then_inc(g.l_rt.sem, 1)
                evac(1)
                if not last:
                    square_x(i + (j + 1) // 2, (j + 1) % 2)
                evac(2)
                evac(3)
                act.wait_ge(g.lT.sem, g.lT.at(layer, t + 1))
                for n in range(3):
                    q = 64 if n == 1 else P
                    nc.scalar.activation(latT[j][0:q, n, :], bk[5][0:q, n * P:(n + 1) * P], ACT.Copy,
                                         scale=s.gain_lat[0:q, n:n + 1]).then_inc(g.lo.sem, 1)
                evac(4)
                evac(5)

            nc.scalar.activation(s.junk[:, 1:2], s.eps[:, 0:1], ACT.Copy).then_inc(g.mo.sem, 3)
            square_x(0, 0)
            with act.Fori(0, NT // 2 - 1) as i:
                tile(i, 0, False)
                tile(i, 1, False)
            tile(NT // 2 - 1, 0, False)
            tile(NT // 2 - 1, 1, True)

        @block.vector
        def _(dve):
            dve.wait_ge(g.small.sem, g.small.at(layer, g.small.per_pass))
            nc.vector.tensor_scalar(s.gain_qk[0:HD, 0:MIXERS], s.gain_raw[0:HD, 0:MIXERS], HD ** -0.5, None,
                                    ALU.mult)
            nc.vector.tensor_copy(s.gain_qk[0:HD, MIXERS:2 * MIXERS],
                                  s.gain_raw[0:HD, MIXERS:2 * MIXERS]).then_inc(g.gq.sem, 1)
            nc.vector.memset(s.junk[:, 0:1], 0.0).then_inc(g.red.sem, 1)
            nc.vector.memset(s.junk[:, 2:3], 0.0).then_inc(g.ao.sem, 1)

            def evac_x(i, j):
                t = 2 * i + j
                dve.wait_ge(g.x_rt.sem, g.x_rt.at(layer, t + 1))
                nc.vector.reciprocal(s.rx[:, j, 2:3], s.rx[:, j, 1:2]).then_inc(g.x_r.sem, 1)
                dve.wait_ge(g.xT.sem, g.xT.at(layer, t + 1))
                for half in range(2):
                    nc.vector.tensor_tensor(
                        uT[j][:, 4 * half:4 * half + 4, :], bk[3 + half][:, :].rearrange("p (k n) -> p k n", k=4),
                        bcast(s.gain1[:, 4 * half:4 * half + 4].unsqueeze(2), [P, 4, P]),
                        ALU.mult).then_inc(g.uT.sem, 1)

            def tile(i, j, last):
                t = 2 * i + j
                if not last:
                    evac_x(i + (j + 1) // 2, (j + 1) % 2)
                dve.wait_ge(g.l_rt.sem, g.l_rt.at(layer, t + 1))
                nc.vector.reciprocal(s.rl[:, j, 2, :], s.rl[:, j, 1, :]).then_inc(g.l_r.sem, 1)
                pa = pm[0][:, t, :]
                kva = bk[7][:, 0:384].rearrange("p (h c) -> p h c", h=HEADS)
                ka = pa[:, GW:2 * GW].rearrange("p (h c) -> p h c", h=HEADS)
                dve.wait_ge(g.am.sem, g.am.at(layer, t + 1))
                dve.wait_ge(g.l_r.sem, g.l_r.at(layer, t + 1))
                nc.vector.tensor_scalar(pa[:, 0:GW], bk[6][:, 0:GW], s.rl[:, j, 2, 0:1], None,
                                        ALU.mult).then_inc(g.ao.sem, 1)
                nc.vector.tensor_scalar(ka[:, :, 0:NNOPE], kva[:, :, 0:NNOPE], s.rl[:, j, 2, 1:2], None,
                                        ALU.mult).then_inc(g.ao.sem, 1)
                nc.vector.tensor_scalar(pa[:, 2 * GW:3 * GW].rearrange("p (h c) -> p h c", h=HEADS),
                                        kva[:, :, NNOPE:NNOPE + HD], s.rl[:, j, 2, 1:2], None,
                                        ALU.mult).then_inc(g.ao.sem, 1)
                nc.vector.tensor_tensor(ka[:, :, NNOPE:HD],
                                        bcast(lat[j][:, 320:352].unsqueeze(1), [P, HEADS, NROPE]),
                                        bcast(s.ones[:, 0:NROPE].unsqueeze(1), [P, HEADS, NROPE]),
                                        ALU.mult).then_inc(g.ao.sem, 1)
                dve.wait_ge(g.sq.sem, g.sq.at(layer, 4 * t + 4))
                nc.vector.tensor_reduce(s.ssq[:, t, :], sqb.rearrange("p (h c) -> p h c", c=HD), AX.X,
                                        ALU.add).then_inc(g.red.sem, 1)

            evac_x(0, 0)
            with dve.Fori(0, NT // 2 - 1) as i:
                tile(i, 0, False)
                tile(i, 1, False)
            tile(NT // 2 - 1, 0, False)
            tile(NT // 2 - 1, 1, True)

        @block.gpsimd
        def _(pool):
            wait_alone(pool, s, g.small.sem, g.small.at(layer, g.small.per_pass))

            def tile(i, j):
                t = 2 * i + j
                wait_alone(pool, s, g.red.sem, g.red.at(layer, t + 1))
                wait_alone(pool, s, g.ao.sem, g.ao.at(layer, 4 * t + 5))
                qk = pm[0][:, t, 0:2 * GW]
                nc.gpsimd.tensor_tensor(sqb[:, 0:512], qk, qk, ALU.mult).then_inc(g.sq.sem, 1)
                wait_alone(pool, s, g.sq.sem, g.sq.at(layer, 4 * t + 1))
                nc.gpsimd.tensor_tensor(qk, qk, s.gain_a[:, :, :].rearrange("p h c -> p (h c)"),
                                        ALU.mult).then_inc(g.rope.sem, 1)
                hv = qk.rearrange("p (h c) -> p h c", c=HD)
                x1, x2 = hv[:, :, 32:48], hv[:, :, 48:64]
                co = bcast(s.cos_sin[:, 0, t, :].unsqueeze(1), [P, 8, 16])
                si = bcast(s.cos_sin[:, 1, t, :].unsqueeze(1), [P, 8, 16])
                wait_alone(pool, s, g.rope.sem, g.rope.at(layer, 7 * t + 1))
                for a, (u, v) in enumerate(((x1, co), (x2, si), (x2, co), (x1, si))):
                    nc.gpsimd.tensor_tensor(rot[:, a], u, v, ALU.mult).then_inc(g.rope.sem, 1)
                wait_alone(pool, s, g.rope.sem, g.rope.at(layer, 7 * t + 5))
                nc.gpsimd.tensor_tensor(x1, rot[:, 0], rot[:, 1], ALU.subtract).then_inc(g.rope.sem, 1)
                nc.gpsimd.tensor_tensor(x2, rot[:, 2], rot[:, 3], ALU.add).then_inc(g.rope.sem, 1)
                for m, reads in ((1, 3), (2, 6), (3, 7)):
                    w = 512 if m < 3 else 384
                    wait_alone(pool, s, g.mo.sem, g.mo.at(layer, 7 * t + reads + 3))
                    pq = pm[m][:, t, 0:w]
                    nc.gpsimd.tensor_tensor(sqb[:, 512 * m:512 * m + w], pq, pq, ALU.mult).then_inc(g.sq.sem, 1)

            with pool.Fori(0, NT // 2) as i:
                tile(i, 0)
                tile(i, 1)

    with nc.Block() as block:
        blockfn(block)


PAIRS = MIXERS * HEADS // 2
AHEAD, AHEAD_WINDOW = 2, 3
RING = 3


def key_span(m, qb):
    k0 = max(0, qb - 1) * P if m == 3 else 0
    return k0, (qb + 1) * P - k0


def head_at(pair, k, nt):
    return (k + (k >= nt) + pair) % 2


class Step:

    def __init__(self, i, nt):
        self.i = i
        self.pair, k = i // (2 * nt), i % (2 * nt)
        self.k = k
        self.m = self.pair // 2
        self.j = head_at(self.pair, k, nt)
        self.qb = k // 2 if (k % 2 == 0) == (k < nt) else nt - 1 - k // 2
        self.head = 2 * (self.pair % 2) + self.j
        self.slot = self.head
        self.k0, self.nk = key_span(self.m, self.qb)
        self.window = self.m == 3
        if self.window:
            self.bank, self.at = i % 3, 256 * (i % 12)
        elif k % 2:
            self.bank, self.at = 0, 1024 * (i // 2 % 2)
        else:
            self.bank, self.at = 2, 2048 + 512 * (i // 2 % 2)
        self.blocks = [(c, min(512, self.nk - c)) for c in range(0, self.nk, 512)]


def plan_steps(nt):
    steps = [Step(i, nt) for i in range(2 * nt * PAIRS)]
    issued, upto = [], 0
    for st in steps:
        ahead = AHEAD_WINDOW if st.window else AHEAD
        end = min(len(steps), st.i + ahead + 1)
        issued.append(list(range(upto, end)))
        upto = max(upto, end)
    return steps, issued


def qk_group(st):
    return st.k - 4 if st.pair + 1 < PAIRS and 4 <= st.k < 12 else None


def mix_half(st):
    return st.k - 2 if st.pair > 0 and st.k in (2, 3) else None


def plan_ring(steps):
    ring = [("qk", (0, q)) for q in range(8)]
    for st in steps:
        if mix_half(st) is not None:
            ring.append(("mix", (st.pair - 1, mix_half(st))))
        if qk_group(st) is not None:
            ring.append(("qk", (st.pair + 1, qk_group(st))))
        ring += [("w2" if c else "w", st.i) for c, _ in st.blocks]
    ring += [("mix", (PAIRS - 1, half)) for half in range(2)]
    return ring


def attend_signals(s):
    sig = s.counted
    NT = s.NT
    steps, _ = plan_steps(NT)
    n = len(steps)
    groups = sum(len(st.blocks) for st in steps)
    g = Shared()
    g.rt = sig("head_roots_taken", 1)
    g.rsr = sig("head_scales_ready", 1)
    g.fxd = sig("fox_vector_steps", 3)
    g.fxa = sig("fox_scalar_steps", 3)
    g.fxp = sig("fox_summed", 1)
    g.fxo = sig("fox_cumulated", 2)
    g.causal = sig("causal_table_loaded", 16)
    g.bias = [sig(f"bias_table_loaded{j}", 16 * 4) for j in range(2)]
    g.wo = sig("w_o_loaded", 16)
    g.stage = sig("heads_scaled", 2 * HEADS * MIXERS + 2 * HEADS)
    g.qkt = sig("qk_transposed", 8 * PAIRS)
    g.qko = sig("qkT_ready", 8 * PAIRS)
    g.lg = sig("logits_done", n)
    g.mx = sig("logits_biased", n)
    g.ng = sig("negmax_ready", n)
    g.ex = sig("weights_ready", n)
    g.pt = sig("weights_transposed", groups)
    g.po = sig("weightsT_ready", n)
    g.pd = sig("weightsT_second_ready", groups - n)
    g.pv = sig("values_summed", n)
    g.sk = sig("sink_terms_ready", HEADS)
    g.dn = sig("denominators_ready", HEADS * (MIXERS + 1))
    g.on = sig("heads_normalised", HEADS * MIXERS)
    g.ot = sig("mix_transposed", 2 * PAIRS)
    g.oo = sig("mixT_ready", 2 * PAIRS)
    return g


def attend(nc, s, g, layer):
    NT, SEQ = s.NT, s.SEQ
    bk, pm = s.banks, s.pm
    w = s.r_win
    steps, issued = plan_steps(NT)
    ring = plan_ring(steps)
    ring_at = {name: n for n, name in enumerate(ring)}
    kinds = [kind for kind, _ in ring]

    def cut(at, n, count):
        return [w[:, at + j * n:at + (j + 1) * n] for j in range(count)]

    qs = [a.rearrange("p (t c) -> p t c", c=AUG) for a in cut(0, 528, 2)]
    ks = [a.rearrange("p (t c) -> p t c", c=AUG) for a in cut(1056, 528, 2)]
    qT, kT = cut(2112, 1024, 4), cut(6208, 1024, 4)
    weights = w[:, 10304:13376]
    pT = cut(13376, 1024, 2)
    bias = cut(15424, 1024, 2)
    o_s = w[:, 17472:18496].rearrange("p (t c) -> p t c", c=P)
    negmax, den, sinkexp, rden = (
        w[:, 18496 + 32 * n:18528 + 32 * n].rearrange("p (a b) -> p a b", a=HEADS) for n in range(4))
    causal = s.w_lat[:, 0:SEQ]
    mixT = s.r_tile[:, :].rearrange("p (k n) -> p k n", k=8)
    s.w_o = s.r_proj[:, 0:8192].rearrange("p (k n) -> p k n", k=8)
    neg_cum, pos_cum = s.cum[:, 1], s.cum[:, 0]

    def stages_done(pair, j):
        n = 2 * pair + j + 1
        return 2 * n + 2 * min(max(n - 2 * HEADS, 0), HEADS)

    def table(st):
        if st.window:
            return bias[st.j][:, 2 * P - st.nk:2 * P]
        return (bias[st.j] if st.m == 1 else causal)[:, SEQ - st.nk:SEQ]

    def last_group(st):
        return sum(len(x.blocks) for x in steps[:st.i + 1])

    def seconds(st):
        return last_group(st) - st.i - 1

    def ring_bank(name):
        return 3 + ring_at[name] % RING

    with nc.Block() as block:
        @block.sync
        def _(sp):
            sp.dma_start(causal, s.consts["causal"]).then_inc(g.causal.sem, 16)
            for m in (1, 3):
                if m == 3:
                    sp.wait_ge(g.on.sem, g.on.at(layer, 2 * HEADS))
                    sp.dma_start(s.w_o, s.ins["w_o"][layer].rearrange("(k p) n -> p k n", p=P)).then_inc(g.wo.sem, 16)
                for h in range(HEADS):
                    if h >= 2 or m == 3:
                        pair = 2 * m + h // 2
                        sp.wait_ge(g.mx.sem, g.mx.at(layer, 2 * NT * pair))
                    src, n = (s.consts["dilated"][h], SEQ) if m == 1 else (s.consts["window"][h], 2 * P)
                    sp.dma_start(bias[h % 2][:, 0:n], src).then_inc(g.bias[h % 2].sem, 16)

        @block.tensor
        def _(pe):
            def bank_for(name):
                n = ring_at[name]
                if n >= RING:
                    kind = kinds[n - RING]
                    sem = {"qk": g.qko, "w": g.po, "w2": g.pd, "mix": g.oo}[kind]
                    wait_alone(pe, s, sem.sem, sem.at(layer, kinds[:n - RING + 1].count(kind)))
                return bk[ring_bank(name)]

            def transpose_heads(pair, q):
                j, a, half = q // 4, q // 2 % 2, q % 2
                K = AUG if pair // 2 == 2 else HD
                wait_alone(pe, s, g.stage.sem, g.stage.at(layer, stages_done(pair, j)))
                bank = bank_for(("qk", (pair, q)))
                for t in range(4):
                    mm = pe.transpose(bank[0:K, t * P:(t + 1) * P], (qs, ks)[a][j][:, 4 * half + t, 0:K],
                                      s.ident[:, :])
                mm.then_inc(g.qkt.sem, 1)

            def transpose_mix(pair, half):
                pe.wait_ge(g.on.sem, g.on.at(layer, 2 * pair + 2))
                bank = bank_for(("mix", (pair, half)))
                for t in range(4):
                    mm = pe.transpose(bank[:, t * P:(t + 1) * P], o_s[:, 4 * half + t, :], s.ident[:, :])
                mm.then_inc(g.ot.sem, 1)

            def logits(st):
                K = AUG if st.m == 2 else HD
                pe.wait_ge(g.qko.sem, g.qko.at(layer, 8 * st.pair + 4 * st.j + 4))
                used = {st.bank + c // 512 for c, _ in st.blocks}
                before = [x.i for x in steps[:st.i] if used & {x.bank + c // 512 for c, _ in x.blocks}]
                if before:
                    pe.wait_ge(g.mx.sem, g.mx.at(layer, before[-1] + 1))
                q = 2 * (st.pair % 2) + st.j
                for c, cw in st.blocks:
                    mm = pe.matmul(bk[st.bank + c // 512][:, 0:cw], qT[q][0:K, st.qb * P:(st.qb + 1) * P],
                                   kT[q][0:K, st.k0 + c:st.k0 + c + cw], start=True, stop=True)
                mm.then_inc(g.lg.sem, 1)

            def transpose_weights(st):
                pe.wait_ge(g.ex.sem, g.ex.at(layer, st.i + 1))
                for c, cw in st.blocks:
                    bank = bank_for(("w2" if c else "w", st.i))
                    for b in range(0, cw, P):
                        at = st.at + c + b
                        mm = pe.transpose(bank[:, b:b + P], weights[:, at:at + P], s.ident[:, :])
                    mm.then_inc(g.pt.sem, 1)

            def values(st):
                pe.wait_ge(g.po.sem, g.po.at(layer, st.i + 1))
                if st.pair > 0 and st.k < 2:
                    pe.wait_ge(g.on.sem, g.on.at(layer, 2 * st.pair - 1 + st.k))
                v0 = 384 + HD * (st.head // 2) if st.window else 2 * GW + HD * st.head
                for b in range(0, st.nk, P):
                    if b == 512:
                        pe.wait_ge(g.pd.sem, g.pd.at(layer, seconds(st)))
                    mm = pe.matmul(bk[6 + st.j][:, st.qb * HD:(st.qb + 1) * HD], pT[st.i % 2][:, b:b + P],
                                   pm[st.m][:, (st.k0 + b) // P, v0:v0 + HD], start=(b == 0),
                                   stop=(b == st.nk - P))
                mm.then_inc(g.pv.sem, 1)

            for q in range(8):
                transpose_heads(0, q)
            pe.wait_ge(g.fxd.sem, g.fxd.at(layer, 3))
            ls = s.fox[:, 3]
            pe.matmul(bk[6][:, 0:NT * HEADS], s.upto[:, :], ls.rearrange("p t h -> p (t h)"),
                      start=True, stop=False)
            for t in range(NT - 1):
                left = NT - 1 - t
                mm = pe.matmul(bk[6][:, (t + 1) * HEADS:NT * HEADS], s.ones[:, :],
                               bcast(ls[:, t:t + 1, :], [P, left, HEADS]),
                               start=False, stop=(t == NT - 2))
            mm.then_inc(g.fxp.sem, 1)
            pe.wait_ge(g.fxo.sem, g.fxo.at(layer, 2))
            for st in steps:
                for i in issued[st.i]:
                    logits(steps[i])
                if mix_half(st) is not None:
                    transpose_mix(st.pair - 1, mix_half(st))
                if qk_group(st) is not None:
                    transpose_heads(st.pair + 1, qk_group(st))
                transpose_weights(st)
                if st.i > 0:
                    values(steps[st.i - 1])
            values(steps[-1])
            for half in range(2):
                transpose_mix(PAIRS - 1, half)

        @block.scalar
        def _(act):
            nc.scalar.activation(s.rs[:, :, :], s.ssq[:, :, :], ACT.Sqrt, scale=1.0 / HD,
                                 bias=s.eps[:, 0:1]).then_inc(g.rt.sem, 1)
            act.wait_ge(g.fxd.sem, g.fxd.at(layer, 1))
            nc.scalar.activation(s.fox[:, 1], s.fox[:, 0], ACT.Abs).then_inc(g.fxa.sem, 1)
            act.wait_ge(g.fxa.sem, g.fxa.at(layer, 1))
            nc.scalar.activation(s.fox[:, 1], s.fox[:, 1], ACT.Exp, scale=-1.0).then_inc(g.fxa.sem, 1)
            act.wait_ge(g.fxa.sem, g.fxa.at(layer, 2))
            nc.scalar.activation(s.fox[:, 2], s.fox[:, 1], ACT.Ln, bias=s.ones[:, 0:1]).then_inc(g.fxa.sem, 1)

            def exponentials(st):
                act.wait_ge(g.ng.sem, g.ng.at(layer, st.i + 1))
                x = weights[:, st.at:st.at + st.nk]
                nc.scalar.activation(x, x, ACT.Exp, bias=negmax[:, st.slot, st.qb:st.qb + 1],
                                     accum_out=den[:, st.slot, st.qb:st.qb + 1]).then_inc(g.ex.sem, 1)

            for i in issued[0]:
                exponentials(steps[i])
            for st in steps:
                n = st.blocks[0][1]
                act.wait_ge(g.pt.sem, g.pt.at(layer, last_group(st) - len(st.blocks) + 1))
                nc.scalar.activation(pT[st.i % 2][:, 0:n], bk[ring_bank(("w", st.i))][:, 0:n],
                                     ACT.Copy).then_inc(g.po.sem, 1)
                if st.i > 0:
                    for i in issued[st.i]:
                        exponentials(steps[i])
                if st.window and st.k >= 2 * NT - 2:
                    nc.scalar.activation(sinkexp[:, st.slot, :], negmax[:, st.slot, :], ACT.Exp,
                                         bias=s.sink_b[:, st.head:st.head + 1]).then_inc(g.sk.sem, 1)

        @block.vector
        def _(dve):
            for j in range(2):
                nc.vector.memset(qs[j][:, :, HD:HD + 1], 1.0)
                nc.vector.memset(ks[j][:, :, HD + 1:HD + 2], 1.0)
            nc.vector.tensor_tensor(s.fox[:, 0], s.fg[:, :, :], bcast(s.fox_b[:, :].unsqueeze(1), [P, NT, HEADS]),
                                    ALU.add).then_inc(g.fxd.sem, 1)
            def scale_head(pair, j):
                m, h = pair // 2, 2 * (pair % 2) + j
                kv = pair % 2 if m == 3 else h
                for dst, col, r in ((qs[j], HD * h, 8 * m + h), (ks[j], GW + HD * kv, 8 * m + HEADS + kv)):
                    nc.vector.tensor_tensor(dst[:, :, 0:HD], pm[m][:, :, col:col + HD],
                                            bcast(s.rs[:, :, r:r + 1], [P, NT, HD]),
                                            ALU.mult).then_inc(g.stage.sem, 1)
                if m == 2:
                    nc.vector.tensor_copy(ks[j][:, :, HD:HD + 1], neg_cum[:, :, h:h + 1]).then_inc(g.stage.sem, 1)
                    nc.vector.tensor_copy(qs[j][:, :, HD + 1:AUG], pos_cum[:, :, h:h + 1]).then_inc(
                        g.stage.sem, 1)

            def evac_heads(pair, q):
                j, a, half = q // 4, q // 2 % 2, q % 2
                m = pair // 2
                K = AUG if m == 2 else HD
                dve.wait_ge(g.qkt.sem, g.qkt.at(layer, 8 * pair + q + 1))
                nc.vector.tensor_scalar(
                    (qT, kT)[a][2 * (pair % 2) + j][0:K, 512 * half:512 * half + 512],
                    bk[ring_bank(("qk", (pair, q)))][0:K, :],
                    s.gain_qk[0:K, MIXERS * a + m:MIXERS * a + m + 1], None, ALU.mult).then_inc(g.qko.sem, 1)

            def bias_and_max(st):
                if st.k < 2 and st.m in (1, 3):
                    dve.wait_ge(g.bias[st.j].sem,
                                g.bias[st.j].at(layer, 16 * (st.pair % 2 + 1) + (32 if st.window else 0)))
                wait_alone(dve, s, g.lg.sem, g.lg.at(layer, st.i + 1))
                behind = [x.i for x in steps[:st.i] if x.at < st.at + st.nk and st.at < x.at + x.nk]
                ahead_of = [x for x in range(len(steps)) if st.i in issued[x]][0]
                if behind and behind[-1] >= ahead_of:
                    wait_alone(dve, s, g.pt.sem, g.pt.at(layer, last_group(steps[behind[-1]])))
                col = 512 * (st.bank % 2)
                banks = s.bank_pairs[st.bank // 2][:, col:col + st.nk]
                nc.vector.tensor_tensor_reduce(out=weights[:, st.at:st.at + st.nk], in0=banks, in1=table(st),
                                               scale=1.0, scalar=-3e38, op0=ALU.add, op1=ALU.max,
                                               accum_out=s.rowmax[:, st.i % 2:st.i % 2 + 1]).then_inc(g.mx.sem, 1)
                dve.wait_ge(g.mx.sem, g.mx.at(layer, st.i + 1))
                floor = s.sink_b[:, st.head:st.head + 1] if st.window else s.never[:, 0:1]
                nc.vector.tensor_scalar(negmax[:, st.slot, st.qb:st.qb + 1], s.rowmax[:, st.i % 2:st.i % 2 + 1],
                                        floor, -1.0, ALU.max, ALU.mult).then_inc(g.ng.sem, 1)

            def second_group(st):
                c, cw = st.blocks[1]
                dve.wait_ge(g.pt.sem, g.pt.at(layer, last_group(st)))
                nc.vector.tensor_copy(pT[st.i % 2][:, c:c + cw],
                                      bk[ring_bank(("w2", st.i))][:, 0:cw]).then_inc(g.pd.sem, 1)

            def normalise(pair, turn):
                j = head_at(pair, 2 * NT - 2 + turn, NT)
                m, h = pair // 2, 2 * (pair % 2) + j
                slot = h
                dve.wait_ge(g.pv.sem, g.pv.at(layer, 2 * NT * (pair + 1) - 1 + turn))
                if m == 3:
                    dve.wait_ge(g.sk.sem, g.sk.at(layer, 2 * (pair % 2) + turn + 1))
                    nc.vector.tensor_tensor(den[:, slot, :], den[:, slot, :], sinkexp[:, slot, :],
                                            ALU.add).then_inc(g.dn.sem, 1)
                    dve.wait_ge(g.dn.sem, g.dn.at(layer, dn_done(pair, turn) - 1))
                nc.vector.reciprocal(rden[:, slot, :], den[:, slot, :]).then_inc(g.dn.sem, 1)
                dve.wait_ge(g.dn.sem, g.dn.at(layer, dn_done(pair, turn)))
                nc.vector.tensor_tensor(o_s[:, :, HD * j:HD * (j + 1)],
                                        bk[6 + j][:, :].rearrange("p (t c) -> p t c", c=HD),
                                        bcast(rden[:, slot, :].unsqueeze(2), [P, NT, HD]),
                                        ALU.mult).then_inc(g.on.sem, 1)

            def evac_mix(pair, half):
                dve.wait_ge(g.ot.sem, g.ot.at(layer, 2 * pair + half + 1))
                nc.vector.tensor_copy(mixT[:, pair, 512 * half:512 * half + 512],
                                      bk[ring_bank(("mix", (pair, half)))]).then_inc(g.oo.sem, 1)

            dve.wait_ge(g.rt.sem, g.rt.at(layer, 1))
            nc.vector.reciprocal(s.rs[:, :, :], s.rs[:, :, :]).then_inc(g.rsr.sem, 1)
            dve.wait_ge(g.rsr.sem, g.rsr.at(layer, 1))
            scale_head(0, 0)
            scale_head(0, 1)
            for q in range(8):
                evac_heads(0, q)
            dve.wait_ge(g.fxa.sem, g.fxa.at(layer, 3))
            dve.wait_ge(g.fxd.sem, g.fxd.at(layer, 1))
            nc.vector.tensor_scalar(s.fox[:, 3], s.fox[:, 0], 0.0, None, ALU.min).then_inc(g.fxd.sem, 1)
            dve.wait_ge(g.fxd.sem, g.fxd.at(layer, 2))
            nc.vector.tensor_tensor(s.fox[:, 3], s.fox[:, 3], s.fox[:, 2], ALU.subtract).then_inc(g.fxd.sem, 1)
            dve.wait_ge(g.fxp.sem, g.fxp.at(layer, 1))
            flat = bk[6][:, 0:NT * HEADS].rearrange("p (t h) -> p t h", h=HEADS)
            nc.vector.tensor_copy(pos_cum, flat).then_inc(g.fxo.sem, 1)
            nc.vector.tensor_scalar(neg_cum, flat, -1.0, None, ALU.mult).then_inc(g.fxo.sem, 1)
            dve.wait_ge(g.causal.sem, g.causal.at(layer, 16))
            dve.wait_ge(g.fxo.sem, g.fxo.at(layer, 2))
            for st in steps:
                for i in issued[st.i]:
                    bias_and_max(steps[i])
                if st.pair + 1 < PAIRS and st.k in (2, 3):
                    scale_head(st.pair + 1, st.k - 2)
                if mix_half(st) is not None:
                    evac_mix(st.pair - 1, mix_half(st))
                if qk_group(st) is not None:
                    evac_heads(st.pair + 1, qk_group(st))
                if len(st.blocks) > 1:
                    second_group(st)
                if st.k == 2 * NT - 1:
                    normalise(st.pair, 0)
                if st.pair > 0 and st.k == 0:
                    normalise(st.pair - 1, 1)
            normalise(PAIRS - 1, 1)
            for half in range(2):
                evac_mix(PAIRS - 1, half)


def dn_done(pair, turn):
    n = 2 * pair + turn + 1
    return n + max(n - 3 * HEADS, 0)


def over_pairs(eng, n, body):
    body(0)
    with eng.Fori(1, n - 1) as i:
        body(i)
    body(n - 1)


def first(i):
    return isinstance(i, int) and i == 0


def out_signals(s):
    sig = s.counted
    NT = s.NT
    half = 16 * NT // 2
    g = Shared()
    g.wr = sig("router_weights_loaded", 32)
    g.x = [sig(f"residual_loaded{j}", half) for j in range(2)]
    g.hs = [sig(f"h_stored{j}", half) for j in range(2)]
    g.xs = [sig(f"normed_stored{j}", half) for j in range(2)]
    g.mt = sig("mix_tile_ready", NT)
    g.wo = sig("output_projected", NT)
    g.h = sig("h_ready", NT)
    g.sq = sig("h_squares_summed", NT)
    g.rt = sig("h_root_taken", NT)
    g.r = sig("h_scale_ready", NT)
    g.xn = sig("normed_ready", NT)
    g.xt = sig("normed_transposed", NT)
    g.xo = sig("normedT_ready", 2 * NT)
    g.lm = sig("router_logits_done", NT)
    g.lo = sig("router_logits_out", NT)
    return g


def out_route(nc, s, g, layer):
    NT, KT, D, R, NG = s.NT, s.KT, s.D, s.R, s.NG
    bk, pairs, ins = s.banks, s.bank_pairs, s.ins
    w = s.r_proj

    def pair_of(at, n):
        return [w[:, at + j * n:at + (j + 1) * n] for j in range(2)]

    mt = [a.rearrange("p (k n) -> p k n", k=KT) for a in pair_of(8192, 1024)]
    x_t, h_t, xn_t = pair_of(10240, 1024), pair_of(12288, 1024), pair_of(14336, 1024)
    xnT = [a.rearrange("p (k n) -> p k n", k=KT) for a in pair_of(16384, 1024)]
    w_r = w[:, 18432:18432 + KT * R].rearrange("p (k n) -> p k n", k=KT)
    s.lg = lg = w[:, 18720:18720 + NT * R].rearrange("p (t n) -> p t n", t=NT)
    mixT = s.r_tile[:, :].rearrange("p (k n) -> p k n", k=KT)
    NP = NT // 2

    def rows(dram, i, j):
        return dram[bass.ds((2 * i + j) * P, P)]

    with nc.Block() as block:
        @block.sync
        def _(sp):
            sp.dma_start(w_r[:, :, 0:NG], ins["w_rg"][layer].rearrange("(p k) n -> p k n", k=KT)).then_inc(
                g.wr.sem, 16)
            sp.dma_start(w_r[:, :, NG:R], ins["w_re"][layer].rearrange("(p k) n -> p k n", k=KT)).then_inc(
                g.wr.sem, 16)

            def body(i):
                for j in range(2):
                    if not first(i):
                        sp.wait_ge(g.h.sem, g.h.at(layer, 2 * i + j - 1))
                    sp.dma_start(x_t[j], rows(s.out_f, i, j)).then_inc(g.x[j].sem, 16)
                for j in range(2):
                    t = 2 * i + j
                    sp.wait_ge(g.h.sem, g.h.at(layer, t + 1))
                    sp.dma_start(rows(s.out_f, i, j), h_t[j]).then_inc(g.hs[j].sem, 16)
                    sp.wait_ge(g.xn.sem, g.xn.at(layer, t + 1))
                    sp.dma_start(rows(s.xn_dram, i, j), xn_t[j]).then_inc(g.xs[j].sem, 16)

            over_pairs(sp, NP, body)
            for j in range(2):
                wait_alone(sp, s, g.hs[j].sem, g.hs[j].at(layer, 16 * NP))
                wait_alone(sp, s, g.xs[j].sem, g.xs[j].at(layer, 16 * NP))

        @block.tensor
        def _(pe):
            def project_tile(i, j):
                t = 2 * i + j
                pe.wait_ge(g.mt.sem, g.mt.at(layer, t + 1))
                for c in range(2):
                    for k in range(KT):
                        mm = pe.matmul(bk[2 * j + c][:, :], mt[j][:, k, :], s.w_o[:, k, 512 * c:512 * c + 512],
                                       start=(k == 0), stop=(k == KT - 1))
                mm.then_inc(g.wo.sem, 1)

            def body(i):
                for j in range(2):
                    t = 2 * i + j
                    if not (isinstance(i, int) and i == NP - 1 and j == 1):
                        project_tile(i + j, 1 - j)
                    pe.wait_ge(g.xn.sem, g.xn.at(layer, t + 1))
                    xs = xn_t[j].rearrange("p (q k) -> p k q", k=KT)
                    for k in range(KT):
                        mm = pe.transpose(bk[4 + k // 4][:, (k % 4) * P:(k % 4 + 1) * P], xs[:, k, :], s.ident[:, :])
                    mm.then_inc(g.xt.sem, 1)
                    pe.wait_ge(g.xo.sem, g.xo.at(layer, 2 * t + 2))
                    if not (first(i) and j == 0):
                        pe.wait_ge(g.lo.sem, g.lo.at(layer, t))
                    for k in range(KT):
                        mm = pe.matmul(bk[6][:, 0:R], xnT[j][:, k, :], w_r[:, k, :], start=(k == 0),
                                       stop=(k == KT - 1))
                    mm.then_inc(g.lm.sem, 1)

            s_wo = s.attend_sems.wo
            pe.wait_ge(s_wo.sem, s_wo.at(layer, 16))
            pe.wait_ge(g.wr.sem, g.wr.at(layer, 32))
            project_tile(0, 0)
            over_pairs(pe, NP, body)

        @block.scalar
        def _(act):
            def body(i):
                for j in range(2):
                    t = 2 * i + j
                    act.wait_ge(g.h.sem, g.h.at(layer, t + 1))
                    if not first(i):
                        act.wait_ge(g.xs[j].sem, g.xs[j].at(layer, 16 * i))
                    nc.scalar.activation(xn_t[j], h_t[j], ACT.Square, scale=D ** -0.5,
                                         accum_out=s.rx[:, j, 0:1]).then_inc(g.sq.sem, 1)
                    act.wait_ge(g.sq.sem, g.sq.at(layer, t + 1))
                    nc.scalar.activation(s.rx[:, j, 1:2], s.rx[:, j, 0:1], ACT.Sqrt,
                                         bias=s.eps[:, 0:1]).then_inc(g.rt.sem, 1)
                    act.wait_ge(g.r.sem, g.r.at(layer, t + 1))
                    nc.scalar.activation(xn_t[j], h_t[j], ACT.Copy, scale=s.rx[:, j, 2:3]).then_inc(g.xn.sem, 1)

            over_pairs(act, NP, body)

        @block.vector
        def _(dve):
            def stage_mix(i, j):
                nc.vector.tensor_scalar(mt[j], mixT[:, :, bass.ds((2 * i + j) * P, P)], 1.0, None,
                                        ALU.mult).then_inc(g.mt.sem, 1)

            def body(i):
                for j in range(2):
                    t = 2 * i + j
                    dve.wait_ge(g.wo.sem, g.wo.at(layer, t + 1))
                    dve.wait_ge(g.x[j].sem, g.x[j].at(layer, 16 * (i + 1)))
                    if not first(i):
                        dve.wait_ge(g.hs[j].sem, g.hs[j].at(layer, 16 * i))
                    nc.vector.tensor_tensor(h_t[j], pairs[j][:, :], x_t[j], ALU.add).then_inc(g.h.sem, 1)
                    if not (isinstance(i, int) and i == NP - 1):
                        stage_mix(i + 1, j)
                    dve.wait_ge(g.rt.sem, g.rt.at(layer, t + 1))
                    nc.vector.reciprocal(s.rx[:, j, 2:3], s.rx[:, j, 1:2]).then_inc(g.r.sem, 1)
                    dve.wait_ge(g.xt.sem, g.xt.at(layer, t + 1))
                    for half in range(2):
                        nc.vector.tensor_tensor(
                            xnT[j][:, 4 * half:4 * half + 4, :], bk[4 + half].rearrange("p (k n) -> p k n", k=4),
                            bcast(s.gain2[:, 4 * half:4 * half + 4].unsqueeze(2), [P, 4, P]),
                            ALU.mult).then_inc(g.xo.sem, 1)
                    dve.wait_ge(g.lm.sem, g.lm.at(layer, t + 1))
                    nc.vector.tensor_tensor(lg[:, t, :], bk[6][:, 0:R], s.route_b[:, :], ALU.add).then_inc(
                        g.lo.sem, 1)

            stage_mix(0, 0)
            stage_mix(0, 1)
            over_pairs(dve, NP, body)


def route_signals(s):
    sig = s.counted
    g = Shared()
    g.v = sig("routing_vector_steps", 0)
    g.e = sig("routing_exps", 2)
    g.p = sig("routing_counted", 2)
    g.sc = sig("slots_scattered", 32 * s.NT)
    return g


def route(nc, s, g, layer):
    NT, NG, PER, E = s.NT, s.NG, s.PER, s.E
    bk, lg, t_ = s.banks, s.lg, s.r_tile
    at = [0]

    def take(*shape, dt=F32):
        n = 1
        for x in shape:
            n *= x
        a = t_[:, at[0]:at[0] + n]
        at[0] += n
        if dt is not F32:
            a = a.bitcast(dt)
        if len(shape) == 2:
            a = a.rearrange("p (a b) -> p a b", a=shape[0])
        return a

    m0, m1, mm_ = take(NT, E), take(NT, E), take(NT, E)
    pos, prod, masked = take(NT, E), take(NT, E), take(NT, E)
    gl, gm, em = take(NT, 8), take(NT, 8), take(NT, 8)
    gi, ei = take(NT, 8, dt=U32), take(NT, 8, dt=U32)
    oh, dg, eg = take(NT, NG), take(NT, NG), take(NT, NG)
    gif, pg, d, ed, den = take(NT, 1), take(NT, 1), take(NT, 1), take(NT, 1), take(NT, 1)
    eif, slf = take(NT, 2), take(NT, 2)
    slots = take(NT, 2, dt=I32)
    cnt, cnti = take(1), take(1, dt=I32)
    steps = 16 + 16 + 28

    with nc.Block() as block:
        g.v.per_pass = ROUTE_STEPS

        @block.vector
        def _(dve):
            n = [0]

            def link(ins):
                n[0] += 1
                ins.then_inc(g.v.sem, 1)
                wait_alone(dve, s, g.v.sem, g.v.at(layer, n[0]))
                return n[0]

            v = nc.vector
            link(v.memset(gl[:, :, NG:8], NEG))
            link(v.tensor_copy(gl[:, :, 0:NG], lg[:, :, 0:NG]))
            for t in range(NT):
                link(v.max(gm[:, t, :], gl[:, t, :]))
                link(v.max_index(gi[:, t, :], gm[:, t, :], gl[:, t, :]))
            g.dg_at = link(v.tensor_tensor(dg, gl[:, :, 0:NG], bcast(gm[:, :, 0:1], [P, NT, NG]), ALU.subtract))
            link(v.tensor_copy(gif, gi[:, :, 0:1]))
            link(v.tensor_tensor(oh, bcast(s.iota[:, 0:NG].unsqueeze(1), [P, NT, NG]),
                                 bcast(gif, [P, NT, NG]), ALU.is_equal))
            link(v.tensor_scalar(oh, oh, -1.0, BIG, ALU.add, ALU.mult))
            for t in range(NT):
                link(v.tensor_tensor(masked[:, t, :].rearrange("p (g e) -> p g e", g=NG),
                                     lg[:, t, NG:NG + E].rearrange("p (g e) -> p g e", g=NG),
                                     bcast(oh[:, t, :].unsqueeze(2), [P, NG, PER]), ALU.add))
                link(v.max(em[:, t, :], masked[:, t, :]))
                link(v.max_index(ei[:, t, :], em[:, t, :], masked[:, t, :]))
            g.d_at = link(v.tensor_tensor(d, em[:, :, 1:2], em[:, :, 0:1], ALU.subtract))
            link(v.tensor_copy(eif, ei[:, :, 0:2]))
            link(v.tensor_tensor(m0, bcast(s.iota[:, :].unsqueeze(1), [P, NT, E]),
                                 bcast(eif[:, :, 0:1], [P, NT, E]), ALU.is_equal))
            link(v.tensor_tensor(m1, bcast(s.iota[:, :].unsqueeze(1), [P, NT, E]),
                                 bcast(eif[:, :, 1:2], [P, NT, E]), ALU.is_equal))
            g.m_at = link(v.tensor_tensor(mm_, m0, m1, ALU.add))
            dve.wait_ge(g.e.sem, g.e.at(layer, 1))
            link(v.tensor_reduce(pg, eg, AX.X, ALU.add))
            link(v.reciprocal(pg, pg))
            dve.wait_ge(g.e.sem, g.e.at(layer, 2))
            link(v.tensor_scalar(den, ed, 1.0, None, ALU.add))
            link(v.reciprocal(den, den))
            link(v.tensor_tensor(s.gates[:, :, 0:1], pg, den, ALU.mult))
            link(v.tensor_tensor(s.gates[:, :, 1:2], s.gates[:, :, 0:1], ed, ALU.mult))
            dve.wait_ge(g.p.sem, g.p.at(layer, 1))
            link(v.tensor_copy(pos, bk[0][:, 0:NT * E].rearrange("p (t e) -> p t e", t=NT)))
            for k, mk in enumerate((m0, m1)):
                link(v.tensor_tensor(prod, mk, pos, ALU.mult))
                link(v.tensor_reduce(s.rel[:, :, k:k + 1], prod, AX.X, ALU.add))
            link(v.scalar_tensor_tensor(out=slf, in0=s.rel[:, :, :], scalar=float(E), in1=eif, op0=ALU.mult,
                                        op1=ALU.add))
            g.slots_at = link(v.tensor_copy(slots, slf))
            link(v.scalar_tensor_tensor(out=s.base_row[:, :, :], in0=eif, scalar=float(P), in1=s.rel[:, :, :],
                                        op0=ALU.mult, op1=ALU.add))
            dve.wait_ge(g.p.sem, g.p.at(layer, 2))
            link(v.tensor_reduce(cnt[0:1], bk[1][0:1, 0:E], AX.X, ALU.max))
            link(v.tensor_scalar(cnti[0:1], cnt[0:1], float(P - 1), None, ALU.add))
            link(v.tensor_scalar(s.nrounds[0:1, 0:1], cnti[0:1], 7, None, ALU.logical_shift_right))
            assert n[0] == ROUTE_STEPS, n[0]

        @block.scalar
        def _(act):
            act.wait_ge(g.v.sem, g.v.at(layer, g.dg_at))
            nc.scalar.activation(eg, dg, ACT.Exp).then_inc(g.e.sem, 1)
            act.wait_ge(g.v.sem, g.v.at(layer, g.d_at))
            nc.scalar.activation(ed, d, ACT.Exp).then_inc(g.e.sem, 1)

        @block.tensor
        def _(pe):
            pe.wait_ge(g.v.sem, g.v.at(layer, g.m_at))
            pe.matmul(bk[0][:, 0:NT * E], s.before[:, :], mm_.rearrange("p t e -> p (t e)"), start=True, stop=False)
            for t in range(NT - 1):
                mm = pe.matmul(bk[0][:, (t + 1) * E:NT * E], s.ones[:, :],
                               bcast(mm_[:, t:t + 1, :], [P, NT - 1 - t, E]), start=False, stop=(t == NT - 2))
            mm.then_inc(g.p.sem, 1)
            for t in range(NT):
                mm = pe.matmul(bk[1][:, 0:E], s.ones[:, :], mm_[:, t, :], start=(t == 0), stop=(t == NT - 1))
            mm.then_inc(g.p.sem, 1)

        @block.gpsimd
        def _(pool):
            wait_alone(pool, s, g.v.sem, g.v.at(layer, g.slots_at))
            for t in range(NT):
                for k in range(2):
                    nc.gpsimd.indirect_dma_start(
                        out=s.table, out_offset=bass.IndirectOffsetOnAxis(ap=slots[:, t, k:k + 1], axis=0),
                        in_=s.tokid[:, t:t + 1], in_offset=None).then_inc(g.sc.sem, 16)
            wait_alone(pool, s, g.sc.sem, g.sc.at(layer, 32 * NT))


ROUTE_STEPS = 68


def wait_alone(eng, s, sem, value):
    reg = s.wait_value[eng.engine]
    eng.reg_mov(reg, value)
    value = eng.snap(reg)
    eng.wait_ge(s.start_sets.sem, 1)
    eng.wait_ge(sem, value)


def expert_signals(s):
    sig = s.counted
    E, NT = s.E, s.NT
    g = Shared()
    g.ix = sig("slot_tokens_loaded", 16)
    g.gx = [sig(f"tokens_gathered{j}", 8 * E) for j in range(2)]
    g.w13 = [sig(f"w1_w3_loaded{j}", 16 * E) for j in range(2)]
    g.w2 = [sig(f"w2_loaded{j}", 8 * E) for j in range(2)]
    g.xt = sig("tokens_transposed", E)
    g.xo = sig("tokensT_ready", 2 * E)
    g.hm = sig("hidden_done", E)
    g.sl = sig("silu_ready", E)
    g.hd = sig("hidden_ready", E)
    g.ht = sig("hidden_transposed", E)
    g.ho = sig("hiddenT_ready", E)
    g.ym = sig("expert_rows_done", E)
    g.ya = sig("expert_rows_out_scalar", E)
    g.yv = sig("expert_rows_out_vector", E)
    g.ys = [sig(f"expert_rows_stored{j}", 8 * E) for j in range(2)]
    g.ci = sig("combine_steps", 7)
    g.yg = [sig(f"expert_rows_gathered{j}", 16 * NT) for j in range(2)]
    g.hl = [sig(f"h_reloaded{j}", 8 * NT) for j in range(2)]
    g.ad = sig("expert_rows_added", 2 * NT)
    g.st = [sig(f"layer_stored{j}", 8 * NT) for j in range(2)]
    return g


def experts(nc, s, g, layer, rnd):
    NT, KT, E, F, D = s.NT, s.KT, s.E, s.F, s.D
    bk, pairs, ins = s.banks, s.bank_pairs, s.ins
    w = s.r_proj
    at = [0]

    def pair_of(n, region=w):
        at[0] += 2 * n
        return [region[:, at[0] - 2 * n + j * n:at[0] - n + j * n] for j in range(2)]

    w13 = [a.rearrange("p (k n) -> p k n", k=KT) for a in pair_of(KT * 2 * F)]
    w2 = [a.rearrange("p (k n) -> p k n", k=F // P) for a in pair_of(F // P * D)]
    xg = pair_of(D)
    xT = [a.rearrange("p (k n) -> p k n", k=KT) for a in pair_of(D)]
    sil, hid = pair_of(F), pair_of(F)
    hidT = [a.rearrange("p (k n) -> p k n", n=P) for a in pair_of(F)]
    y_t = pair_of(D)
    at[0] = 0
    h_t = pair_of(D, s.r_tile)
    yg = [[s.r_tile[:, 2048 + 1024 * (2 * j + k):3072 + 1024 * (2 * j + k)] for k in range(2)] for j in range(2)]
    idx = s.r_tile[:, 6144:6144 + E].bitcast(I32)
    small = s.r_tile[:, 6176:6176 + 5 * 2 * NT].rearrange("p (a b) -> p a b", a=5)
    va, vb = small[:, 0], small[:, 1]
    cidx, geff, vc = small[:, 2].bitcast(I32), small[:, 3], small[:, 4]
    NP = E // 2
    table_r = s.table.rearrange("(r p e) o -> r p (e o)", p=P, e=E)

    def count(eng):
        return eng.snap(s.rounds_done[eng.engine])

    def next_round(eng):
        eng.reg_add(s.rounds_done[eng.engine], s.rounds_done[eng.engine], 1)

    with nc.Block() as block:
        @block.sync
        def _(sp):
            done = count(sp)
            sp.dma_start(idx, table_r[rnd]).then_inc(g.ix.sem, 16)

            def body(i):
                for j in range(2):
                    e = 2 * i + j
                    if not first(i):
                        sp.wait_ge(g.hm.sem, g.hm.at(done, e - 1))
                    for c, name in enumerate(("w1", "w3")):
                        sp.dma_start(w13[j][:, :, F * c:F * (c + 1)],
                                     ins[name][layer, e].rearrange("(p k) n -> p k n", k=KT)).then_inc(
                                         g.w13[j].sem, 16)
                    if not first(i):
                        sp.wait_ge(g.ym.sem, g.ym.at(done, e - 1))
                    sp.dma_start(w2[j], ins["w2"][layer, e].rearrange("(k p) n -> p k n", p=P)).then_inc(
                        g.w2[j].sem, 16)

            over_pairs(sp, NP, body)
            for j in range(2):
                sp.wait_ge(g.ys[j].sem, g.ys[j].at(done, 8 * E))
            for t in range(NT):
                j = t % 2
                if t >= 2:
                    sp.wait_ge(g.ad.sem, g.ad.at(done, 2 * (t - 1)))
                    sp.dma_start(s.out_f[(t - 2) * P:(t - 1) * P], h_t[j]).then_inc(g.st[j].sem, 16)
                    sp.wait_ge(g.st[j].sem, g.st[j].at(done, 16 * (t // 2)))
                sp.dma_start(h_t[j], s.out_f[t * P:(t + 1) * P]).then_inc(g.hl[j].sem, 16)
            for t in range(NT - 2, NT):
                sp.wait_ge(g.ad.sem, g.ad.at(done, 2 * (t + 1)))
                sp.dma_start(s.out_f[t * P:(t + 1) * P], h_t[t % 2]).then_inc(g.st[t % 2].sem, 16)
            for j in range(2):
                wait_alone(sp, s, g.st[j].sem, g.st[j].at(done, 8 * NT))
            next_round(sp)

        @block.gpsimd
        def _(pool):
            done = count(pool)
            wait_alone(pool, s, g.ix.sem, g.ix.at(done, 16))
            for e in range(E):
                if e >= 2:
                    wait_alone(pool, s, g.xt.sem, g.xt.at(done, e - 1))
                nc.gpsimd.indirect_dma_start(
                    out=xg[e % 2], out_offset=None, in_=s.xn_dram,
                    in_offset=bass.IndirectOffsetOnAxis(ap=idx[:, e:e + 1], axis=0)).then_inc(g.gx[e % 2].sem, 16)
            for j in range(2):
                wait_alone(pool, s, g.ys[j].sem, g.ys[j].at(done, 8 * E))
            wait_alone(pool, s, g.ci.sem, g.ci.at(done, 5))
            for t in range(NT):
                if t >= 2:
                    wait_alone(pool, s, g.ad.sem, g.ad.at(done, 2 * (t - 1)))
                for k in range(2):
                    nc.gpsimd.indirect_dma_start(
                        out=yg[t % 2][k], out_offset=None, in_=s.y_dram,
                        in_offset=bass.IndirectOffsetOnAxis(ap=cidx[:, 2 * t + k:2 * t + k + 1], axis=0)).then_inc(
                            g.yg[t % 2].sem, 16)
            next_round(pool)

        @block.tensor
        def _(pe):
            done = count(pe)

            def transpose_tokens(i, j):
                pe.wait_ge(g.gx[j].sem, g.gx[j].at(done, 16 * (i + 1)))
                xs = xg[j].rearrange("p (q k) -> p k q", k=KT)
                for k in range(KT):
                    mm = pe.transpose(bk[k // 4][:, (k % 4) * P:(k % 4 + 1) * P], xs[:, k, :], s.ident[:, :])
                mm.then_inc(g.xt.sem, 1)

            def body(i):
                for j in range(2):
                    e = 2 * i + j
                    pe.wait_ge(g.w13[j].sem, g.w13[j].at(done, 32 * (i + 1)))
                    pe.wait_ge(g.xo.sem, g.xo.at(done, 2 * e + 2))
                    if not first(i):
                        pe.wait_ge(g.hd.sem, g.hd.at(done, e - 1))
                    for k in range(KT):
                        mm = pe.matmul(bk[2 + j][:, 0:2 * F], xT[j][:, k, :], w13[j][:, k, :], start=(k == 0),
                                       stop=(k == KT - 1))
                    mm.then_inc(g.hm.sem, 1)
                    if not (isinstance(i, int) and i == NP - 1 and j == 1):
                        transpose_tokens(i + j, 1 - j)
                    pe.wait_ge(g.hd.sem, g.hd.at(done, e + 1))
                    for k in range(F // P):
                        mm = pe.transpose(bk[4][:, k * P:(k + 1) * P], hid[j][:, k * P:(k + 1) * P], s.ident[:, :])
                    mm.then_inc(g.ht.sem, 1)
                    pe.wait_ge(g.ho.sem, g.ho.at(done, e + 1))
                    pe.wait_ge(g.w2[j].sem, g.w2[j].at(done, 16 * (i + 1)))
                    if not (first(i) and j == 0):
                        pe.wait_ge(g.ya.sem, g.ya.at(done, e))
                        pe.wait_ge(g.yv.sem, g.yv.at(done, e))
                    for c in range(2):
                        for k in range(F // P):
                            mm = pe.matmul(bk[6 + c][:, :], hidT[j][:, k, :], w2[j][:, k, 512 * c:512 * c + 512],
                                           start=(k == 0), stop=(k == F // P - 1))
                    mm.then_inc(g.ym.sem, 1)

            transpose_tokens(0, 0)
            over_pairs(pe, NP, body)
            next_round(pe)

        @block.scalar
        def _(act):
            done = count(act)

            def body(i):
                for j in range(2):
                    e = 2 * i + j
                    act.wait_ge(g.hm.sem, g.hm.at(done, e + 1))
                    nc.scalar.activation(sil[j], bk[2 + j][:, 0:F], ACT.Silu).then_inc(g.sl.sem, 1)
                    act.wait_ge(g.ht.sem, g.ht.at(done, e + 1))
                    nc.scalar.activation(hidT[j], bk[4][:, 0:F].rearrange("p (k n) -> p k n", n=P),
                                         ACT.Copy).then_inc(g.ho.sem, 1)
                    act.wait_ge(g.ym.sem, g.ym.at(done, e + 1))
                    if not first(i):
                        act.wait_ge(g.ys[j].sem, g.ys[j].at(done, 16 * i))
                    nc.scalar.activation(y_t[j][:, 0:512], bk[6][:, :], ACT.Copy).then_inc(g.ya.sem, 1)
                    act.wait_ge(g.ya.sem, g.ya.at(done, e + 1))
                    act.wait_ge(g.yv.sem, g.yv.at(done, e + 1))
                    act.dma_start(s.y_dram[bass.ds(e * P, P)], y_t[j]).then_inc(g.ys[j].sem, 16)

            over_pairs(act, NP, body)
            next_round(act)

        @block.vector
        def _(dve):
            done = count(dve)

            def evac_tokens(i, j):
                e = 2 * i + j
                dve.wait_ge(g.xt.sem, g.xt.at(done, e + 1))
                for half in range(2):
                    nc.vector.tensor_tensor(
                        xT[j][:, 4 * half:4 * half + 4, :], bk[half].rearrange("p (k n) -> p k n", k=4),
                        bcast(s.gain2[:, 4 * half:4 * half + 4].unsqueeze(2), [P, 4, P]),
                        ALU.mult).then_inc(g.xo.sem, 1)

            def body(i):
                for j in range(2):
                    e = 2 * i + j
                    dve.wait_ge(g.sl.sem, g.sl.at(done, e + 1))
                    nc.vector.tensor_tensor(hid[j], sil[j], bk[2 + j][:, F:2 * F], ALU.mult).then_inc(g.hd.sem, 1)
                    if not (isinstance(i, int) and i == NP - 1 and j == 1):
                        evac_tokens(i + j, 1 - j)
                    dve.wait_ge(g.ym.sem, g.ym.at(done, e + 1))
                    if not first(i):
                        dve.wait_ge(g.ys[j].sem, g.ys[j].at(done, 16 * i))
                    nc.vector.tensor_copy(y_t[j][:, 512:1024], bk[7][:, :]).then_inc(g.yv.sem, 1)

            def step(n, ins):
                ins.then_inc(g.ci.sem, 1)
                wait_alone(dve, s, g.ci.sem, g.ci.at(done, n))

            rel, base, gates = (a[:, :, :].rearrange("p t k -> p (t k)") for a in (s.rel, s.base_row, s.gates))
            step(1, nc.vector.tensor_scalar(va, rel, 0.0, None, ALU.is_ge))
            step(2, nc.vector.tensor_scalar(vb, rel, float(P), None, ALU.is_lt))
            step(3, nc.vector.tensor_tensor(vc, va, vb, ALU.mult))
            step(4, nc.vector.tensor_tensor(geff, vc, gates, ALU.mult))
            step(5, nc.vector.tensor_tensor(cidx, vc, base, ALU.mult))
            step(6, nc.vector.tensor_scalar(rel, rel, -float(P), None, ALU.add))
            step(7, nc.vector.tensor_scalar(base, base, -float(P), None, ALU.add))

            evac_tokens(0, 0)
            over_pairs(dve, NP, body)

            for t in range(NT):
                j = t % 2
                dve.wait_ge(g.hl[j].sem, g.hl[j].at(done, 16 * (t // 2 + 1)))
                dve.wait_ge(g.yg[j].sem, g.yg[j].at(done, 32 * (t // 2 + 1)))
                for k in range(2):
                    nc.vector.scalar_tensor_tensor(out=h_t[j], in0=yg[j][k], scalar=geff[:, 2 * t + k:2 * t + k + 1],
                                                   in1=h_t[j], op0=ALU.mult, op1=ALU.add).then_inc(g.ad.sem, 1)
                    if k == 0:
                        dve.wait_ge(g.ad.sem, g.ad.at(done, 2 * t + 1))
            next_round(dve)


def tables(seq, experts_n):
    import numpy as np

    p = np.arange(P)
    nt = seq // P
    slopes = 2.0 ** (-8.0 * np.arange(1, 2 * HEADS + 1) / (2 * HEADS))
    inv = np.float32(10000.0) ** (-np.arange(0, NROPE, 2, dtype=np.float32) / np.float32(NROPE))
    ang = (np.arange(seq, dtype=np.float32)[:, None] * inv[None, :]).astype(np.float32)
    cs = np.stack([np.cos(ang), np.sin(ang)], 0).reshape(2, nt, P, NROPE // 2).transpose(2, 0, 1, 3)
    dist = p[:, None] + (seq - P) - np.arange(seq)[None, :]
    mult = sum(((dist >= 0) & (dist <= w) & (dist % dl == 0)).astype(np.float64)
               for w, dl in ((128, 1), (512, 4), (2048, 16)))
    dilated = [np.where(mult > 0, np.log(np.maximum(mult, 1)) - sl * dist, NEG) for sl in slopes[HEADS:]]
    near = p[:, None] + P - np.arange(2 * P)[None, :]
    window = [np.where((near >= 0) & (near < P), -sl * near, NEG) for sl in slopes[:HEADS]]
    f = np.float32
    return {
        "ident": np.eye(P, dtype=f), "ones": np.ones((P, P), f),
        "upto": (p[:, None] <= p[None, :]).astype(f), "before": (p[:, None] < p[None, :]).astype(f),
        "cos_sin": np.ascontiguousarray(cs).astype(f),
        "iota": np.tile(np.arange(experts_n, dtype=f), (P, 1)),
        "tokid": (p[:, None] + P * np.arange(nt)[None, :]).astype(np.int32),
        "causal": np.where(dist >= 0, 0.0, NEG).astype(f),
        "dilated": np.stack(dilated).astype(f), "window": np.stack(window).astype(f),
    }


_INS = ("x", "norm1_g", "w_in", "mla_gcq", "mla_gckv", "mla_wuq", "mla_wukv", "qk_gq", "qk_gk", "fox_bf", "sink",
        "w_o", "norm2_g", "w_rg", "b_rg", "w_re", "b_re", "w1", "w3", "w2")


def kernel(**inputs):
    import numpy as np
    import concourse.bacc as bacc
    from concourse.bass_utils import run_bass_kernel_spmd

    nc = bacc.Bacc("TRN2", target_bir_lowering=False, num_devices=1)
    arrays, ins, consts = {}, {}, {}
    for name in _INS:
        a = np.ascontiguousarray(inputs[name])
        arrays["in_" + name] = a
        ins[name] = nc.dram_tensor("in_" + name, a.shape, F32, kind="ExternalInput").ap()
    seq, d = inputs["x"].shape[1:]
    n_exp = inputs["w1"].shape[1]
    for name, a in tables(seq, n_exp).items():
        arrays["table_" + name] = a
        consts[name] = nc.dram_tensor("table_" + name, a.shape, mybir.dt.from_np(a.dtype), kind="ExternalInput").ap()
    scratch = {
        "xn": nc.dram_tensor("normed", (seq, d), F32, kind="Internal").ap(),
        "y": nc.dram_tensor("expert_rows", (n_exp * P, d), F32, kind="Internal").ap(),
        "table": nc.dram_tensor("slot_tokens", (seq * n_exp, 1), I32, kind="Internal").ap(),
    }
    out = nc.dram_tensor("out", inputs["x"].shape, F32, kind="ExternalOutput").ap()
    trunk(nc, ins, consts, scratch, out)
    return run_bass_kernel_spmd(nc, [arrays], core_ids=[0]).results[0]["out"]
```

```python
from contextlib import ExitStack

import concourse.bass as bass
from concourse import mybir

ALU = mybir.AluOpType
ACT = mybir.ActivationFunctionType
AX = mybir.AxisListType
F32 = mybir.dt.float32
I32 = mybir.dt.int32
U32 = mybir.dt.uint32

P = 128
EPS = 1e-6
NEG = -1e30
HD = 64
HEADS = 4
MIXERS = 4
NQR, NKV, NROPE, NNOPE = 192, 128, 32, 32
GW = HEADS * HD
START_LOADS, START_LATE = 16 * 2, 16 * 2
CHUNKS = (352, 384, 384, 384, 388, 512)
AUG = HD + 2
BIG = 1e30


class Signal:

    def __init__(self, sem, per_pass):
        self.sem, self.per_pass = sem, per_pass

    def at(self, done, k):
        return done * self.per_pass + k


def trunk(nc, ins, consts, scratch, out):
    x_in = ins["x"]
    _, SEQ, D = x_in.shape
    L = ins["w_in"].shape[0]
    NT = SEQ // P
    KT = D // P
    E = ins["w1"].shape[1]
    F = ins["w1"].shape[3]
    NG = ins["w_rg"].shape[2]
    PER = E // NG
    R = NG + E
    ROUNDS = SEQ // P
    W1D = sum(CHUNKS)
    coff = [sum(CHUNKS[:c]) for c in range(len(CHUNKS))]
    widths = (3 * GW, 3 * GW, 3 * GW, 2 * GW)
    pbase = [NT * sum(widths[:m]) for m in range(MIXERS)]

    out_f = out.rearrange("b s d -> (b s) d")
    x_f = x_in.rearrange("b s d -> (b s) d")
    xn_dram, y_dram, table = scratch["xn"], scratch["y"], scratch["table"]

    ctx = ExitStack()
    with ctx:
        def sb(name, shape, dt=F32):
            return ctx.enter_context(nc.sbuf_tensor(name, shape, dt))

        def counted(name, per_pass):
            return Signal(ctx.enter_context(nc.semaphore(name)), per_pass)

        r_proj = sb("r_proj", [P, NT * sum(widths)])
        r_win = sb("r_win", [P, KT * W1D])
        r_tile = sb("r_tile", [P, 8 * SEQ])
        bank_pairs = [ctx.enter_context(nc.psum_tensor(f"banks{b}", [P, 1024], F32)) for b in range(4)]
        banks = [bank_pairs[b // 2][:, 512 * (b % 2):512 * (b % 2) + 512] for b in range(8)]

        fixed = sb("fixed", [P, 4 * P + E + 2 * NT * (NROPE // 2)])
        ident, ones, upto, before = (fixed[:, n * P:(n + 1) * P] for n in range(4))
        iota = fixed[:, 4 * P:4 * P + E]
        cos_sin = fixed[:, 4 * P + E:].rearrange("p (a t c) -> p a t c", a=2, t=NT)
        w_lat = sb("w_lat", [P, 1024])
        tokid = sb("tokid", [P, NT], I32)
        eps = sb("eps", [P, 1])
        gain1 = sb("gain1", [P, KT])
        gain2 = sb("gain2", [P, KT])
        gain_lat = sb("gain_lat", [P, 3])
        gain_a = sb("gain_a", [P, 2 * HEADS, HD])
        gain_raw = sb("gain_raw", [P, 2 * MIXERS])
        gain_qk = sb("gain_qk", [P, 2 * MIXERS])
        sink_b = sb("sink_b", [P, HEADS])
        fox_b = sb("fox_b", [P, HEADS])
        route_b = sb("route_b", [P, R])
        rx = sb("rx", [P, 2, 3])
        rl = sb("rl", [P, 2, 3, 2])
        ssq = sb("ssq", [P, NT, 30])
        rs = sb("rs", [P, NT, 30])
        fg = sb("fg", [P, NT, HEADS])
        fox = sb("fox", [P, 4, NT, HEADS])
        cum = sb("cum", [P, 2, NT, HEADS])
        rowmax = sb("rowmax", [P, 2])
        never = sb("never", [P, 1])
        gates = sb("gates", [P, NT, 2])
        base_row = sb("base_row", [P, NT, 2])
        rel = sb("rel", [P, NT, 2])
        nrounds = sb("nrounds", [1, 1], I32)
        junk = sb("junk", [P, 4])

        start_loads = counted("start_loads", 0)
        start_sets = counted("start_sets", 0)
        start_late = counted("start_late_loads", 0)
        zeros_i = r_proj[:, 0:256].bitcast(I32)

        s = Shared()
        s.ins = ins
        s.KT = KT
        s.NT = NT
        s.NG = NG
        s.R = R
        s.L = L
        s.coff = coff
        s.counted = counted
        s.r_win = r_win
        s.gain1 = gain1
        s.gain2 = gain2
        s.gain_lat = gain_lat
        s.gain_a = gain_a
        s.gain_raw = gain_raw
        s.sink_b = sink_b
        s.fox_b = fox_b
        s.route_b = route_b
        s.next_layer = {e.engine: e.alloc_register("next_layer") for e in (nc.sync, nc.scalar)}
        project_sems = project_signals(s)

        with nc.Block() as block:
            @block.sync
            def _(sp):
                sp.dma_start(fixed[:, :], consts["fixed"]).then_inc(start_loads.sem, 16)
                for j in range(2):
                    sp.dma_start(r_tile[:, j * D:(j + 1) * D], x_f[j * P:(j + 1) * P]).then_inc(
                        project_sems.x[j].sem, 16)
                sp.wait_ge(start_sets.sem, 1)
                sp.dma_start(table.rearrange("(p c) o -> p (c o)", p=P), zeros_i).then_inc(start_loads.sem, 16)
                sp.wait_ge(project_sems.small.sem, project_sems.small.per_pass)
                load_w_in(sp, s, project_sems, 0)
                sp.dma_start(out_f, x_f).then_inc(start_late.sem, 16)
                sp.dma_start(tokid[:, :], consts["tokid"]).then_inc(start_late.sem, 16)

            @block.scalar
            def _(act):
                act.wait_ge(start_sets.sem, 2)
                load_tables(act, s, project_sems, 0)

            @block.vector
            def _(dve):
                nc.vector.memset(zeros_i, 0).then_inc(start_sets.sem, 1)
                nc.vector.memset(eps[:, :], EPS)
                nc.vector.memset(never[:, :], NEG)
                nc.vector.memset(gain_raw[:, :], 1.0)
                nc.vector.memset(gain_qk[:, :], 1.0)
                nc.vector.memset(gain_lat[:, :], 1.0)
                nc.vector.memset(junk[:, :], 0.0).then_inc(start_sets.sem, 1)

        s.project_sems = project_sems
        s.D = D
        s.E = E
        s.F = F
        s.PER = PER
        s.SEQ = SEQ
        s.bank_pairs = bank_pairs
        s.banks = banks
        s.base_row = base_row
        s.before = before
        s.consts = consts
        s.cos_sin = cos_sin
        s.cum = cum
        s.eps = eps
        s.fg = fg
        s.fox = fox
        s.gain_qk = gain_qk
        s.gates = gates
        s.ident = ident
        s.iota = iota
        s.junk = junk
        s.never = never
        s.nrounds = nrounds
        s.ones = ones
        s.out_f = out_f
        s.pbase = pbase
        s.r_proj = r_proj
        s.r_tile = r_tile
        s.rel = rel
        s.rl = rl
        s.rowmax = rowmax
        s.rs = rs
        s.rx = rx
        s.ssq = ssq
        s.start_sets = start_sets
        s.start_loads = start_loads
        s.start_late = start_late
        s.table = table
        s.tokid = tokid
        s.upto = upto
        s.w_lat = w_lat
        s.widths = widths
        s.xn_dram = xn_dram
        s.y_dram = y_dram
        attend_sems = attend_signals(s)
        out_sems = out_signals(s)
        expert_sems = expert_signals(s)

        rounds_done = {}
        for eng in (nc.sync, nc.scalar, nc.vector, nc.gpsimd, nc.tensor):
            rounds_done[eng.engine] = eng.alloc_register("rounds_done")
            eng.reg_mov(rounds_done[eng.engine], 0)
        s.rounds_done = rounds_done
        s.attend_sems = attend_sems
        s.out_sems = out_sems
        s.wait_value = {e.engine: e.alloc_register("wait_value") for e in (nc.sync, nc.scalar, nc.vector, nc.gpsimd, nc.tensor)}

        with nc.Fori(0, L) as layer:
            project(nc, s, project_sems, layer)
            attend(nc, s, attend_sems, layer)
            out_route(nc, s, out_sems, layer)
            rounds = nc.values_load(nrounds[0:1, 0:1], min_val=1, max_val=ROUNDS)
            with nc.Fori(0, rounds) as rnd:
                experts(nc, s, expert_sems, layer, rnd)
        with nc.Block() as block:
            @block.sync
            def _(sp):
                for w_in in project_sems.w_in:
                    sp.wait_ge(w_in.sem, 16 * (L + 1))
                sp.wait_ge(project_sems.small.sem, project_sems.small.at(L, project_sems.small.per_pass))



class Shared:
    pass


def bcast(ap, shape):
    return ap.to_broadcast(shape)


def w_in_chunk(s, c):
    return s.r_win[:, s.KT * s.coff[c]:s.KT * (s.coff[c] + CHUNKS[c])].rearrange("p (k n) -> p k n", k=s.KT)


def layer_tables(s, layer):
    ins = s.ins
    gq, gk = ins["qk_gq"][layer], ins["qk_gk"][layer]
    cq, ck = ins["mla_gcq"][layer], ins["mla_gckv"][layer]
    tabs = [(s.gain1[:, :], ins["norm1_g"][layer].rearrange("(p k) -> p k", k=s.KT)),
            (s.gain_lat[:, 0:1], cq[0:128].rearrange("(p o) -> p o", o=1)),
            (s.gain_lat[0:64, 1:2], cq[128:192].rearrange("(p o) -> p o", o=1)),
            (s.gain_lat[:, 2:3], ck.rearrange("(p o) -> p o", o=1))]
    for n, gain in enumerate((gq, gk)):
        tabs.append((s.gain_a[:, HEADS * n:HEADS * (n + 1), :],
                     bcast(gain[0].partition_broadcast(P).unsqueeze(1), [P, HEADS, HD])))
        tabs.append((s.gain_raw[0:HD, MIXERS * n + 1:MIXERS * (n + 1)].unsqueeze(2),
                     gain[1:MIXERS].rearrange("m (p o) -> p m o", o=1)))
    for dst, name in ((s.sink_b, "sink"), (s.fox_b, "fox_bf")):
        tabs.append((dst[:, :], ins[name][layer].partition_broadcast(P)))
    return tabs


def late_tables(s, layer):
    return [(s.gain2[:, :], s.ins["norm2_g"][layer].rearrange("(p k) -> p k", k=s.KT)),
            (s.route_b[:, 0:s.NG], s.ins["b_rg"][layer].partition_broadcast(P)),
            (s.route_b[:, s.NG:s.R], s.ins["b_re"][layer].partition_broadcast(P))]


def load_tables(act, s, g, layer):
    for dst, src in layer_tables(s, layer):
        act.dma_start(dst, src, allow_slow_non_contiguous=True).then_inc(g.small.sem, 16)


def load_w_in(sp, s, g, layer, chunks=range(len(CHUNKS))):
    for c in chunks:
        src = s.ins["w_in"][layer].rearrange("(p k) n -> p k n", k=s.KT)[:, :, s.coff[c]:s.coff[c] + CHUNKS[c]]
        sp.dma_start(w_in_chunk(s, c), src).then_inc(g.w_in[c].sem, 16)


def project_signals(s):
    sig = s.counted
    NT = s.NT
    g = Shared()
    g.w_in = [sig(f"w_in_loaded{c}", 16) for c in range(len(CHUNKS))]
    g.small = sig("layer_tables_loaded", 16 * len(layer_tables(s, 0)))
    g.late = sig("late_tables_loaded", 16 * 3)
    g.x = [sig(f"x_loaded{j}", 16 * (NT // 2 - 1)) for j in range(2)]
    g.x_sq = sig("x_squares_summed", NT)
    g.x_rt = sig("x_root_taken", NT)
    g.x_r = sig("x_scale_ready", NT)
    g.xT = sig("x_transposed", NT)
    g.uT = sig("uT_ready", 2 * NT)
    g.mm = sig("projected", 6 * NT)
    g.mo = sig("projection_out", 7 * NT + 3)
    g.l_sq = sig("latent_squares_summed", 2 * NT)
    g.l_rt = sig("latent_root_taken", NT)
    g.l_r = sig("latent_scale_ready", NT)
    g.lT = sig("latent_transposed", NT)
    g.lo = sig("latentT_ready", 3 * NT)
    g.am = sig("latents_expanded", NT)
    g.ao = sig("mixer_a_out", 4 * NT + 1)
    g.rope = sig("rope_steps", 7 * NT)
    g.sq = sig("head_squares_ready", 4 * NT)
    g.red = sig("head_squares_summed", NT + 1)
    g.wl = sig("expand_weights_loaded", 0)
    g.gq = sig("gain_tables_ready", 1)
    return g


def project(nc, s, g, layer):
    P_, NT, KT = P, s.NT, s.KT
    D = s.D
    x_t = [s.r_tile[:, j * 1024:(j + 1) * 1024] for j in range(2)]
    uT = [s.r_tile[:, 2048 + j * 1024:2048 + (j + 1) * 1024].rearrange("p (k n) -> p k n", n=P) for j in range(2)]
    uT_flat = [s.r_tile[:, 2048 + j * 1024:2048 + (j + 1) * 1024] for j in range(2)]
    latT_flat = [s.r_tile[:, 4800 + j * 384:4800 + (j + 1) * 384] for j in range(2)]
    lat = [s.r_tile[:, 4096 + j * 352:4096 + (j + 1) * 352] for j in range(2)]
    latT = [s.r_tile[:, 4800 + j * 384:4800 + (j + 1) * 384].rearrange("p (k n) -> p k n", n=P) for j in range(2)]
    sqb = s.r_tile[:, 5568:5568 + 1920]
    rot = s.r_tile[:, 7488:7488 + 512].rearrange("p (a h c) -> p a h c", a=4, h=8)
    w_ch = [w_in_chunk(s, c) for c in range(6)]
    pm = [s.r_proj[:, s.pbase[m]:s.pbase[m] + NT * s.widths[m]].rearrange("p (t n) -> p t n", t=NT)
          for m in range(4)]
    s.pm = pm
    w_l = s.w_lat
    bk = s.banks
    ins = s.ins

    def blockfn(block):
        @block.sync
        def _(sp):
            sp.dma_start(w_l[:, 0:GW], ins["mla_wuq"][layer][0:128]).then_inc(g.wl.sem, 16)
            sp.dma_start(w_l[0:64, GW:2 * GW], ins["mla_wuq"][layer][128:192]).then_inc(g.wl.sem, 16)
            sp.dma_start(w_l[:, 2 * GW:2 * GW + 384], ins["mla_wukv"][layer]).then_inc(g.wl.sem, 16)
            for dst, src in late_tables(s, layer):
                sp.dma_start(dst, src).then_inc(g.late.sem, 16)
            sp.wait_ge(s.start_late.sem, START_LATE)
            with sp.Fori(0, NT // 2 - 1) as i:
                for j in range(2):
                    sp.wait_ge(g.uT.sem, g.uT.at(layer, 2 * (2 * i + j + 1)))
                    sp.dma_start(x_t[j], s.out_f[bass.ds((2 * i + 2 + j) * P, P)]).then_inc(g.x[j].sem, 16)

        @block.tensor
        def _(pe):
            def transpose_x(i, j):
                pe.wait_ge(g.x[j].sem, g.x[j].at(layer, 16 * (i + 1)))
                xs = x_t[j].rearrange("p (q k) -> p k q", k=KT)
                for k in range(KT):
                    mm = pe.transpose(bk[3 + k // 4][:, (k % 4) * P:(k % 4 + 1) * P], xs[:, k, :], s.ident[:, :])
                mm.then_inc(g.xT.sem, 1)

            def tile(i, j, last):
                t = 2 * i + j

                def chunk(c):
                    n = 6 * j + c
                    b = n % 3
                    pe.wait_ge(g.w_in[c].sem, g.w_in[c].at(layer, 16))
                    if c == 0:
                        pe.wait_ge(g.uT.sem, g.uT.at(layer, 2 * t + 2))
                    prev = n - 3
                    reads = 7 * (prev // 6) + (prev % 6 + 1) + (1 if prev % 6 >= 4 else 0)
                    if n > 0:
                        pe.wait_ge(g.mo.sem, g.mo.at(layer, 14 * i + reads + 3))
                    for k in range(KT):
                        mm = pe.matmul(bk[b][:, 0:CHUNKS[c]], uT[j][:, k, :], w_ch[c][:, k, :],
                                       start=(k == 0), stop=(k == KT - 1))
                    mm.then_inc(g.mm.sem, 1)

                chunk(0)
                chunk(1)
                if not last:
                    transpose_x(i + (j + 1) // 2, (j + 1) % 2)
                chunk(2)
                chunk(3)
                pe.wait_ge(g.mo.sem, g.mo.at(layer, 7 * t + 4))
                for n, (a, b) in enumerate(((0, 128), (128, 192), (192, 320))):
                    mm = pe.transpose(bk[5][0:b - a, n * P:(n + 1) * P], lat[j][:, a:b], s.ident[:, :])
                mm.then_inc(g.lT.sem, 1)
                chunk(4)
                chunk(5)
                pe.wait_ge(g.lo.sem, g.lo.at(layer, 3 * t + 3))
                pe.wait_ge(g.wl.sem, layer * 48 + 48)
                pe.wait_ge(g.ao.sem, g.ao.at(layer, 4 * t + 1))
                pe.matmul(bk[6][:, 0:GW], latT[j][:, 0, :], w_l[:, 0:GW], start=True, stop=False)
                pe.matmul(bk[6][:, 0:GW], latT[j][0:64, 1, :], w_l[0:64, GW:2 * GW], start=False, stop=True)
                pe.matmul(bk[7][:, 0:384], latT[j][:, 2, :], w_l[:, 2 * GW:2 * GW + 384],
                          start=True, stop=True).then_inc(g.am.sem, 1)

            pe.wait_ge(s.start_loads.sem, START_LOADS)
            transpose_x(0, 0)
            with pe.Fori(0, NT // 2 - 1) as i:
                tile(i, 0, False)
                tile(i, 1, False)
            tile(NT // 2 - 1, 0, False)
            tile(NT // 2 - 1, 1, True)

        @block.scalar
        def _(act):
            act.wait_ge(g.small.sem, g.small.at(layer, g.small.per_pass))

            def square_x(i, j):
                t = 2 * i + j
                act.wait_ge(g.x[j].sem, g.x[j].at(layer, 16 * (i + 1)))
                nc.scalar.activation(uT_flat[j], x_t[j], ACT.Square, scale=D ** -0.5,
                                     accum_out=s.rx[:, j, 0:1]).then_inc(g.x_sq.sem, 1)
                act.wait_ge(g.x_sq.sem, g.x_sq.at(layer, t + 1))
                nc.scalar.activation(s.rx[:, j, 1:2], s.rx[:, j, 0:1], ACT.Sqrt,
                                     bias=s.eps[:, 0:1]).then_inc(g.x_rt.sem, 1)

            def tile(i, j, last):
                t = 2 * i + j

                def evac(c):
                    n = 6 * j + c
                    b = n % 3
                    act.wait_ge(g.mm.sem, g.mm.at(layer, 6 * t + c + 1))
                    if c == 0:
                        act.wait_ge(g.x_r.sem, g.x_r.at(layer, t + 1))
                        dst = lat[j]
                    elif c < 3:
                        dst = pm[1][:, t, (c - 1) * 384:c * 384]
                    elif c < 5:
                        dst = pm[2][:, t, (c - 3) * 384:(c - 2) * 384]
                    else:
                        dst = pm[3][:, t, :]
                    if c == 4:
                        nc.scalar.activation(s.fg[:, t, :], bk[b][:, 384:388], ACT.Copy,
                                             scale=s.rx[:, j, 2:3]).then_inc(g.mo.sem, 1)
                    nc.scalar.activation(dst, bk[b][:, 0:(384 if c == 4 else CHUNKS[c])], ACT.Copy,
                                         scale=s.rx[:, j, 2:3]).then_inc(g.mo.sem, 1)

                evac(0)
                act.wait_ge(g.mo.sem, g.mo.at(layer, 7 * t + 4))
                nc.scalar.activation(latT_flat[j][:, 0:192], lat[j][:, 0:192], ACT.Square, scale=192 ** -0.5,
                                     accum_out=s.rl[:, j, 0, 0:1]).then_inc(g.l_sq.sem, 1)
                nc.scalar.activation(latT_flat[j][:, 192:320], lat[j][:, 192:320], ACT.Square, scale=128 ** -0.5,
                                     accum_out=s.rl[:, j, 0, 1:2]).then_inc(g.l_sq.sem, 1)
                act.wait_ge(g.l_sq.sem, g.l_sq.at(layer, 2 * t + 2))
                nc.scalar.activation(s.rl[:, j, 1, :], s.rl[:, j, 0, :], ACT.Sqrt,
                                     bias=s.eps[:, 0:1]).then_inc(g.l_rt.sem, 1)
                evac(1)
                if not last:
                    square_x(i + (j + 1) // 2, (j + 1) % 2)
                evac(2)
                evac(3)
                act.wait_ge(g.lT.sem, g.lT.at(layer, t + 1))
                for n in range(3):
                    q = 64 if n == 1 else P
                    nc.scalar.activation(latT[j][0:q, n, :], bk[5][0:q, n * P:(n + 1) * P], ACT.Copy,
                                         scale=s.gain_lat[0:q, n:n + 1]).then_inc(g.lo.sem, 1)
                evac(4)
                evac(5)

            act.wait_ge(s.start_loads.sem, START_LOADS)
            nc.scalar.activation(s.junk[:, 1:2], s.eps[:, 0:1], ACT.Copy).then_inc(g.mo.sem, 3)
            square_x(0, 0)
            with act.Fori(0, NT // 2 - 1) as i:
                tile(i, 0, False)
                tile(i, 1, False)
            tile(NT // 2 - 1, 0, False)
            tile(NT // 2 - 1, 1, True)

        @block.vector
        def _(dve):
            dve.wait_ge(s.start_loads.sem, START_LOADS)
            dve.wait_ge(g.small.sem, g.small.at(layer, g.small.per_pass))
            nc.vector.tensor_scalar(s.gain_qk[0:HD, 0:MIXERS], s.gain_raw[0:HD, 0:MIXERS], HD ** -0.5, None,
                                    ALU.mult)
            nc.vector.tensor_copy(s.gain_qk[0:HD, MIXERS:2 * MIXERS],
                                  s.gain_raw[0:HD, MIXERS:2 * MIXERS]).then_inc(g.gq.sem, 1)
            nc.vector.memset(s.junk[:, 0:1], 0.0).then_inc(g.red.sem, 1)
            nc.vector.memset(s.junk[:, 2:3], 0.0).then_inc(g.ao.sem, 1)

            def evac_x(i, j):
                t = 2 * i + j
                dve.wait_ge(g.x_rt.sem, g.x_rt.at(layer, t + 1))
                nc.vector.reciprocal(s.rx[:, j, 2:3], s.rx[:, j, 1:2]).then_inc(g.x_r.sem, 1)
                dve.wait_ge(g.xT.sem, g.xT.at(layer, t + 1))
                for half in range(2):
                    nc.vector.tensor_tensor(
                        uT[j][:, 4 * half:4 * half + 4, :], bk[3 + half][:, :].rearrange("p (k n) -> p k n", k=4),
                        bcast(s.gain1[:, 4 * half:4 * half + 4].unsqueeze(2), [P, 4, P]),
                        ALU.mult).then_inc(g.uT.sem, 1)

            def tile(i, j, last):
                t = 2 * i + j
                if not last:
                    evac_x(i + (j + 1) // 2, (j + 1) % 2)
                dve.wait_ge(g.l_rt.sem, g.l_rt.at(layer, t + 1))
                nc.vector.reciprocal(s.rl[:, j, 2, :], s.rl[:, j, 1, :]).then_inc(g.l_r.sem, 1)
                pa = pm[0][:, t, :]
                kva = bk[7][:, 0:384].rearrange("p (h c) -> p h c", h=HEADS)
                ka = pa[:, GW:2 * GW].rearrange("p (h c) -> p h c", h=HEADS)
                dve.wait_ge(g.am.sem, g.am.at(layer, t + 1))
                dve.wait_ge(g.l_r.sem, g.l_r.at(layer, t + 1))
                nc.vector.tensor_scalar(pa[:, 0:GW], bk[6][:, 0:GW], s.rl[:, j, 2, 0:1], None,
                                        ALU.mult).then_inc(g.ao.sem, 1)
                nc.vector.tensor_scalar(ka[:, :, 0:NNOPE], kva[:, :, 0:NNOPE], s.rl[:, j, 2, 1:2], None,
                                        ALU.mult).then_inc(g.ao.sem, 1)
                nc.vector.tensor_scalar(pa[:, 2 * GW:3 * GW].rearrange("p (h c) -> p h c", h=HEADS),
                                        kva[:, :, NNOPE:NNOPE + HD], s.rl[:, j, 2, 1:2], None,
                                        ALU.mult).then_inc(g.ao.sem, 1)
                nc.vector.tensor_tensor(ka[:, :, NNOPE:HD],
                                        bcast(lat[j][:, 320:352].unsqueeze(1), [P, HEADS, NROPE]),
                                        bcast(s.ones[:, 0:NROPE].unsqueeze(1), [P, HEADS, NROPE]),
                                        ALU.mult).then_inc(g.ao.sem, 1)
                dve.wait_ge(g.sq.sem, g.sq.at(layer, 4 * t + 4))
                nc.vector.tensor_reduce(s.ssq[:, t, :], sqb.rearrange("p (h c) -> p h c", c=HD), AX.X,
                                        ALU.add).then_inc(g.red.sem, 1)

            evac_x(0, 0)
            with dve.Fori(0, NT // 2 - 1) as i:
                tile(i, 0, False)
                tile(i, 1, False)
            tile(NT // 2 - 1, 0, False)
            tile(NT // 2 - 1, 1, True)

        @block.gpsimd
        def _(pool):
            wait_alone(pool, s, s.start_loads.sem, START_LOADS)
            wait_alone(pool, s, g.small.sem, g.small.at(layer, g.small.per_pass))

            def tile(i, j):
                t = 2 * i + j
                wait_alone(pool, s, g.red.sem, g.red.at(layer, t + 1))
                wait_alone(pool, s, g.ao.sem, g.ao.at(layer, 4 * t + 5))
                qk = pm[0][:, t, 0:2 * GW]
                nc.gpsimd.tensor_tensor(sqb[:, 0:512], qk, qk, ALU.mult).then_inc(g.sq.sem, 1)
                wait_alone(pool, s, g.sq.sem, g.sq.at(layer, 4 * t + 1))
                nc.gpsimd.tensor_tensor(qk, qk, s.gain_a[:, :, :].rearrange("p h c -> p (h c)"),
                                        ALU.mult).then_inc(g.rope.sem, 1)
                hv = qk.rearrange("p (h c) -> p h c", c=HD)
                x1, x2 = hv[:, :, 32:48], hv[:, :, 48:64]
                co = bcast(s.cos_sin[:, 0, t, :].unsqueeze(1), [P, 8, 16])
                si = bcast(s.cos_sin[:, 1, t, :].unsqueeze(1), [P, 8, 16])
                wait_alone(pool, s, g.rope.sem, g.rope.at(layer, 7 * t + 1))
                for a, (u, v) in enumerate(((x1, co), (x2, si), (x2, co), (x1, si))):
                    nc.gpsimd.tensor_tensor(rot[:, a], u, v, ALU.mult).then_inc(g.rope.sem, 1)
                wait_alone(pool, s, g.rope.sem, g.rope.at(layer, 7 * t + 5))
                nc.gpsimd.tensor_tensor(x1, rot[:, 0], rot[:, 1], ALU.subtract).then_inc(g.rope.sem, 1)
                nc.gpsimd.tensor_tensor(x2, rot[:, 2], rot[:, 3], ALU.add).then_inc(g.rope.sem, 1)
                for m, reads in ((1, 3), (2, 6), (3, 7)):
                    w = 512 if m < 3 else 384
                    wait_alone(pool, s, g.mo.sem, g.mo.at(layer, 7 * t + reads + 3))
                    pq = pm[m][:, t, 0:w]
                    nc.gpsimd.tensor_tensor(sqb[:, 512 * m:512 * m + w], pq, pq, ALU.mult).then_inc(g.sq.sem, 1)

            with pool.Fori(0, NT // 2) as i:
                tile(i, 0)
                tile(i, 1)

    with nc.Block() as block:
        blockfn(block)


PAIRS = MIXERS * HEADS // 2
AHEAD, AHEAD_WINDOW = 2, 3
RING = 3


def key_span(m, qb):
    k0 = max(0, qb - 1) * P if m == 3 else 0
    return k0, (qb + 1) * P - k0


def head_at(pair, k, nt):
    return (k + (k >= nt) + pair) % 2


class Step:

    def __init__(self, i, nt):
        self.i = i
        self.pair, k = i // (2 * nt), i % (2 * nt)
        self.k = k
        self.m = self.pair // 2
        self.j = head_at(self.pair, k, nt)
        self.qb = k // 2 if (k % 2 == 0) == (k < nt) else nt - 1 - k // 2
        self.head = 2 * (self.pair % 2) + self.j
        self.slot = self.head
        self.k0, self.nk = key_span(self.m, self.qb)
        self.window = self.m == 3
        if self.window:
            self.bank, self.at = i % 3, 256 * (i % 12)
        elif k % 2:
            self.bank, self.at = 0, 1024 * (i // 2 % 2)
        else:
            self.bank, self.at = 2, 2048 + 512 * (i // 2 % 2)
        self.blocks = [(c, min(512, self.nk - c)) for c in range(0, self.nk, 512)]


def plan_steps(nt):
    steps = [Step(i, nt) for i in range(2 * nt * PAIRS)]
    issued, upto = [], 0
    for st in steps:
        ahead = AHEAD_WINDOW if st.window else AHEAD
        end = min(len(steps), st.i + ahead + 1)
        issued.append(list(range(upto, end)))
        upto = max(upto, end)
    return steps, issued


def qk_group(st):
    return st.k - 4 if st.pair + 1 < PAIRS and 4 <= st.k < 12 else None


def mix_half(st):
    return st.k - 2 if st.pair > 0 and st.k in (2, 3) else None


def plan_ring(steps):
    ring = [("qk", (0, q)) for q in range(8)]
    for st in steps:
        if mix_half(st) is not None:
            ring.append(("mix", (st.pair - 1, mix_half(st))))
        if qk_group(st) is not None:
            ring.append(("qk", (st.pair + 1, qk_group(st))))
        ring += [("w2" if c else "w", st.i) for c, _ in st.blocks]
    ring += [("mix", (PAIRS - 1, half)) for half in range(2)]
    return ring


def attend_signals(s):
    sig = s.counted
    NT = s.NT
    steps, _ = plan_steps(NT)
    n = len(steps)
    groups = sum(len(st.blocks) for st in steps)
    g = Shared()
    g.rt = sig("head_roots_taken", 1)
    g.rsr = sig("head_scales_ready", 1)
    g.fxd = sig("fox_vector_steps", 3)
    g.fxa = sig("fox_scalar_steps", 3)
    g.fxp = sig("fox_summed", 1)
    g.fxo = sig("fox_cumulated", 2)
    g.causal = sig("causal_table_loaded", 16)
    g.bias = [sig(f"bias_table_loaded{j}", 16 * 4) for j in range(2)]
    g.wo = sig("w_o_loaded", 16)
    g.stage = sig("heads_scaled", 2 * HEADS * MIXERS + 2 * HEADS)
    g.qkt = sig("qk_transposed", 8 * PAIRS)
    g.qko = sig("qkT_ready", 8 * PAIRS)
    g.lg = sig("logits_done", n)
    g.mx = sig("logits_biased", n)
    g.ng = sig("negmax_ready", n)
    g.ex = sig("weights_ready", n)
    g.pt = sig("weights_transposed", groups)
    g.po = sig("weightsT_ready", n)
    g.pd = sig("weightsT_second_ready", groups - n)
    g.pv = sig("values_summed", n)
    g.sk = sig("sink_terms_ready", HEADS)
    g.dn = sig("denominators_ready", HEADS * (MIXERS + 1))
    g.on = sig("heads_normalised", HEADS * MIXERS)
    g.ot = sig("mix_transposed", 2 * PAIRS)
    g.oo = sig("mixT_ready", 2 * PAIRS)
    return g


def attend(nc, s, g, layer):
    NT, SEQ = s.NT, s.SEQ
    bk, pm = s.banks, s.pm
    w = s.r_win
    steps, issued = plan_steps(NT)
    ring = plan_ring(steps)
    ring_at = {name: n for n, name in enumerate(ring)}
    kinds = [kind for kind, _ in ring]

    def cut(at, n, count):
        return [w[:, at + j * n:at + (j + 1) * n] for j in range(count)]

    qs = [a.rearrange("p (t c) -> p t c", c=AUG) for a in cut(0, 528, 2)]
    ks = [a.rearrange("p (t c) -> p t c", c=AUG) for a in cut(1056, 528, 2)]
    qT, kT = cut(2112, 1024, 4), cut(6208, 1024, 4)
    weights = w[:, 10304:13376]
    pT = cut(13376, 1024, 2)
    bias = cut(15424, 1024, 2)
    o_s = w[:, 17472:18496].rearrange("p (t c) -> p t c", c=P)
    negmax, den, sinkexp, rden = (
        w[:, 18496 + 32 * n:18528 + 32 * n].rearrange("p (a b) -> p a b", a=HEADS) for n in range(4))
    causal = s.w_lat[:, 0:SEQ]
    mixT = s.r_tile[:, :].rearrange("p (t k n) -> p k t n", t=NT, k=8)
    s.w_o = s.r_proj[:, 0:8192].rearrange("p (k n) -> p k n", k=8)
    neg_cum, pos_cum = s.cum[:, 1], s.cum[:, 0]

    def stages_done(pair, j):
        n = 2 * pair + j + 1
        return 2 * n + 2 * min(max(n - 2 * HEADS, 0), HEADS)

    def table(st):
        if st.window:
            return bias[st.j][:, 2 * P - st.nk:2 * P]
        return (bias[st.j] if st.m == 1 else causal)[:, SEQ - st.nk:SEQ]

    def last_group(st):
        return sum(len(x.blocks) for x in steps[:st.i + 1])

    def seconds(st):
        return last_group(st) - st.i - 1

    def ring_bank(name):
        return 3 + ring_at[name] % RING

    with nc.Block() as block:
        @block.sync
        def _(sp):
            sp.dma_start(causal, s.consts["causal"]).then_inc(g.causal.sem, 16)
            for m in (1, 3):
                if m == 3:
                    sp.wait_ge(g.on.sem, g.on.at(layer, 2 * HEADS))
                    sp.dma_start(s.w_o, s.ins["w_o"][layer].rearrange("(k p) n -> p k n", p=P)).then_inc(g.wo.sem, 16)
                for h in range(HEADS):
                    if h >= 2 or m == 3:
                        pair = 2 * m + h // 2
                        sp.wait_ge(g.mx.sem, g.mx.at(layer, 2 * NT * pair))
                    src, n = (s.consts["dilated"][h], SEQ) if m == 1 else (s.consts["window"][h], 2 * P)
                    sp.dma_start(bias[h % 2][:, 0:n], src).then_inc(g.bias[h % 2].sem, 16)

        @block.tensor
        def _(pe):
            def bank_for(name):
                n = ring_at[name]
                if n >= RING:
                    kind = kinds[n - RING]
                    sem = {"qk": g.qko, "w": g.po, "w2": g.pd, "mix": g.oo}[kind]
                    wait_alone(pe, s, sem.sem, sem.at(layer, kinds[:n - RING + 1].count(kind)))
                return bk[ring_bank(name)]

            def transpose_heads(pair, q):
                j, a, half = q // 4, q // 2 % 2, q % 2
                K = AUG if pair // 2 == 2 else HD
                wait_alone(pe, s, g.stage.sem, g.stage.at(layer, stages_done(pair, j)))
                bank = bank_for(("qk", (pair, q)))
                for t in range(4):
                    mm = pe.transpose(bank[0:K, t * P:(t + 1) * P], (qs, ks)[a][j][:, 4 * half + t, 0:K],
                                      s.ident[:, :])
                mm.then_inc(g.qkt.sem, 1)

            def transpose_mix(pair, half):
                pe.wait_ge(g.on.sem, g.on.at(layer, 2 * pair + 2))
                bank = bank_for(("mix", (pair, half)))
                for t in range(4):
                    mm = pe.transpose(bank[:, t * P:(t + 1) * P], o_s[:, 4 * half + t, :], s.ident[:, :])
                mm.then_inc(g.ot.sem, 1)

            def logits(st):
                K = AUG if st.m == 2 else HD
                pe.wait_ge(g.qko.sem, g.qko.at(layer, 8 * st.pair + 4 * st.j + 4))
                used = {st.bank + c // 512 for c, _ in st.blocks}
                before = [x.i for x in steps[:st.i] if used & {x.bank + c // 512 for c, _ in x.blocks}]
                if before:
                    pe.wait_ge(g.mx.sem, g.mx.at(layer, before[-1] + 1))
                q = 2 * (st.pair % 2) + st.j
                for c, cw in st.blocks:
                    mm = pe.matmul(bk[st.bank + c // 512][:, 0:cw], qT[q][0:K, st.qb * P:(st.qb + 1) * P],
                                   kT[q][0:K, st.k0 + c:st.k0 + c + cw], start=True, stop=True)
                mm.then_inc(g.lg.sem, 1)

            def transpose_weights(st):
                pe.wait_ge(g.ex.sem, g.ex.at(layer, st.i + 1))
                for c, cw in st.blocks:
                    bank = bank_for(("w2" if c else "w", st.i))
                    for b in range(0, cw, P):
                        at = st.at + c + b
                        mm = pe.transpose(bank[:, b:b + P], weights[:, at:at + P], s.ident[:, :])
                    mm.then_inc(g.pt.sem, 1)

            def values(st):
                pe.wait_ge(g.po.sem, g.po.at(layer, st.i + 1))
                if st.pair > 0 and st.k < 2:
                    pe.wait_ge(g.on.sem, g.on.at(layer, 2 * st.pair - 1 + st.k))
                v0 = 384 + HD * (st.head // 2) if st.window else 2 * GW + HD * st.head
                for b in range(0, st.nk, P):
                    if b == 512:
                        pe.wait_ge(g.pd.sem, g.pd.at(layer, seconds(st)))
                    mm = pe.matmul(bk[6 + st.j][:, st.qb * HD:(st.qb + 1) * HD], pT[st.i % 2][:, b:b + P],
                                   pm[st.m][:, (st.k0 + b) // P, v0:v0 + HD], start=(b == 0),
                                   stop=(b == st.nk - P))
                mm.then_inc(g.pv.sem, 1)

            for q in range(4):
                transpose_heads(0, q)
            logits(steps[0])
            for q in range(4, 8):
                transpose_heads(0, q)
            logits(steps[1])
            pe.wait_ge(g.fxd.sem, g.fxd.at(layer, 3))
            ls = s.fox[:, 3]
            pe.matmul(bk[6][:, 0:NT * HEADS], s.upto[:, :], ls.rearrange("p t h -> p (t h)"),
                      start=True, stop=False)
            for t in range(NT - 1):
                left = NT - 1 - t
                mm = pe.matmul(bk[6][:, (t + 1) * HEADS:NT * HEADS], s.ones[:, :],
                               bcast(ls[:, t:t + 1, :], [P, left, HEADS]),
                               start=False, stop=(t == NT - 2))
            mm.then_inc(g.fxp.sem, 1)
            logits(steps[2])
            pe.wait_ge(g.fxo.sem, g.fxo.at(layer, 2))
            for st in steps:
                for i in issued[st.i]:
                    if i > 2:
                        logits(steps[i])
                if mix_half(st) is not None:
                    transpose_mix(st.pair - 1, mix_half(st))
                if qk_group(st) is not None:
                    transpose_heads(st.pair + 1, qk_group(st))
                transpose_weights(st)
                if st.i > 0:
                    values(steps[st.i - 1])
            values(steps[-1])
            for half in range(2):
                transpose_mix(PAIRS - 1, half)

        @block.scalar
        def _(act):
            nc.scalar.activation(s.rs[:, :, :], s.ssq[:, :, :], ACT.Sqrt, scale=1.0 / HD,
                                 bias=s.eps[:, 0:1]).then_inc(g.rt.sem, 1)
            act.wait_ge(g.fxd.sem, g.fxd.at(layer, 1))
            nc.scalar.activation(s.fox[:, 1], s.fox[:, 0], ACT.Abs).then_inc(g.fxa.sem, 1)
            act.wait_ge(g.fxa.sem, g.fxa.at(layer, 1))
            nc.scalar.activation(s.fox[:, 1], s.fox[:, 1], ACT.Exp, scale=-1.0).then_inc(g.fxa.sem, 1)
            act.wait_ge(g.fxa.sem, g.fxa.at(layer, 2))
            nc.scalar.activation(s.fox[:, 2], s.fox[:, 1], ACT.Ln, bias=s.ones[:, 0:1]).then_inc(g.fxa.sem, 1)

            def exponentials(st):
                act.wait_ge(g.ng.sem, g.ng.at(layer, st.i + 1))
                x = weights[:, st.at:st.at + st.nk]
                nc.scalar.activation(x, x, ACT.Exp, bias=negmax[:, st.slot, st.qb:st.qb + 1],
                                     accum_out=den[:, st.slot, st.qb:st.qb + 1]).then_inc(g.ex.sem, 1)

            for i in issued[0]:
                exponentials(steps[i])
            for st in steps:
                n = st.blocks[0][1]
                act.wait_ge(g.pt.sem, g.pt.at(layer, last_group(st) - len(st.blocks) + 1))
                nc.scalar.activation(pT[st.i % 2][:, 0:n], bk[ring_bank(("w", st.i))][:, 0:n],
                                     ACT.Copy).then_inc(g.po.sem, 1)
                if st.i > 0:
                    for i in issued[st.i]:
                        exponentials(steps[i])
                if st.window and st.k >= 2 * NT - 2:
                    nc.scalar.activation(sinkexp[:, st.slot, :], negmax[:, st.slot, :], ACT.Exp,
                                         bias=s.sink_b[:, st.head:st.head + 1]).then_inc(g.sk.sem, 1)

        @block.vector
        def _(dve):
            for j in range(2):
                nc.vector.memset(qs[j][:, :, HD:HD + 1], 1.0)
                nc.vector.memset(ks[j][:, :, HD + 1:HD + 2], 1.0)
            nc.vector.tensor_tensor(s.fox[:, 0], s.fg[:, :, :], bcast(s.fox_b[:, :].unsqueeze(1), [P, NT, HEADS]),
                                    ALU.add).then_inc(g.fxd.sem, 1)
            def scale_head(pair, j):
                m, h = pair // 2, 2 * (pair % 2) + j
                kv = pair % 2 if m == 3 else h
                for dst, col, r in ((qs[j], HD * h, 8 * m + h), (ks[j], GW + HD * kv, 8 * m + HEADS + kv)):
                    nc.vector.tensor_tensor(dst[:, :, 0:HD], pm[m][:, :, col:col + HD],
                                            bcast(s.rs[:, :, r:r + 1], [P, NT, HD]),
                                            ALU.mult).then_inc(g.stage.sem, 1)
                if m == 2:
                    nc.vector.tensor_copy(ks[j][:, :, HD:HD + 1], neg_cum[:, :, h:h + 1]).then_inc(g.stage.sem, 1)
                    nc.vector.tensor_copy(qs[j][:, :, HD + 1:AUG], pos_cum[:, :, h:h + 1]).then_inc(
                        g.stage.sem, 1)

            def evac_heads(pair, q):
                j, a, half = q // 4, q // 2 % 2, q % 2
                m = pair // 2
                K = AUG if m == 2 else HD
                dve.wait_ge(g.qkt.sem, g.qkt.at(layer, 8 * pair + q + 1))
                nc.vector.tensor_scalar(
                    (qT, kT)[a][2 * (pair % 2) + j][0:K, 512 * half:512 * half + 512],
                    bk[ring_bank(("qk", (pair, q)))][0:K, :],
                    s.gain_qk[0:K, MIXERS * a + m:MIXERS * a + m + 1], None, ALU.mult).then_inc(g.qko.sem, 1)

            def bias_and_max(st):
                if st.k < 2 and st.m in (1, 3):
                    dve.wait_ge(g.bias[st.j].sem,
                                g.bias[st.j].at(layer, 16 * (st.pair % 2 + 1) + (32 if st.window else 0)))
                wait_alone(dve, s, g.lg.sem, g.lg.at(layer, st.i + 1))
                behind = [x.i for x in steps[:st.i] if x.at < st.at + st.nk and st.at < x.at + x.nk]
                ahead_of = [x for x in range(len(steps)) if st.i in issued[x]][0]
                if behind and behind[-1] >= ahead_of:
                    wait_alone(dve, s, g.pt.sem, g.pt.at(layer, last_group(steps[behind[-1]])))
                col = 512 * (st.bank % 2)
                banks = s.bank_pairs[st.bank // 2][:, col:col + st.nk]
                nc.vector.tensor_tensor_reduce(out=weights[:, st.at:st.at + st.nk], in0=banks, in1=table(st),
                                               scale=1.0, scalar=-3e38, op0=ALU.add, op1=ALU.max,
                                               accum_out=s.rowmax[:, st.i % 2:st.i % 2 + 1]).then_inc(g.mx.sem, 1)
                dve.wait_ge(g.mx.sem, g.mx.at(layer, st.i + 1))
                floor = s.sink_b[:, st.head:st.head + 1] if st.window else s.never[:, 0:1]
                nc.vector.tensor_scalar(negmax[:, st.slot, st.qb:st.qb + 1], s.rowmax[:, st.i % 2:st.i % 2 + 1],
                                        floor, -1.0, ALU.max, ALU.mult).then_inc(g.ng.sem, 1)

            def second_group(st):
                c, cw = st.blocks[1]
                dve.wait_ge(g.pt.sem, g.pt.at(layer, last_group(st)))
                nc.vector.tensor_copy(pT[st.i % 2][:, c:c + cw],
                                      bk[ring_bank(("w2", st.i))][:, 0:cw]).then_inc(g.pd.sem, 1)

            def normalise(pair, turn):
                j = head_at(pair, 2 * NT - 2 + turn, NT)
                m, h = pair // 2, 2 * (pair % 2) + j
                slot = h
                dve.wait_ge(g.pv.sem, g.pv.at(layer, 2 * NT * (pair + 1) - 1 + turn))
                if m == 3:
                    dve.wait_ge(g.sk.sem, g.sk.at(layer, 2 * (pair % 2) + turn + 1))
                    nc.vector.tensor_tensor(den[:, slot, :], den[:, slot, :], sinkexp[:, slot, :],
                                            ALU.add).then_inc(g.dn.sem, 1)
                    dve.wait_ge(g.dn.sem, g.dn.at(layer, dn_done(pair, turn) - 1))
                nc.vector.reciprocal(rden[:, slot, :], den[:, slot, :]).then_inc(g.dn.sem, 1)
                dve.wait_ge(g.dn.sem, g.dn.at(layer, dn_done(pair, turn)))
                nc.vector.tensor_tensor(o_s[:, :, HD * j:HD * (j + 1)],
                                        bk[6 + j][:, :].rearrange("p (t c) -> p t c", c=HD),
                                        bcast(rden[:, slot, :].unsqueeze(2), [P, NT, HD]),
                                        ALU.mult).then_inc(g.on.sem, 1)

            def evac_mix(pair, half):
                dve.wait_ge(g.ot.sem, g.ot.at(layer, 2 * pair + half + 1))
                nc.vector.tensor_copy(mixT[:, pair, 4 * half:4 * half + 4, :],
                                      bk[ring_bank(("mix", (pair, half)))].rearrange("p (t n) -> p t n", n=P)).then_inc(g.oo.sem, 1)

            dve.wait_ge(g.rt.sem, g.rt.at(layer, 1))
            nc.vector.reciprocal(s.rs[:, :, :], s.rs[:, :, :]).then_inc(g.rsr.sem, 1)
            dve.wait_ge(g.rsr.sem, g.rsr.at(layer, 1))
            scale_head(0, 0)
            scale_head(0, 1)
            for q in range(4):
                evac_heads(0, q)
            dve.wait_ge(g.causal.sem, g.causal.at(layer, 16))
            bias_and_max(steps[0])
            for q in range(4, 8):
                evac_heads(0, q)
            bias_and_max(steps[1])
            dve.wait_ge(g.fxa.sem, g.fxa.at(layer, 3))
            dve.wait_ge(g.fxd.sem, g.fxd.at(layer, 1))
            nc.vector.tensor_scalar(s.fox[:, 3], s.fox[:, 0], 0.0, None, ALU.min).then_inc(g.fxd.sem, 1)
            dve.wait_ge(g.fxd.sem, g.fxd.at(layer, 2))
            nc.vector.tensor_tensor(s.fox[:, 3], s.fox[:, 3], s.fox[:, 2], ALU.subtract).then_inc(g.fxd.sem, 1)
            dve.wait_ge(g.fxp.sem, g.fxp.at(layer, 1))
            flat = bk[6][:, 0:NT * HEADS].rearrange("p (t h) -> p t h", h=HEADS)
            nc.vector.tensor_copy(pos_cum, flat).then_inc(g.fxo.sem, 1)
            nc.vector.tensor_scalar(neg_cum, flat, -1.0, None, ALU.mult).then_inc(g.fxo.sem, 1)
            bias_and_max(steps[2])
            dve.wait_ge(g.fxo.sem, g.fxo.at(layer, 2))
            for st in steps:
                for i in issued[st.i]:
                    if i > 2:
                        bias_and_max(steps[i])
                if mix_half(st) is not None:
                    evac_mix(st.pair - 1, mix_half(st))
                if qk_group(st) is not None:
                    evac_heads(st.pair + 1, qk_group(st))
                if len(st.blocks) > 1:
                    second_group(st)
                if st.pair + 1 < PAIRS and st.k in (1, 3):
                    scale_head(st.pair + 1, st.k // 2)
                if st.k == 2 * NT - 1:
                    normalise(st.pair, 0)
                if st.pair > 0 and st.k == 0:
                    normalise(st.pair - 1, 1)
            normalise(PAIRS - 1, 1)
            for half in range(2):
                evac_mix(PAIRS - 1, half)


def dn_done(pair, turn):
    n = 2 * pair + turn + 1
    return n + max(n - 3 * HEADS, 0)


def over_pairs(eng, n, body, peeled=1):
    for i in range(peeled):
        body(i)
    with eng.Fori(peeled, n - 1) as i:
        body(i)
    body(n - 1)


def first(i):
    return isinstance(i, int) and i == 0


CHOICE_STEPS, PLACE_STEPS, GATE_STEPS = 12, 5, 11


def out_signals(s):
    sig = s.counted
    NT = s.NT
    half = 16 * NT // 2
    g = Shared()
    g.wr = sig("router_weights_loaded", 32)
    g.x = [sig(f"residual_loaded{j}", half) for j in range(2)]
    g.xs = [sig(f"normed_stored{j}", half) for j in range(2)]
    g.mt = sig("mix_tile_ready", NT)
    g.wo = sig("output_projected", NT)
    g.h = sig("h_ready", NT)
    g.sq = sig("h_squares_summed", NT)
    g.rt = sig("h_root_taken", NT)
    g.r = sig("h_scale_ready", NT)
    g.xn = sig("normed_ready", NT)
    g.xt = sig("normed_transposed", NT)
    g.xo = sig("normedT_ready", 2 * NT)
    g.lm = sig("router_logits_done", NT)
    g.lo = sig("router_logits_out", 2 * NT)
    g.ch = sig("tile_choice_steps", CHOICE_STEPS * NT)
    g.ps = sig("pairs_counted", NT)
    g.pl = sig("tile_place_steps", PLACE_STEPS * NT)
    g.ct = sig("experts_counted", 1)
    g.sc = sig("slots_scattered", 32 * NT)
    g.v = sig("gate_steps", GATE_STEPS)
    g.e = sig("gate_exps", 2)
    return g


def out_route(nc, s, g, layer):
    NT, KT, D, R, NG = s.NT, s.KT, s.D, s.R, s.NG
    bk, pairs, ins = s.banks, s.bank_pairs, s.ins
    w = s.r_proj

    def pair_of(at, n):
        return [w[:, at + j * n:at + (j + 1) * n] for j in range(2)]

    mt_flat = pair_of(8192, 1024)
    mt = [a.rearrange("p (k n) -> p k n", k=KT) for a in mt_flat]
    x_t, xn_t = pair_of(10240, 1024), pair_of(14336, 1024)
    xnT = [a.rearrange("p (k n) -> p k n", k=KT) for a in pair_of(16384, 1024)]
    w_r = w[:, 18432:18432 + KT * R].rearrange("p (k n) -> p k n", k=KT)
    lg = w[:, 18720:18720 + NT * R].rearrange("p (t n) -> p t n", t=NT)
    NP = NT // 2
    at = [18720 + NT * R]

    def take(n, dt=F32):
        at[0] += NT * n
        return w[:, at[0] - NT * n:at[0]].bitcast(dt).rearrange("p (t n) -> p t n", t=NT)

    s.gl, s.gm, s.em, s.gi, s.ei = take(8), take(8), take(8), take(8, U32), take(8, U32)
    masked, other, gif = take(s.E), take(NG), take(1)
    eif, prod, slf, s.slots = take(2), take(2 * s.E), take(2), take(2, I32)
    masks = [a.rearrange("p (k e) -> p k e", k=2) for a in pair_of(at[0], 2 * s.E)]
    both, upto_now = pair_of(at[0] + 4 * s.E, s.E), pair_of(at[0] + 6 * s.E, s.E)
    at[0] += 8 * s.E
    dg, eg, pg, d, ed, den = take(NG), take(NG), take(1), take(1), take(1), take(1)
    cnt, cnti = w[0:1, at[0]:at[0] + 1], w[0:1, at[0] + 1:at[0] + 2].bitcast(I32)

    def h_of(i, j):
        return s.r_tile[:, bass.ds((2 * i + j) * D, D)]

    def rows(dram, i, j):
        return dram[bass.ds((2 * i + j) * P, P)]

    with nc.Block() as block:
        @block.sync
        def _(sp):
            sp.dma_start(w_r[:, :, 0:NG], ins["w_rg"][layer].rearrange("(p k) n -> p k n", k=KT)).then_inc(
                g.wr.sem, 16)
            sp.dma_start(w_r[:, :, NG:R], ins["w_re"][layer].rearrange("(p k) n -> p k n", k=KT)).then_inc(
                g.wr.sem, 16)

            def body(i):
                for j in range(2):
                    if not first(i):
                        sp.wait_ge(g.h.sem, g.h.at(layer, 2 * i + j - 1))
                    sp.dma_start(x_t[j], rows(s.out_f, i, j)).then_inc(g.x[j].sem, 16)
                if isinstance(i, int) and (i < 2 or i == NP - 1):
                    n = min(i, 2)
                    load_w_in(sp, s, s.project_sems, next_layer(sp, s, layer), range(2 * n, 2 * n + 2))
                for j in range(2):
                    t = 2 * i + j
                    sp.wait_ge(g.xn.sem, g.xn.at(layer, t + 1))
                    sp.dma_start(rows(s.xn_dram, i, j), xn_t[j]).then_inc(g.xs[j].sem, 16)

            over_pairs(sp, NP, body, 2)
            for j in range(2):
                wait_alone(sp, s, g.xs[j].sem, g.xs[j].at(layer, 16 * NP))

        @block.tensor
        def _(pe):
            def project_half(i, j, c):
                t = 2 * i + j
                if c == 0:
                    pe.wait_ge(g.mt.sem, g.mt.at(layer, t + 1))
                for k in range(KT):
                    mm = pe.matmul(bk[2 * j + c][:, :], mt[j][:, k, :], s.w_o[:, k, 512 * c:512 * c + 512],
                                   start=(k == 0), stop=(k == KT - 1))
                if c == 1:
                    mm.then_inc(g.wo.sem, 1)

            def count_pairs(i, j):
                t = 2 * i + j
                wait_alone(pe, s, g.ch.sem, g.ch.at(layer, CHOICE_STEPS * (t + 1)))
                pe.matmul(bk[7][:, 0:s.E], s.before[:, :], both[j], start=True, stop=False)
                pe.matmul(bk[7][:, 0:s.E], s.ones[:, :], upto_now[1 - j], start=False, stop=True).then_inc(
                    g.ps.sem, 1)

            def router_logits(i, j):
                t = 2 * i + j
                pe.wait_ge(g.xo.sem, g.xo.at(layer, 2 * t + 2))
                if first(i) and j == 0:
                    pe.wait_ge(g.wr.sem, g.wr.at(layer, 32))
                else:
                    pe.wait_ge(g.lo.sem, g.lo.at(layer, 2 * t))
                for k in range(KT):
                    mm = pe.matmul(bk[6][:, 0:R], xnT[j][:, k, :], w_r[:, k, :], start=(k == 0),
                                   stop=(k == KT - 1))
                mm.then_inc(g.lm.sem, 1)

            def transpose_normed(i, j):
                pe.wait_ge(g.xn.sem, g.xn.at(layer, 2 * i + j + 1))
                xs = xn_t[j].rearrange("p (q k) -> p k q", k=KT)
                for k in range(KT):
                    mm = pe.transpose(bk[4 + k // 4][:, (k % 4) * P:(k % 4 + 1) * P], xs[:, k, :], s.ident[:, :])
                mm.then_inc(g.xt.sem, 1)

            def body(i):
                for j in range(2):
                    if isinstance(i, int) and i == NP - 1 and j == 1:
                        router_logits(i, 0)
                        transpose_normed(i, 1)
                        count_pairs(i, 0)
                        router_logits(i, 1)
                        count_pairs(i, 1)
                        continue
                    project_half(i + j, 1 - j, 0)
                    if not (first(i) and j == 0):
                        router_logits(i - (1 - j), 1 - j)
                    project_half(i + j, 1 - j, 1)
                    if not (first(i) and j == 0):
                        count_pairs(i - (1 - j), 1 - j)
                    transpose_normed(i, j)

            s_wo = s.attend_sems.wo
            pe.wait_ge(s_wo.sem, s_wo.at(layer, 16))
            project_half(0, 0, 0)
            project_half(0, 0, 1)
            over_pairs(pe, NP, body, 2)
            pe.matmul(bk[1][:, 0:s.E], s.ones[:, :], upto_now[1], start=True, stop=True).then_inc(g.ct.sem, 1)

        @block.scalar
        def _(act):
            def body(i):
                for j in range(2):
                    t = 2 * i + j
                    wait_alone(act, s, g.h.sem, g.h.at(layer, t + 1))
                    if not first(i):
                        wait_alone(act, s, g.xs[j].sem, g.xs[j].at(layer, 16 * i))
                    nc.scalar.activation(xn_t[j], h_of(i, j), ACT.Square, scale=D ** -0.5,
                                         accum_out=s.rx[:, j, 0:1]).then_inc(g.sq.sem, 1)
                    act.wait_ge(g.sq.sem, g.sq.at(layer, t + 1))
                    nc.scalar.activation(s.rx[:, j, 1:2], s.rx[:, j, 0:1], ACT.Sqrt,
                                         bias=s.eps[:, 0:1]).then_inc(g.rt.sem, 1)
                    wait_alone(act, s, g.r.sem, g.r.at(layer, t + 1))
                    nc.scalar.activation(xn_t[j], h_of(i, j), ACT.Copy, scale=s.rx[:, j, 2:3]).then_inc(g.xn.sem, 1)

            load_tables(act, s, s.project_sems, next_layer(act, s, layer))
            over_pairs(act, NP, body)
            act.wait_ge(g.v.sem, g.v.at(layer, 1))
            nc.scalar.activation(eg, dg, ACT.Exp).then_inc(g.e.sem, 1)
            act.wait_ge(g.v.sem, g.v.at(layer, 2))
            nc.scalar.activation(ed, d, ACT.Exp).then_inc(g.e.sem, 1)

        @block.vector
        def _(dve):
            def stage_mix(i, j):
                nc.vector.tensor_scalar(mt_flat[j], h_of(i, j), 1.0, None, ALU.mult).then_inc(g.mt.sem, 1)

            def choose(i, j):
                t = 2 * i + j
                v = nc.vector
                n = [0]

                def link(ins):
                    n[0] += 1
                    ins.then_inc(g.ch.sem, 1)
                    wait_alone(dve, s, g.ch.sem, g.ch.at(layer, CHOICE_STEPS * t + n[0]))

                wait_alone(dve, s, g.lm.sem, g.lm.at(layer, t + 1))
                v.tensor_tensor(lg[:, t, :], bk[6][:, 0:R], s.route_b[:, :], ALU.add).then_inc(g.lo.sem, 1)
                v.tensor_tensor(s.gl[:, t, 0:NG], bk[6][:, 0:NG], s.route_b[:, 0:NG], ALU.add).then_inc(g.lo.sem, 1)
                wait_alone(dve, s, g.lo.sem, g.lo.at(layer, 2 * t + 2))
                link(v.max(s.gm[:, t, :], s.gl[:, t, :]))
                link(v.max_index(s.gi[:, t, :], s.gm[:, t, :], s.gl[:, t, :]))
                link(v.tensor_copy(gif[:, t, :], s.gi[:, t, 0:1]))
                link(v.tensor_scalar(other[:, t, :], s.iota[:, 0:NG], gif[:, t, :], -1.0, ALU.is_equal, ALU.add))
                link(v.scalar_tensor_tensor(out=masked[:, t, :].rearrange("p (g e) -> p g e", g=NG),
                                            in0=bcast(other[:, t, :].unsqueeze(2), [P, NG, s.PER]), scalar=BIG,
                                            in1=lg[:, t, NG:R].rearrange("p (g e) -> p g e", g=NG),
                                            op0=ALU.mult, op1=ALU.add))
                link(v.max(s.em[:, t, :], masked[:, t, :]))
                link(v.max_index(s.ei[:, t, :], s.em[:, t, :], masked[:, t, :]))
                link(v.tensor_copy(eif[:, t, :], s.ei[:, t, 0:2]))
                for k in range(2):
                    link(v.tensor_scalar(masks[j][:, k, :], s.iota[:, :], eif[:, t, k:k + 1], None, ALU.is_equal))
                link(v.tensor_tensor(both[j], masks[j][:, 0, :], masks[j][:, 1, :], ALU.add))
                link(v.tensor_tensor(upto_now[j], upto_now[1 - j], both[j], ALU.add))

            def place(i, j):
                t = 2 * i + j
                v = nc.vector
                n = [0]

                def link(ins, last=1):
                    n[0] += 1
                    ins.then_inc(g.pl.sem, 1)
                    if last:
                        wait_alone(dve, s, g.pl.sem, g.pl.at(layer, PLACE_STEPS * t + n[0]))

                rel = s.rel[:, t, :]
                pr = prod[:, t, :].rearrange("p (k e) -> p k e", k=2)
                wait_alone(dve, s, g.ps.sem, g.ps.at(layer, t + 1))
                link(v.tensor_tensor(pr, masks[j], bcast(bk[7][:, 0:s.E].unsqueeze(1), [P, 2, s.E]), ALU.mult))
                link(v.tensor_reduce(rel, pr, AX.X, ALU.add))
                link(v.scalar_tensor_tensor(out=slf[:, t, :], in0=rel, scalar=float(s.E), in1=eif[:, t, :],
                                            op0=ALU.mult, op1=ALU.add))
                link(v.tensor_copy(s.slots[:, t, :], slf[:, t, :]), 0)
                link(v.scalar_tensor_tensor(out=s.base_row[:, t, :], in0=eif[:, t, :], scalar=float(P), in1=rel,
                                            op0=ALU.mult, op1=ALU.add), 0)

            def h_tile(i, j):
                t = 2 * i + j
                dve.wait_ge(g.wo.sem, g.wo.at(layer, t + 1))
                dve.wait_ge(g.x[j].sem, g.x[j].at(layer, 16 * (i + 1)))
                nc.vector.tensor_tensor(h_of(i, j), pairs[j][:, :], x_t[j], ALU.add).then_inc(g.h.sem, 1)
                if not (isinstance(i, int) and i == NP - 1):
                    stage_mix(i + 1, j)

            def scale(i, j):
                t = 2 * i + j
                dve.wait_ge(g.rt.sem, g.rt.at(layer, t + 1))
                nc.vector.reciprocal(s.rx[:, j, 2:3], s.rx[:, j, 1:2]).then_inc(g.r.sem, 1)

            def evac_normed(i, j):
                dve.wait_ge(g.xt.sem, g.xt.at(layer, 2 * i + j + 1))
                for half in range(2):
                    nc.vector.tensor_tensor(
                        xnT[j][:, 4 * half:4 * half + 4, :], bk[4 + half].rearrange("p (k n) -> p k n", k=4),
                        bcast(s.gain2[:, 4 * half:4 * half + 4].unsqueeze(2), [P, 4, P]),
                        ALU.mult).then_inc(g.xo.sem, 1)

            def body(i):
                for j in range(2):
                    if not (first(i) and j == 0):
                        choose(i - (1 - j), 1 - j)
                    evac_normed(i, j)
                    last = isinstance(i, int) and i == NP - 1 and j == 1
                    if not last:
                        h_tile(i + j, 1 - j)
                    if not (first(i) and j == 0):
                        place(i - (1 - j), 1 - j)
                    if not last:
                        scale(i + j, 1 - j)

            dve.wait_ge(s.project_sems.late.sem, s.project_sems.late.at(layer, 48))
            stage_mix(0, 0)
            stage_mix(0, 1)
            nc.vector.memset(s.gl[:, :, NG:8], NEG)
            nc.vector.memset(upto_now[1], 0.0)
            h_tile(0, 0)
            scale(0, 0)
            over_pairs(dve, NP, body, 2)
            choose(NP - 1, 1)
            n = [0]

            def step(ins):
                n[0] += 1
                ins.then_inc(g.v.sem, 1)

            def link(ins):
                step(ins)
                wait_alone(dve, s, g.v.sem, g.v.at(layer, n[0]))

            v = nc.vector
            step(v.tensor_tensor(dg, s.gl[:, :, 0:NG], bcast(s.gm[:, :, 0:1], [P, NT, NG]), ALU.subtract))
            step(v.tensor_tensor(d, s.em[:, :, 1:2], s.em[:, :, 0:1], ALU.subtract))
            place(NP - 1, 1)
            wait_alone(dve, s, g.ct.sem, g.ct.at(layer, 1))
            link(v.tensor_reduce(cnt, bk[1][0:1, 0:s.E], AX.X, ALU.max))
            link(v.tensor_scalar(cnti, cnt, float(P - 1), None, ALU.add))
            link(v.tensor_scalar(s.nrounds[0:1, 0:1], cnti, 7, None, ALU.logical_shift_right))
            wait_alone(dve, s, g.e.sem, g.e.at(layer, 2))
            step(v.tensor_reduce(pg, eg, AX.X, ALU.add))
            link(v.tensor_scalar(den, ed, 1.0, None, ALU.add))
            step(v.reciprocal(pg, pg))
            link(v.reciprocal(den, den))
            link(v.tensor_tensor(s.gates[:, :, 0:1], pg, den, ALU.mult))
            step(v.tensor_tensor(s.gates[:, :, 1:2], s.gates[:, :, 0:1], ed, ALU.mult))
            assert n[0] == GATE_STEPS, n[0]

        @block.gpsimd
        def _(pool):
            for t in range(NT):
                wait_alone(pool, s, g.pl.sem, g.pl.at(layer, PLACE_STEPS * t + 4))
                for k in range(2):
                    nc.gpsimd.indirect_dma_start(
                        out=s.table, out_offset=bass.IndirectOffsetOnAxis(ap=s.slots[:, t, k:k + 1], axis=0),
                        in_=s.tokid[:, t:t + 1], in_offset=None).then_inc(g.sc.sem, 16)
            wait_alone(pool, s, g.sc.sem, g.sc.at(layer, 32 * NT))


def next_layer(eng, s, layer):
    reg = s.next_layer[eng.engine]
    eng.reg_mov(reg, layer)
    eng.reg_add(reg, reg, 1)
    eng.reg_alu(reg, reg, s.L - 1, ALU.min)
    return eng.snap(reg, min_val=0, max_val=s.L - 1)


def wait_alone(eng, s, sem, value):
    reg = s.wait_value[eng.engine]
    eng.reg_mov(reg, value)
    value = eng.snap(reg)
    eng.wait_ge(s.start_sets.sem, 1)
    eng.wait_ge(sem, value)


def expert_signals(s):
    sig = s.counted
    E, NT = s.E, s.NT
    g = Shared()
    g.ix = sig("slot_tokens_loaded", 16)
    g.gx = [sig(f"tokens_gathered{j}", 8 * E) for j in range(2)]
    g.w13 = [sig(f"w1_w3_loaded{j}", 16 * E) for j in range(2)]
    g.w2 = [sig(f"w2_loaded{j}", 8 * E) for j in range(2)]
    g.xt = sig("tokens_transposed", E)
    g.xo = sig("tokensT_ready", 2 * E)
    g.hm = sig("hidden_done", E)
    g.sl = sig("silu_ready", E)
    g.hd = sig("hidden_ready", E)
    g.ht = sig("hidden_transposed", E)
    g.ho = sig("hiddenT_ready", E)
    g.ym = sig("expert_rows_done", E)
    g.ya = sig("expert_rows_out_scalar", E)
    g.yv = sig("expert_rows_out_vector", E)
    g.ys = [sig(f"expert_rows_stored{j}", 8 * E) for j in range(2)]
    g.ci = sig("combine_steps", 7)
    g.yg = [sig(f"expert_rows_gathered{t}", 32) for t in range(NT)]
    g.ad = sig("expert_rows_added", 2 * NT)
    g.st = sig("layer_stored", 16 * NT)
    return g


def experts(nc, s, g, layer, rnd):
    NT, KT, E, F, D = s.NT, s.KT, s.E, s.F, s.D
    bk, pairs, ins = s.banks, s.bank_pairs, s.ins
    w = s.r_proj
    at = [0]

    def pair_of(n, region=w):
        at[0] += 2 * n
        return [region[:, at[0] - 2 * n + j * n:at[0] - n + j * n] for j in range(2)]

    w13 = [a.rearrange("p (k n) -> p k n", k=KT) for a in pair_of(KT * 2 * F)]
    w2 = [a.rearrange("p (k n) -> p k n", k=F // P) for a in pair_of(F // P * D)]
    xg = pair_of(D)
    xT = [a.rearrange("p (k n) -> p k n", k=KT) for a in pair_of(D)]
    sil, hid = pair_of(F), pair_of(F)
    hidT = [a.rearrange("p (k n) -> p k n", n=P) for a in pair_of(F)]
    y_t = pair_of(D)
    idx = w[:, at[0]:at[0] + E].bitcast(I32)
    small = w[:, at[0] + E:at[0] + E + 5 * 2 * NT].rearrange("p (a b) -> p a b", a=5)
    h_t = [s.r_tile[:, t * D:(t + 1) * D] for t in range(NT)]
    yg = [[w[:, (2 * t + k) * D:(2 * t + k + 1) * D] for k in range(2)] for t in range(NT)]
    va, vb = small[:, 0], small[:, 1]
    cidx, geff, vc = small[:, 2].bitcast(I32), small[:, 3], small[:, 4]
    NP = E // 2
    table_r = s.table.rearrange("(r p e) o -> r p (e o)", p=P, e=E)

    def count(eng):
        return eng.snap(s.rounds_done[eng.engine])

    def next_round(eng):
        eng.reg_add(s.rounds_done[eng.engine], s.rounds_done[eng.engine], 1)

    with nc.Block() as block:
        @block.sync
        def _(sp):
            done = count(sp)
            sp.dma_start(idx, table_r[rnd]).then_inc(g.ix.sem, 16)

            def load_w2(i, j):
                e = 2 * i + j
                if not first(i):
                    sp.wait_ge(g.ym.sem, g.ym.at(done, e - 1))
                sp.dma_start(w2[j], ins["w2"][layer, e].rearrange("(k p) n -> p k n", p=P)).then_inc(
                    g.w2[j].sem, 16)

            def body(i):
                for j in range(2):
                    e = 2 * i + j
                    if not first(i):
                        sp.wait_ge(g.hm.sem, g.hm.at(done, e - 1))
                    for c, name in enumerate(("w1", "w3")):
                        sp.dma_start(w13[j][:, :, F * c:F * (c + 1)],
                                     ins[name][layer, e].rearrange("(p k) n -> p k n", k=KT)).then_inc(
                                         g.w13[j].sem, 16)
                    if first(i) and j == 0:
                        sp.wait_ge(g.gx[0].sem, g.gx[0].at(done, 16))
                    if not (first(i) and j == 0):
                        load_w2(i - (1 - j), 1 - j)

            over_pairs(sp, NP, body, 2)
            load_w2(NP - 1, 1)
            for t in range(NT):
                sp.wait_ge(g.ad.sem, g.ad.at(done, 2 * (t + 1)))
                sp.dma_start(s.out_f[t * P:(t + 1) * P], h_t[t]).then_inc(g.st.sem, 16)
            wait_alone(sp, s, g.st.sem, g.st.at(done, 16 * NT))
            next_round(sp)

        @block.gpsimd
        def _(pool):
            done = count(pool)
            wait_alone(pool, s, g.ix.sem, g.ix.at(done, 16))
            for e in range(E):
                if e >= 2:
                    wait_alone(pool, s, g.xt.sem, g.xt.at(done, e - 1))
                nc.gpsimd.indirect_dma_start(
                    out=xg[e % 2], out_offset=None, in_=s.xn_dram,
                    in_offset=bass.IndirectOffsetOnAxis(ap=idx[:, e:e + 1], axis=0)).then_inc(g.gx[e % 2].sem, 16)
            for j in range(2):
                wait_alone(pool, s, g.ys[j].sem, g.ys[j].at(done, 8 * E))
            wait_alone(pool, s, g.ci.sem, g.ci.at(done, 5))
            for t in range(NT):
                for k in range(2):
                    nc.gpsimd.indirect_dma_start(
                        out=yg[t][k], out_offset=None, in_=s.y_dram,
                        in_offset=bass.IndirectOffsetOnAxis(ap=cidx[:, 2 * t + k:2 * t + k + 1], axis=0)).then_inc(
                            g.yg[t].sem, 16)
            next_round(pool)

        @block.tensor
        def _(pe):
            done = count(pe)

            def transpose_tokens(i, j):
                pe.wait_ge(g.gx[j].sem, g.gx[j].at(done, 16 * (i + 1)))
                xs = xg[j].rearrange("p (q k) -> p k q", k=KT)
                for k in range(KT):
                    mm = pe.transpose(bk[k // 4][:, (k % 4) * P:(k % 4 + 1) * P], xs[:, k, :], s.ident[:, :])
                mm.then_inc(g.xt.sem, 1)

            def expert_rows(i, j):
                e = 2 * i + j
                pe.wait_ge(g.ho.sem, g.ho.at(done, e + 1))
                pe.wait_ge(g.w2[j].sem, g.w2[j].at(done, 16 * (i + 1)))
                if not (first(i) and j == 0):
                    pe.wait_ge(g.ya.sem, g.ya.at(done, e))
                    pe.wait_ge(g.yv.sem, g.yv.at(done, e))
                for c in range(2):
                    for k in range(F // P):
                        mm = pe.matmul(bk[6 + c][:, :], hidT[j][:, k, :], w2[j][:, k, 512 * c:512 * c + 512],
                                       start=(k == 0), stop=(k == F // P - 1))
                mm.then_inc(g.ym.sem, 1)

            def body(i):
                for j in range(2):
                    e = 2 * i + j
                    pe.wait_ge(g.w13[j].sem, g.w13[j].at(done, 32 * (i + 1)))
                    pe.wait_ge(g.xo.sem, g.xo.at(done, 2 * e + 2))
                    if not first(i):
                        pe.wait_ge(g.hd.sem, g.hd.at(done, e - 1))
                    for k in range(KT):
                        mm = pe.matmul(bk[2 + j][:, 0:2 * F], xT[j][:, k, :], w13[j][:, k, :], start=(k == 0),
                                       stop=(k == KT - 1))
                    mm.then_inc(g.hm.sem, 1)
                    if not (isinstance(i, int) and i == NP - 1 and j == 1):
                        transpose_tokens(i + j, 1 - j)
                    if not (first(i) and j == 0):
                        expert_rows(i - (1 - j), 1 - j)
                    pe.wait_ge(g.hd.sem, g.hd.at(done, e + 1))
                    for k in range(F // P):
                        mm = pe.transpose(bk[4][:, k * P:(k + 1) * P], hid[j][:, k * P:(k + 1) * P], s.ident[:, :])
                    mm.then_inc(g.ht.sem, 1)

            transpose_tokens(0, 0)
            over_pairs(pe, NP, body, 2)
            expert_rows(NP - 1, 1)
            next_round(pe)

        @block.scalar
        def _(act):
            done = count(act)

            def first_half(i, j):
                e = 2 * i + j
                act.wait_ge(g.ym.sem, g.ym.at(done, e + 1))
                if not first(i):
                    act.wait_ge(g.ys[j].sem, g.ys[j].at(done, 16 * i))
                nc.scalar.activation(y_t[j][:, 0:512], bk[6][:, :], ACT.Copy).then_inc(g.ya.sem, 1)
                act.wait_ge(g.ya.sem, g.ya.at(done, e + 1))
                act.wait_ge(g.yv.sem, g.yv.at(done, e + 1))
                act.dma_start(s.y_dram[bass.ds(e * P, P)], y_t[j]).then_inc(g.ys[j].sem, 16)

            def body(i):
                for j in range(2):
                    e = 2 * i + j
                    act.wait_ge(g.hm.sem, g.hm.at(done, e + 1))
                    nc.scalar.activation(sil[j], bk[2 + j][:, 0:F], ACT.Silu).then_inc(g.sl.sem, 1)
                    if not (first(i) and j == 0):
                        first_half(i - (1 - j), 1 - j)
                    act.wait_ge(g.ht.sem, g.ht.at(done, e + 1))
                    nc.scalar.activation(hidT[j], bk[4][:, 0:F].rearrange("p (k n) -> p k n", n=P),
                                         ACT.Copy).then_inc(g.ho.sem, 1)

            over_pairs(act, NP, body, 2)
            first_half(NP - 1, 1)
            next_round(act)

        @block.vector
        def _(dve):
            done = count(dve)

            def evac_tokens(i, j):
                e = 2 * i + j
                dve.wait_ge(g.xt.sem, g.xt.at(done, e + 1))
                for half in range(2):
                    nc.vector.tensor_tensor(
                        xT[j][:, 4 * half:4 * half + 4, :], bk[half].rearrange("p (k n) -> p k n", k=4),
                        bcast(s.gain2[:, 4 * half:4 * half + 4].unsqueeze(2), [P, 4, P]),
                        ALU.mult).then_inc(g.xo.sem, 1)

            def second_half(i, j):
                e = 2 * i + j
                dve.wait_ge(g.ym.sem, g.ym.at(done, e + 1))
                if not first(i):
                    dve.wait_ge(g.ys[j].sem, g.ys[j].at(done, 16 * i))
                nc.vector.tensor_copy(y_t[j][:, 512:1024], bk[7][:, :]).then_inc(g.yv.sem, 1)

            def body(i):
                for j in range(2):
                    e = 2 * i + j
                    dve.wait_ge(g.sl.sem, g.sl.at(done, e + 1))
                    nc.vector.tensor_tensor(hid[j], sil[j], bk[2 + j][:, F:2 * F], ALU.mult).then_inc(g.hd.sem, 1)
                    if not (isinstance(i, int) and i == NP - 1 and j == 1):
                        evac_tokens(i + j, 1 - j)
                    if not (first(i) and j == 0):
                        second_half(i - (1 - j), 1 - j)

            def step(n, ins):
                ins.then_inc(g.ci.sem, 1)
                wait_alone(dve, s, g.ci.sem, g.ci.at(done, n))

            rel, base, gates = (a[:, :, :].rearrange("p t k -> p (t k)") for a in (s.rel, s.base_row, s.gates))
            step(1, nc.vector.tensor_scalar(va, rel, 0.0, None, ALU.is_ge))
            step(2, nc.vector.tensor_scalar(vb, rel, float(P), None, ALU.is_lt))
            step(3, nc.vector.tensor_tensor(vc, va, vb, ALU.mult))
            step(4, nc.vector.tensor_tensor(geff, vc, gates, ALU.mult))
            step(5, nc.vector.tensor_tensor(cidx, vc, base, ALU.mult))
            step(6, nc.vector.tensor_scalar(rel, rel, -float(P), None, ALU.add))
            step(7, nc.vector.tensor_scalar(base, base, -float(P), None, ALU.add))

            evac_tokens(0, 0)
            over_pairs(dve, NP, body, 2)
            second_half(NP - 1, 1)

            for t in range(NT):
                dve.wait_ge(g.yg[t].sem, g.yg[t].at(done, 32))
                for k in range(2):
                    nc.vector.scalar_tensor_tensor(out=h_t[t], in0=yg[t][k], scalar=geff[:, 2 * t + k:2 * t + k + 1],
                                                   in1=h_t[t], op0=ALU.mult, op1=ALU.add).then_inc(g.ad.sem, 1)
                    if k == 0:
                        dve.wait_ge(g.ad.sem, g.ad.at(done, 2 * t + 1))
            next_round(dve)


def tables(seq, experts_n):
    import numpy as np

    p = np.arange(P)
    nt = seq // P
    slopes = 2.0 ** (-8.0 * np.arange(1, 2 * HEADS + 1) / (2 * HEADS))
    inv = np.float32(10000.0) ** (-np.arange(0, NROPE, 2, dtype=np.float32) / np.float32(NROPE))
    ang = (np.arange(seq, dtype=np.float32)[:, None] * inv[None, :]).astype(np.float32)
    cs = np.stack([np.cos(ang), np.sin(ang)], 0).reshape(2, nt, P, NROPE // 2).transpose(2, 0, 1, 3)
    dist = p[:, None] + (seq - P) - np.arange(seq)[None, :]
    mult = sum(((dist >= 0) & (dist <= w) & (dist % dl == 0)).astype(np.float64)
               for w, dl in ((128, 1), (512, 4), (2048, 16)))
    dilated = [np.where(mult > 0, np.log(np.maximum(mult, 1)) - sl * dist, NEG) for sl in slopes[HEADS:]]
    near = p[:, None] + P - np.arange(2 * P)[None, :]
    window = [np.where((near >= 0) & (near < P), -sl * near, NEG) for sl in slopes[:HEADS]]
    f = np.float32
    fixed = [np.eye(P), np.ones((P, P)), p[:, None] <= p[None, :], p[:, None] < p[None, :],
             np.tile(np.arange(experts_n), (P, 1)), cs.reshape(P, -1)]
    return {
        "fixed": np.concatenate([a.astype(f) for a in fixed], 1),
        "tokid": (p[:, None] + P * np.arange(nt)[None, :]).astype(np.int32),
        "causal": np.where(dist >= 0, 0.0, NEG).astype(f),
        "dilated": np.stack(dilated).astype(f), "window": np.stack(window).astype(f),
    }


_INS = ("x", "norm1_g", "w_in", "mla_gcq", "mla_gckv", "mla_wuq", "mla_wukv", "qk_gq", "qk_gk", "fox_bf", "sink",
        "w_o", "norm2_g", "w_rg", "b_rg", "w_re", "b_re", "w1", "w3", "w2")


def kernel(**inputs):
    import numpy as np
    import concourse.bacc as bacc
    from concourse.bass_utils import run_bass_kernel_spmd

    nc = bacc.Bacc("TRN2", target_bir_lowering=False, num_devices=1)
    arrays, ins, consts = {}, {}, {}
    for name in _INS:
        a = np.ascontiguousarray(inputs[name])
        arrays["in_" + name] = a
        ins[name] = nc.dram_tensor("in_" + name, a.shape, F32, kind="ExternalInput").ap()
    seq, d = inputs["x"].shape[1:]
    n_exp = inputs["w1"].shape[1]
    for name, a in tables(seq, n_exp).items():
        arrays["table_" + name] = a
        consts[name] = nc.dram_tensor("table_" + name, a.shape, mybir.dt.from_np(a.dtype), kind="ExternalInput").ap()
    scratch = {
        "xn": nc.dram_tensor("normed", (seq, d), F32, kind="Internal").ap(),
        "y": nc.dram_tensor("expert_rows", (n_exp * P, d), F32, kind="Internal").ap(),
        "table": nc.dram_tensor("slot_tokens", (seq * n_exp, 1), I32, kind="Internal").ap(),
    }
    out = nc.dram_tensor("out", inputs["x"].shape, F32, kind="ExternalOutput").ap()
    trunk(nc, ins, consts, scratch, out)
    return run_bass_kernel_spmd(nc, [arrays], core_ids=[0]).results[0]["out"]
```
